# Optimizing a Trainium2 kernel written in Bass

```python
import math
import jax, jax.numpy as jnp
from jax import lax
import numpy as np

D_MODEL = 1024
BATCH = 1
SEQ = 1024
DEPTH = 2

GRID_W = 64
CTX_LEN = 256
HEAD_DIM = 64
ROPE_THETA = 10000.0
NORM_EPS = 1e-6
Q_BLOCK = 128
A_HEADS = 4
A_KV_HEADS = 2
B_HEADS = 4
B_QK_DIM = 32
B_V_DIM = 2 * B_QK_DIM
C_HEADS = 8
C_HEAD = 64
C_WIDTH = C_HEADS * C_HEAD
C_DECAY_LORA = 64
C_ICL_LORA = 64
C_GATE_LORA = 128
N_DIR = 2
C_GN_EPS = 64e-5
A_Q = A_HEADS * HEAD_DIM
A_KV = A_KV_HEADS * HEAD_DIM
B_Q = B_HEADS * 2 * B_QK_DIM
B_V = B_HEADS * B_V_DIM
C_SLICE = 3 * C_WIDTH + N_DIR * C_DECAY_LORA + N_DIR * C_ICL_LORA + C_GATE_LORA
IN_SPLITS = (A_Q, A_Q + A_KV, A_Q + 2 * A_KV, A_Q + 2 * A_KV + B_Q, A_Q + 2 * A_KV + 2 * B_Q, A_Q + 2 * A_KV + 2 * B_Q + B_V)
IN_WIDTH = A_Q + 2 * A_KV + 2 * B_Q + B_V + C_SLICE
MIX_WIDTH = A_HEADS * HEAD_DIM + B_HEADS * B_V_DIM + C_WIDTH
N_GROUPS = 4
EXPERTS_PER_GROUP = 8
N_EXPERTS = N_GROUPS * EXPERTS_PER_GROUP
TOP_K = 2
EXPERT_FF = 512
EXPERT_BLOCK = 128

kernel_name = "hymba_style_diff_rwkv7_hier_moe_dit"

def rms_norm(x, gain, eps=NORM_EPS):
    xf = x.astype(jnp.float32)
    y = xf * lax.rsqrt(jnp.mean(xf * xf, axis=-1, keepdims=True) + eps)
    return (y * gain.astype(jnp.float32)).astype(x.dtype)

def ada_norm(x, gain, shift, scale):
    return rms_norm(x, gain) * (1 + scale) + shift

def axial_rope_tables(row_idx, col_idx, dim):
    half = dim // 2
    inv = ROPE_THETA ** (-jnp.arange(0, half, 2, dtype=jnp.float32) / half)
    ar = row_idx.astype(jnp.float32)[:, None] * inv
    ac = col_idx.astype(jnp.float32)[:, None] * inv
    ang = jnp.concatenate([ar, ar, ac, ac], axis=-1)
    return jnp.cos(ang), jnp.sin(ang)

def rotate_halves(x):
    q = x.shape[-1] // 4
    x = x.reshape(x.shape[:-1] + (2, 2, q))
    x = jnp.stack([-x[..., 1, :], x[..., 0, :]], axis=-2)
    return x.reshape(x.shape[:-3] + (4 * q,))

def apply_rope(x, cos, sin):
    xf = x.astype(jnp.float32)
    return (xf * cos + rotate_halves(xf) * sin).astype(x.dtype)

def split_combined(p):
    bsz, t = p.shape[:2]
    aq, ak, av, bq, bk, bv, cp = jnp.split(p, list(IN_SPLITS), axis=-1)
    return (aq.reshape(bsz, t, A_HEADS, HEAD_DIM), ak.reshape(bsz, t, A_KV_HEADS, HEAD_DIM),
            av.reshape(bsz, t, A_KV_HEADS, HEAD_DIM), bq.reshape(bsz, t, B_HEADS, 2, B_QK_DIM),
            bk.reshape(bsz, t, B_HEADS, 2, B_QK_DIM), bv.reshape(bsz, t, B_HEADS, B_V_DIM), cp)

def sweep_query_blocks(attend, q, *args):
    b, s = q.shape[:2]
    nb = s // Q_BLOCK
    qb = jnp.moveaxis(q.reshape((b, nb, Q_BLOCK) + q.shape[2:]), 1, 0)
    out = lax.map(lambda blk: attend(blk, *args), qb)
    return jnp.moveaxis(out, 0, 1).reshape(b, s, -1)

def gqa_attend(q, k, v):
    b, t, h, d = q.shape
    kvh = k.shape[2]
    qg = q.reshape(b, t, kvh, h // kvh, d)
    s = jnp.einsum('btkgd,bskd->bkgts', qg, k, preferred_element_type=jnp.float32) * (d ** -0.5)
    p = jax.nn.softmax(s, axis=-1).astype(v.dtype)
    o = jnp.einsum('bkgts,bskd->btkgd', p, v)
    return o.reshape(b, t, h * d)

def diff_attend(q, k, v, lam):
    b, t = q.shape[:2]
    d = q.shape[-1]
    s = jnp.einsum('bthmd,bshmd->bhmts', q, k, preferred_element_type=jnp.float32) * (d ** -0.5)
    p = jax.nn.softmax(s, axis=-1)
    a = (p[:, :, 0] - lam * p[:, :, 1]).astype(v.dtype)
    o = jnp.einsum('bhts,bshe->bthe', a, v)
    return o.reshape(b, t, -1)

def diff_head_norm(o, gain, lam_init):
    b, t = o.shape[:2]
    o = rms_norm(o.reshape(b, t, B_HEADS, B_V_DIM), gain) * (1.0 - lam_init)
    return o.reshape(b, t, B_HEADS * B_V_DIM)

def rwkv_inputs(p, mu, w0, w2, a0, a2, g2, k_k, k_a):
    prev = jnp.pad(p[:, :-1], ((0, 0), (1, 0), (0, 0)))
    nxt = jnp.pad(p[:, 1:], ((0, 0), (0, 1), (0, 0)))
    pf = (p + mu * (0.5 * (prev + nxt) - p)).astype(jnp.float32)
    o1 = C_WIDTH; o2 = 2 * C_WIDTH; o3 = 3 * C_WIDTH
    o4 = o3 + N_DIR * C_DECAY_LORA; o5 = o4 + N_DIR * C_ICL_LORA
    r, k, v, wd, ad, gd = jnp.split(pf, [o1, o2, o3, o4, o5], axis=-1)
    bsz, t = p.shape[:2]
    wd = wd.reshape(bsz, t, N_DIR, C_DECAY_LORA)
    ad = ad.reshape(bsz, t, N_DIR, C_ICL_LORA)
    wlog = -jax.nn.softplus(-(w0 + jnp.einsum('btzr,zrc->btzc', jnp.tanh(wd), w2))) - 0.5
    decay = jnp.exp(-jnp.exp(wlog))
    icl = jax.nn.sigmoid(a0 + jnp.einsum('btzr,zrc->btzc', ad, a2))
    g = jax.nn.sigmoid(gd) @ g2.astype(jnp.float32)
    heads = lambda z: z.reshape(z.shape[:-1] + (C_HEADS, C_HEAD))
    kk = heads(k * k_k)
    kk = kk / jnp.maximum(jnp.sqrt(jnp.sum(kk * kk, axis=-1, keepdims=True)), 1e-12)
    k_dir = k[:, :, None] * (1 + (icl - 1) * k_a)
    return heads(r), heads(k_dir), heads(v), heads(decay), heads(icl), kk, g

def rwkv_direction(inp, z):
    r, kd, v, dec, icl, kk, g = inp
    return r, dec[:, :, z], kd[:, :, z], v, -kk, kk * icl[:, :, z]

def wkv7_scan(state0, r, w, k, v, a, b, reverse, emit):
    xs = tuple(jnp.moveaxis(t_, 1, 0) for t_ in (r, w, k, v, a, b))

    def step(S, inp):
        r_t, w_t, k_t, v_t, a_t, b_t = inp
        sa = jnp.einsum('bhvk,bhk->bhv', S, a_t)
        S = S * w_t[:, :, None, :] + sa[..., None] * b_t[:, :, None, :] + v_t[..., None] * k_t[:, :, None, :]
        y = jnp.einsum('bhvk,bhk->bhv', S, r_t) if emit else None
        return S, y

    S, ys = lax.scan(step, state0, xs, reverse=reverse)
    return S, (jnp.moveaxis(ys, 0, 1) if emit else None)

def rwkv_readout(y_dirs, inp, r_k, ln_w, ln_b):
    r, kd, v, dec, icl, kk, g = inp
    y = y_dirs[0] + y_dirs[1]
    mean = jnp.mean(y, axis=-1, keepdims=True)
    var = jnp.mean(jnp.square(y - mean), axis=-1, keepdims=True)
    y = (y - mean) * lax.rsqrt(var + C_GN_EPS) * ln_w.reshape(C_HEADS, C_HEAD) + ln_b.reshape(C_HEADS, C_HEAD)
    bonus = jnp.sum(jnp.sum(r[:, :, None] * kd * r_k, axis=-1, keepdims=True) * v[:, :, None], axis=2)
    bsz, t = y.shape[:2]
    return (y + bonus).reshape(bsz, t, C_WIDTH) * g

def routed_experts(t, experts, gates, w1, w3, w2):
    n_tok, d = t.shape
    n_assign = n_tok * TOP_K
    n_exp = w1.shape[0]
    n_blocks = (n_assign + n_exp * (EXPERT_BLOCK - 1) + EXPERT_BLOCK - 1) // EXPERT_BLOCK
    n_rows = n_blocks * EXPERT_BLOCK
    flat_e = experts.reshape(-1)
    order = jnp.argsort(flat_e)
    sorted_e = flat_e[order]
    counts = jnp.bincount(flat_e, length=n_exp)
    padded = (counts + EXPERT_BLOCK - 1) // EXPERT_BLOCK * EXPERT_BLOCK
    pad_end = jnp.cumsum(padded)
    pad_start = pad_end - padded
    raw_start = jnp.cumsum(counts) - counts
    dest = pad_start[sorted_e] + jnp.arange(n_assign, dtype=jnp.int32) - raw_start[sorted_e]
    row_tok = jnp.full((n_rows,), n_tok, jnp.int32).at[dest].set((order // TOP_K).astype(jnp.int32))
    row_gate = jnp.zeros((n_rows,), jnp.float32).at[dest].set(gates.reshape(-1)[order])
    block_exp = jnp.minimum(jnp.searchsorted(pad_end, jnp.arange(n_blocks, dtype=jnp.int32) * EXPERT_BLOCK, side='right'), n_exp - 1)
    t_pad = jnp.concatenate([t, jnp.zeros((1, d), t.dtype)], axis=0)

    def expert_block(args):
        rows, e = args
        xb = t_pad[rows]
        h = jax.nn.silu(xb @ w1[e]) * (xb @ w3[e])
        return h @ w2[e]

    y_rows = lax.map(expert_block, (row_tok.reshape(n_blocks, EXPERT_BLOCK), block_exp))
    y_rows = y_rows.reshape(n_rows, d) * row_gate[:, None].astype(t.dtype)
    out = jnp.zeros((n_tok + 1, d), t.dtype).at[row_tok].add(y_rows)
    return out[:n_tok]

def hier_moe(t, w_group, b_group, w_expert, b_expert, w1, w3, w2):
    n_tok = t.shape[0]
    tf = t.astype(jnp.float32)
    group_prob = jax.nn.softmax(tf @ w_group.astype(jnp.float32) + b_group, axis=-1)
    g_idx = jnp.argmax(group_prob, axis=-1).astype(jnp.int32)
    g_p = jnp.max(group_prob, axis=-1)
    e_logits = (tf @ w_expert.astype(jnp.float32) + b_expert).reshape(n_tok, N_GROUPS, EXPERTS_PER_GROUP)
    e_logits = jnp.take_along_axis(e_logits, g_idx[:, None, None], axis=1)[:, 0]
    top_v, top_i = lax.top_k(e_logits, TOP_K)
    gates = jax.nn.softmax(top_v, axis=-1) * g_p[:, None]
    experts = g_idx[:, None] * EXPERTS_PER_GROUP + top_i.astype(jnp.int32)
    return routed_experts(t, experts, gates, w1, w3, w2)

def setup_inputs(seed: int = 0) -> dict:
    key = jax.random.key(seed)
    ks = iter(jax.random.split(key, 40))
    f32 = jnp.float32
    nrm = lambda shape, s: jax.random.normal(next(ks), shape, f32) * s
    D = D_MODEL
    return {
        "x": nrm((BATCH, SEQ, D), 1.0),
        "c": nrm((BATCH, D), 1.0),
        "ctx": nrm((BATCH, CTX_LEN, D), 1.0),
        "c_ctx": nrm((D,), 1.0),
        "w_mod": nrm((DEPTH, D, 6 * D), 0.5 * D ** -0.5),
        "b_mod": nrm((DEPTH, 6 * D), 0.02),
        "g_mix": 1.0 + nrm((DEPTH, D), 0.05),
        "g_ffn": 1.0 + nrm((DEPTH, D), 0.05),
        "w_in": nrm((DEPTH, D, IN_WIDTH), D ** -0.5),
        "a_q_gain": 1.0 + nrm((DEPTH, HEAD_DIM), 0.05),
        "a_k_gain": 1.0 + nrm((DEPTH, HEAD_DIM), 0.05),
        "b_lq1": nrm((DEPTH, B_QK_DIM), 0.1),
        "b_lk1": nrm((DEPTH, B_QK_DIM), 0.1),
        "b_lq2": nrm((DEPTH, B_QK_DIM), 0.1),
        "b_lk2": nrm((DEPTH, B_QK_DIM), 0.1),
        "b_subln": 1.0 + nrm((DEPTH, B_V_DIM), 0.05),
        "c_mu": jax.random.uniform(next(ks), (DEPTH, C_SLICE), f32),
        "c_w0": jax.random.uniform(next(ks), (DEPTH, N_DIR, C_WIDTH), f32, -6.0, -1.0),
        "c_w2": nrm((DEPTH, N_DIR, C_DECAY_LORA, C_WIDTH), 0.1),
        "c_a0": nrm((DEPTH, N_DIR, C_WIDTH), 0.5),
        "c_a2": nrm((DEPTH, N_DIR, C_ICL_LORA, C_WIDTH), 0.1),
        "c_g2": nrm((DEPTH, C_GATE_LORA, C_WIDTH), C_GATE_LORA ** -0.5),
        "c_k_k": 0.85 + nrm((DEPTH, C_WIDTH), 0.05),
        "c_k_a": 1.0 + nrm((DEPTH, C_WIDTH), 0.05),
        "c_r_k": nrm((DEPTH, C_HEADS, C_HEAD), 0.1),
        "c_ln_w": 1.0 + nrm((DEPTH, C_WIDTH), 0.05),
        "c_ln_b": nrm((DEPTH, C_WIDTH), 0.01),
        "w_out": nrm((DEPTH, MIX_WIDTH, D), MIX_WIDTH ** -0.5),
        "r_w_group": nrm((DEPTH, D, N_GROUPS), D ** -0.5),
        "r_b_group": nrm((DEPTH, N_GROUPS), 0.01),
        "r_w_expert": nrm((DEPTH, D, N_EXPERTS), D ** -0.5),
        "r_b_expert": nrm((DEPTH, N_EXPERTS), 0.01),
        "e_w1": nrm((DEPTH, N_EXPERTS, D, EXPERT_FF), D ** -0.5),
        "e_w3": nrm((DEPTH, N_EXPERTS, D, EXPERT_FF), D ** -0.5),
        "e_w2": nrm((DEPTH, N_EXPERTS, EXPERT_FF, D), EXPERT_FF ** -0.5),
        "g_final": 1.0 + nrm((D,), 0.05),
    }

def reference(x, c, ctx, c_ctx, w_mod, b_mod, g_mix, g_ffn, w_in, a_q_gain, a_k_gain,
              b_lq1, b_lk1, b_lq2, b_lk2, b_subln, c_mu, c_w0, c_w2, c_a0, c_a2, c_g2,
              c_k_k, c_k_a, c_r_k, c_ln_w, c_ln_b, w_out, r_w_group, r_b_group,
              r_w_expert, r_b_expert, e_w1, e_w3, e_w2, g_final):
    bsz, n_lat, d = x.shape
    n_ctx = ctx.shape[1]
    ROWS = n_lat // GRID_W
    row_idx = jnp.repeat(jnp.arange(ROWS, dtype=jnp.int32), GRID_W)
    col_idx = jnp.tile(jnp.arange(GRID_W, dtype=jnp.int32), ROWS)
    cos_a, sin_a = axial_rope_tables(row_idx, col_idx, HEAD_DIM)
    cos_a, sin_a = cos_a[None, :, None, :], sin_a[None, :, None, :]
    cos_b, sin_b = axial_rope_tables(row_idx, col_idx, B_QK_DIM)
    cos_b, sin_b = cos_b[None, :, None, None, :], sin_b[None, :, None, None, :]
    act_c = jax.nn.silu(c)
    act_cc = jax.nn.silu(c_ctx)
    state0 = jnp.zeros((bsz, C_HEADS, C_HEAD, C_HEAD), jnp.float32)
    xc = ctx
    for i in range(DEPTH):
        update_ctx = i < DEPTH - 1
        mod_l = (act_c @ w_mod[i] + b_mod[i]).reshape(bsz, 6, 1, d)
        sh1, sc1, ga1, sh2, sc2, ga2 = [mod_l[:, j] for j in range(6)]
        mod_c = (act_cc @ w_mod[i] + b_mod[i]).reshape(6, d)
        csh1, csc1, cga1, csh2, csc2, cga2 = [mod_c[j] for j in range(6)]

        p_l = ada_norm(x, g_mix[i], sh1, sc1) @ w_in[i]
        p_c = ada_norm(xc, g_mix[i], csh1, csc1) @ w_in[i]
        aq_l, ak_l, av_l, bq_l, bk_l, bv_l, cp_l = split_combined(p_l)
        aq_c, ak_c, av_c, bq_c, bk_c, bv_c, cp_c = split_combined(p_c)

        aq_l = apply_rope(rms_norm(aq_l, a_q_gain[i]), cos_a, sin_a)
        ak_l = apply_rope(rms_norm(ak_l, a_k_gain[i]), cos_a, sin_a)
        ak_c = rms_norm(ak_c, a_k_gain[i])
        ak_all = jnp.concatenate([ak_c, ak_l], axis=1)
        av_all = jnp.concatenate([av_c, av_l], axis=1)
        ya_l = sweep_query_blocks(gqa_attend, aq_l, ak_all, av_all)

        lam_init = 0.8 - 0.6 * math.exp(-0.3 * i)
        lam = (jnp.exp(jnp.sum(b_lq1[i].astype(jnp.float32) * b_lk1[i].astype(jnp.float32)))
               - jnp.exp(jnp.sum(b_lq2[i].astype(jnp.float32) * b_lk2[i].astype(jnp.float32))) + lam_init)
        bq_l = apply_rope(bq_l, cos_b, sin_b)
        bk_l = apply_rope(bk_l, cos_b, sin_b)
        bk_all = jnp.concatenate([bk_c, bk_l], axis=1)
        bv_all = jnp.concatenate([bv_c, bv_l], axis=1)
        yb_l = diff_head_norm(sweep_query_blocks(diff_attend, bq_l, bk_all, bv_all, lam), b_subln[i], lam_init)

        rw = (c_mu[i], c_w0[i], c_w2[i], c_a0[i], c_a2[i], c_g2[i], c_k_k[i], c_k_a[i])
        cin_l = rwkv_inputs(cp_l, *rw)
        cin_c = rwkv_inputs(cp_c, *rw)
        yl_dirs, yc_dirs = [], []
        for z, rev in enumerate((False, True)):
            s_c, y_c = wkv7_scan(state0, *rwkv_direction(cin_c, z), reverse=rev, emit=update_ctx)
            _, y_l = wkv7_scan(s_c, *rwkv_direction(cin_l, z), reverse=rev, emit=True)
            yl_dirs.append(y_l)
            yc_dirs.append(y_c)
        yc_l = rwkv_readout(yl_dirs, cin_l, c_r_k[i], c_ln_w[i], c_ln_b[i]).astype(x.dtype)

        if update_ctx:
            ya_c = gqa_attend(rms_norm(aq_c, a_q_gain[i]), ak_c, av_c)
            yb_c = diff_head_norm(diff_attend(bq_c, bk_c, bv_c, lam), b_subln[i], lam_init)
            yc_c = rwkv_readout(yc_dirs, cin_c, c_r_k[i], c_ln_w[i], c_ln_b[i]).astype(xc.dtype)
            xc = xc + cga1 * (jnp.concatenate([ya_c, yb_c, yc_c], axis=-1) @ w_out[i])
        x = x + ga1 * (jnp.concatenate([ya_l, yb_l, yc_l], axis=-1) @ w_out[i])

        f_l = ada_norm(x, g_ffn[i], sh2, sc2).reshape(bsz * n_lat, d)
        if update_ctx:
            f_c = ada_norm(xc, g_ffn[i], csh2, csc2).reshape(bsz * n_ctx, d)
            tokens = jnp.concatenate([f_l, f_c], axis=0)
        else:
            tokens = f_l
        y = hier_moe(tokens, r_w_group[i], r_b_group[i], r_w_expert[i], r_b_expert[i], e_w1[i], e_w3[i], e_w2[i])
        x = x + ga2 * y[:bsz * n_lat].reshape(bsz, n_lat, d)
        if update_ctx:
            xc = xc + cga2 * y[bsz * n_lat:].reshape(bsz, n_ctx, d)
    return rms_norm(x, g_final)


_drawn_inputs = setup_inputs


def setup_inputs(seed=0):
    import zlib

    import numpy as np

    out = dict(_drawn_inputs(seed))
    spreads = {}
    factors = {'g_mix': 2.713,
     'a_q_gain': 8.0,
     'a_k_gain': 8.0,
     'b_lq1': 4.688,
     'b_lk1': 5.81,
     'b_lq2': 8.0,
     'b_lk2': 8.0,
     'b_subln': 4.68,
     'c_w2': 3.236,
     'c_ln_w': 4.315,
     'c_ln_b': 8.0,
     'r_b_group': 7.4,
     'r_b_expert': 5.99}
    for name, (base, spread) in spreads.items():
        noise = np.random.default_rng([zlib.crc32(name.encode()), seed]).standard_normal(out[name].shape)
        drawn = base * np.exp(spread * noise) if base else spread * noise
        out[name] = __import__('jax').numpy.asarray(drawn.astype(out[name].dtype))
    for name, factor in factors.items():
        out[name] = (out[name] * factor).astype(out[name].dtype)
    return out
```

```python
from contextlib import ExitStack, contextmanager

import numpy as np

import concourse.bass as bass
from concourse import mybir

F32 = mybir.dt.float32
I32 = mybir.dt.int32
U32 = mybir.dt.uint32
ALU = mybir.AluOpType
ACT = mybir.ActivationFunctionType
AX = mybir.AxisListType
ds = bass.ds

P = 128
D = 1024
DT = D // P
DEPTH = 2
SEQ = 1024
CTX = 256
TOK = SEQ + CTX
NT = TOK // P
CT = CTX // P
LT = SEQ // P
GRID_W = 64
EPS = 1e-6
HD = 64
A_Q, A_KV, B_Q, B_V = 256, 128, 256, 256
ATT = A_Q + 2 * A_KV + 2 * B_Q + B_V
CW = 512
CH = 8
LORA = 384
CS = 3 * CW + LORA
IN_W = ATT + CS
GN_EPS = 64e-5
NG, EPG, NE, FF = 4, 8, 32, 512
SLOTS = TOK * 2
OVER = 2 * ((SLOTS - 1) // P // 2 + 1)
NB = NE + OVER
C = 64
NC_CTX = CTX // C
NC_LAT = SEQ // C
NZ = 2
ST = NZ * CH

PAD_ROWS = TOK + 3
SEGMENTS = {"ctx": (0, CT, 1), "lat": (CTX, LT, CTX + 2)}


def tokens_of(seg):
    return SEGMENTS[seg]


@contextmanager
def phase(nc):
    sems = []
    with ExitStack() as ctx:
        def sb(name, shape, dt=F32):
            return ctx.enter_context(nc.sbuf_tensor(nc_name(name), shape, dt))

        def sem(name):
            s = nc.alloc_semaphore(nc_name(name))
            sems.append(s)
            return s

        yield sb, sem
        nc.clear_and_free_semaphores(sems)
        nc.all_engine_barrier()


_names = {}


def nc_name(name):
    _names[name] = _names.get(name, 0) + 1
    return f"{name}_{_names[name]}"


def rows(ap, start, n=P):
    return ap[ds(start, n), :]


def rope_tables():
    def table(dim):
        half = dim // 2
        inv = np.float32(10000.0) ** (-np.arange(0, half, 2, dtype=np.float32) / np.float32(half))
        t = np.arange(SEQ)
        ar = (t // GRID_W).astype(np.float32)[:, None] * inv.astype(np.float32)
        ac = (t % GRID_W).astype(np.float32)[:, None] * inv.astype(np.float32)
        ang = np.concatenate([ar, ar, ac, ac], -1).astype(np.float32)
        q = dim // 4
        sign = np.tile(np.concatenate([-np.ones(q), np.ones(q)]), 2).astype(np.float32)
        return np.cos(ang).astype(np.float32), (np.sin(ang) * sign).astype(np.float32)
    ca, sa = table(64)
    cb, sb = table(32)
    return np.concatenate([np.tile(ca, 6), np.tile(cb, 16), np.tile(sa, 6), np.tile(sb, 16)], -1)


ROPE_W = 6 * 64 + 16 * 32


def scan_constants():
    i = np.arange(C)
    before = [i[:, None] < i[None, :], i[:, None] > i[None, :]]
    eye = np.eye(C, dtype=bool)
    tri = np.zeros((C, NZ, 2 * P), np.float32)
    mask = np.zeros((P, NZ, P), np.float32)
    for z in range(NZ):
        incl = (before[z] | eye).astype(np.float32)
        excl = before[z].astype(np.float32)
        tri[:, z] = np.concatenate([incl, excl, -incl, -incl], 1)
        half = np.concatenate([incl, excl], 1)
        mask[:, z] = np.concatenate([half, half], 0)
    levels = []
    n = 1
    while n < C:
        up = (i[:, None] // (2 * n) == i[None, :] // (2 * n)) & (i[:, None] // n != i[None, :] // n)
        levels.append(np.stack([(up & before[z]).astype(np.float32) for z in range(NZ)], 1))
        n *= 2
    lv = np.stack(levels, 1).reshape(C, -1)
    return tri.reshape(C, -1), mask.reshape(P, -1), lv


LEVELS = 6


class Net:

    def __init__(self, nc, ins, out):
        self.ins = ins
        self.out = out
        self.x = nc.dram_tensor("s_x", [TOK, D], F32).ap()
        self.mod = nc.dram_tensor("s_mod", [DEPTH, 2, 6 * D], F32).ap()
        self.p = nc.dram_tensor("s_p", [PAD_ROWS, IN_W], F32).ap()
        self.y = nc.dram_tensor("s_y", [TOK, D], F32).ap()
        self.scan = nc.dram_tensor("s_scan", [TOK, 9 * CW], F32).ap()
        self.gb = nc.dram_tensor("s_gb", [TOK, 2 * CW], F32).ap()
        self.yd = nc.dram_tensor("s_yd", [NZ, TOK, CW], F32).ap()
        self.f = nc.dram_tensor("s_f", [TOK, D], F32).ap()
        self.table = nc.dram_tensor("s_table", [NB * P, 1], I32).ap()
        self.ye = nc.dram_tensor("s_ye", [NB * P, D], F32).ap()


def modulation_phase(nc, net, ps):
    NW = 512
    NCH = 6 * D // NW
    ins = net.ins
    with phase(nc) as (sb, sem):
        cond = sb("cond", [P, 2, DT])
        sig = sb("sig", [P, 2, DT])
        act = sb("act", [P, DT, 2])
        wt = [sb(f"wt{b}", [P, DT, NW]) for b in range(2)]
        bias = [sb(f"bias{b}", [2, NW]) for b in range(2)]
        res = [sb(f"res{b}", [2, NW]) for b in range(2)]
        zrow = sb("zrow", [1, CS])
        cond_in, sig_done, act_done = sem("cond_in"), sem("sig_done"), sem("act_done")
        w_in = [sem(f"w_in{b}") for b in range(2)]
        w_used, sums, added, stored, zeroed, side = (sem(n) for n in
                                                     ("w_used", "sums", "added", "stored", "zeroed", "side"))
        with nc.Block() as block:
            @block.sync
            def _(sp):
                sp.dma_start(cond[:, 0, :], ins["c"].rearrange("o (p t) -> p (o t)", t=DT)).then_inc(cond_in, 16)
                sp.dma_start(cond[:, 1, :], ins["c_ctx"].rearrange("(p t) -> p t", t=DT)).then_inc(cond_in, 16)
                sp.sem_inc(w_used, 2)
                for layer in range(DEPTH):
                    w = ins["w_mod"][layer].rearrange("(p t) n -> p t n", t=DT)
                    with sp.Fori(0, NCH // 2) as i:
                        for b in range(2):
                            n = (i * 2 + b)
                            sp.wait_ge(w_used, n + (1 + layer * NCH))
                            sp.dma_start(wt[b][:], w[:, :, ds(n * NW, NW)]).then_inc(w_in[b], 16)
                            src = ins["b_mod"][layer][ds(n * NW, NW)].partition_broadcast(2)
                            sp.dma_start(bias[b][:], src).then_inc(w_in[b], 16)

            @block.gpsimd
            def _(pool):
                pool.memset(zrow[:], 0.0).then_inc(zeroed, 1)

            @block.scalar
            def _(act_e):
                act_e.wait_ge(cond_in, 32)
                act_e.activation(sig[:], cond[:], ACT.Sigmoid).then_inc(sig_done, 1)
                act_e.dma_start(net.x[0:CTX, :], ins["ctx"][0]).then_inc(side, 16)
                act_e.dma_start(net.x[CTX:TOK, :], ins["x"][0]).then_inc(side, 16)
                act_e.wait_ge(zeroed, 1)
                for r in (0, CTX + 1, PAD_ROWS - 1):
                    act_e.dma_start(net.p[r:r + 1, ATT:IN_W], zrow[:]).then_inc(side, 16)
                act_e.wait_ge(side, 5 * 16)
                for layer in range(DEPTH):
                    with act_e.Fori(0, NCH // 2) as i:
                        for b in range(2):
                            n = (i * 2 + b)
                            act_e.wait_ge(added, n + (1 + layer * NCH))
                            act_e.dma_start(net.mod[layer][:, ds(n * NW, NW)], res[b][:]).then_inc(stored, 16)
                            act_e.wait_ge(stored, (n + (3 + layer * NCH)) * 16)

            @block.vector
            def _(dve):
                dve.wait_ge(sig_done, 1)
                dve.tensor_tensor(act[:].rearrange("p t j -> p j t"), cond[:], sig[:], ALU.mult).then_inc(act_done, 1)
                dve.sem_inc(stored, 32)
                for layer in range(DEPTH):
                    with dve.Fori(0, NCH // 2) as i:
                        for b in range(2):
                            n = (i * 2 + b)
                            dve.wait_ge(sums, n + (1 + layer * NCH))
                            dve.wait_ge(stored, (n + (1 + layer * NCH)) * 16)
                            dve.tensor_tensor(res[b][:], ps[0:2, b, :], bias[b][:], ALU.add).then_inc(added, 1)

            @block.tensor
            def _(pe):
                pe.wait_ge(act_done, 1)
                for layer in range(DEPTH):
                    with pe.Fori(0, NCH // 2) as i:
                        for b in range(2):
                            n = (i * 2 + b)
                            pe.wait_ge(w_in[b], (i + 1 + layer * NCH // 2) * 32)
                            if b == 0 and layer == 0:
                                pass
                            for t in range(DT):
                                mm = pe.matmul(ps[0:2, b, :], act[:, t, :], wt[b][:, t, :],
                                               start=(t == 0), stop=(t == DT - 1))
                            mm.then_inc(sums, 1)
                            pe.wait_ge(added, n + (1 + layer * NCH))
                            pe.sem_inc(w_used, 1)



NCK = [(n, min(512, IN_W - n)) for n in range(0, IN_W, 512)]
FIRST = {"ctx": 0, "lat": CT}


def input_projection_phase(nc, net, ps, layer):
    ins = net.ins
    with phase(nc) as (sb, sem):
        w = sb("w", [P, DT, IN_W])
        ident = sb("ident", [P, P])
        gain = sb("gain", [P, D])
        G = sb("G", [P, 2, D])
        S = sb("S", [P, 2, D])
        x = sb("x", [P, D])
        h = sb("h", [P, D])
        hT = sb("hT", [P, DT, P])
        small = sb("small", [P, 4])
        po = sb("po", [P, IN_W])
        w_in, c_in, x_in, x_used = sem("w_in"), sem("c_in"), sem("x_in"), sem("x_used")
        mean_done, root_done, h_done = sem("mean_done"), sem("root_done"), sem("h_done")
        hT_ps, hT_done, prod, out_done, stored = (sem(n) for n in ("hT_ps", "hT_done", "prod", "out_done", "stored"))
        with nc.Block() as block:
            @block.sync
            def _(sp):
                sp.dma_start(ident[:], ins["k_ident"]).then_inc(c_in, 16)
                sp.dma_start(gain[:], ins["g_mix"][layer].partition_broadcast(P)).then_inc(c_in, 16)
                for j in range(2):
                    m = net.mod[layer][j]
                    sp.dma_start(S[:, j, :], m[0:D].partition_broadcast(P)).then_inc(c_in, 16)
                    sp.dma_start(G[:, j, :], m[D:2 * D].partition_broadcast(P)).then_inc(c_in, 16)
                sp.sem_inc(x_used, 1)
                for seg in ("ctx", "lat"):
                    r0, n, _ = tokens_of(seg)
                    with sp.Fori(0, n) as i:
                        sp.wait_ge(x_used, i + (1 + FIRST[seg]))
                        sp.dma_start(x[:], rows(net.x, i * P + r0)).then_inc(x_in, 16)

            @block.gpsimd
            def _(pool):
                for t in range(DT):
                    pool.dma_start(w[:, t, :], ins["w_in"][layer][t * P:(t + 1) * P, :]).then_inc(w_in, 16)

            @block.scalar
            def _(act):
                act.sem_inc(out_done, 6)
                act.sem_inc(stored, 16)
                for seg in ("ctx", "lat"):
                    _, n, pr = tokens_of(seg)
                    with act.Fori(0, n) as i:
                        k = i + (1 + FIRST[seg])
                        act.wait_ge(mean_done, k)
                        act.activation(small[:, 2:3], small[:, 1:2], ACT.Sqrt).then_inc(root_done, 1)
                        act.wait_ge(hT_ps, k * 2 + 2)
                        act.wait_ge(prod, (k - 1) * len(NCK) + 1)
                        act.activation(hT[:, 4:8, :], ps[:, 1, :].rearrange("p (t n) -> p t n", n=P),
                                       ACT.Copy).then_inc(hT_done, 1)
                        act.wait_ge(stored, k * 16)
                        for c, (c0, cn) in enumerate(NCK):
                            act.wait_ge(prod, (k - 1) * len(NCK) + (c + 2))
                            act.activation(po[:, c0:c0 + cn], ps[:, 2 + c % 6, 0:cn], ACT.Copy).then_inc(out_done, 1)
                        act.wait_ge(out_done, k * len(NCK) + 6)
                        act.dma_start(rows(net.p, i * P + pr), po[:]).then_inc(stored, 16)
                act.wait_ge(stored, 16 * (NT + 1))

            @block.vector
            def _(dve):
                dve.wait_ge(c_in, 16 * 6)
                for j in range(2):
                    dve.scalar_tensor_tensor(G[:, j, :], G[:, j, :], 1.0, gain[:], ALU.add, ALU.mult)
                dve.sem_inc(hT_ps, 2)
                dve.drain()
                for seg in ("ctx", "lat"):
                    _, n, _ = tokens_of(seg)
                    j = 1 if seg == "ctx" else 0
                    with dve.Fori(0, n) as i:
                        k = i + (1 + FIRST[seg])
                        dve.wait_ge(x_in, k * 16)
                        dve.wait_ge(hT_ps, (k - 1) * 2 + 2)
                        dve.scalar_tensor_tensor(h[:], x[:], 1.0, x[:], ALU.mult, ALU.mult, accum_out=small[:, 0:1])
                        dve.drain()
                        dve.tensor_scalar(small[:, 1:2], small[:, 0:1], 1.0 / D, EPS, ALU.mult, ALU.add
                                          ).then_inc(mean_done, 1)
                        dve.wait_ge(root_done, k)
                        dve.reciprocal(small[:, 3:4], small[:, 2:3])
                        dve.drain()
                        dve.scalar_tensor_tensor(h[:], x[:], small[:, 3:4], G[:, j, :], ALU.mult, ALU.mult
                                                 ).then_inc(x_used, 1)
                        dve.drain()
                        dve.tensor_tensor(h[:], h[:], S[:, j, :], ALU.add).then_inc(h_done, 1)
                        dve.wait_ge(hT_ps, k * 2 + 1)
                        dve.wait_ge(prod, (k - 1) * len(NCK) + 1)
                        dve.tensor_copy(hT[:, 0:4, :], ps[:, 0, :].rearrange("p (t n) -> p t n", n=P)
                                        ).then_inc(hT_done, 1)

            @block.tensor
            def _(pe):
                pe.sem_inc(prod, 1)
                pe.wait_ge(c_in, 16 * 6)
                for seg in ("ctx", "lat"):
                    _, n, _ = tokens_of(seg)
                    with pe.Fori(0, n) as i:
                        k = i + (1 + FIRST[seg])
                        pe.wait_ge(h_done, k)
                        for t in range(DT):
                            tr = pe.transpose(ps[:, t // 4, (t % 4) * P:(t % 4 + 1) * P],
                                              h[:, t * P:(t + 1) * P], ident[:])
                            if t % 4 == 3:
                                tr.then_inc(hT_ps, 1)
                        pe.wait_ge(hT_done, k * 2)
                        pe.wait_ge(w_in, 16 * DT)
                        for c, (c0, cn) in enumerate(NCK):
                            pe.wait_ge(out_done, (k - 1) * len(NCK) + (c + 1))
                            for t in range(DT):
                                mm = pe.matmul(ps[:, 2 + c % 6, 0:cn], hT[:, t, :], w[:, t, c0:c0 + cn],
                                               start=(t == 0), stop=(t == DT - 1))
                            mm.then_inc(prod, 1)



QK_W = A_Q + A_KV + 2 * B_Q
QB = QK_W // P
MAPS = 12
HEADS = 8
ORDER = [0, 1, 2, 3, 4, 5, 7, 6, 9, 8, 11, 10]
PLACE = [ORDER.index(m) for m in range(MAPS)]
FIRST_MAP = [0, 1, 2, 3, 4, 6, 8, 10]


def map_operands(m):
    if m < 4:
        return m % 2, 2, 64 * (m // 2), 64
    n = m - 4
    return 2 + n // 4, 5 + n // 4, 32 * (n % 4), 32


def attention_phase(nc, net, ps, layer):
    ins = net.ins
    lam_init = 0.8 - 0.6 * float(np.exp(-0.3 * layer))
    parts = [("ctx", CT)] * (layer < DEPTH - 1) + [("lat", NT)]
    tiles_before = {"ctx": 0, "lat": CT if layer < DEPTH - 1 else 0}
    n_tiles = tiles_before["lat"] + LT
    with phase(nc) as (sb, sem):
        ident = sb("ident", [P, P])
        QKT = sb("QKT", [P, QB, TOK])
        V = sb("V", [P, NT, A_KV + B_V])
        gains = sb("gains", [P, 6, HD])
        sub_gain = sb("sub_gain", [P, 4, HD])
        lam_in = sb("lam_in", [P, 4, 32])
        lam_pr = sb("lam_pr", [P, 2, 32])
        lam_s = sb("lam_s", [P, 4])
        neg_lam = sb("neg_lam", [P, 1])
        qk = sb("qk", [P, QK_W])
        rope = sb("rope", [P, 2, ROPE_W])
        turned = sb("turned", [P, QK_W])
        qkr = sb("qkr", [P, QK_W])
        small = sb("small", [P, 4, 6])
        qs = sb("qs", [P, 4, P])
        p = [sb(f"p{s}", [P, TOK]) for s in range(2)]
        pT = [sb(f"pT{s}", [P, TOK]) for s in range(2)]
        mx = sb("mx", [P, MAPS])
        nm = sb("nm", [P, MAPS])
        sums = sb("sums", [P, MAPS])
        cs = sb("cs", [P, 3, 4])
        rs = sb("rs", [P, HEADS])
        yo = sb("yo", [P, HEADS * HD])
        ysq = sb("ysq", [P, 4 * HD])
        yst = sb("yst", [P, 4, 4])
        c_in, v_in, lam_ready, lam_exp = sem("c_in"), sem("v_in"), sem("lam_ready"), sem("lam_exp")
        qk_in, qk_used, mean_done, root_done, qkr_done, qkr_ps, qkt_done = (
            sem(n) for n in ("qk_in", "qk_used", "mean_done", "root_done", "qkr_done", "qkr_ps", "qkt_done"))
        qs_done, scores, max_done, exp_done, comb_done = (
            sem(n) for n in ("qs_done", "scores", "max_done", "exp_done", "comb_done"))
        pT_ps, pT_done, pv_done, o_used = sem("pT_ps"), sem("pT_done"), sem("pv_done"), sem("o_used")
        y_mean, y_root, y_done, stored = sem("y_mean"), sem("y_root"), sem("y_done"), sem("stored")
        SCORE = [ps[:, 3 * s:3 * s + 3, :].rearrange("p b n -> p (b n)") for s in range(2)]
        O = ps[:, 7, :]
        with nc.Block() as block:
            @block.sync
            def _(sp):
                sp.dma_start(ident[:], ins["k_ident"]).then_inc(c_in, 16)
                for g, (src, n) in enumerate((("a_q_gain", 4), ("a_k_gain", 2))):
                    for h in range(n):
                        sp.dma_start(gains[:, 4 * g + h, :], ins[src][layer].partition_broadcast(P)
                                     ).then_inc(c_in, 16)
                for j, src in enumerate(("b_lq1", "b_lq2", "b_lk1", "b_lk2")):
                    sp.dma_start(lam_in[:, j, :], ins[src][layer].partition_broadcast(P)).then_inc(c_in, 16)
                for j in range(4):
                    sp.dma_start(sub_gain[:, j, :], ins["b_subln"][layer].partition_broadcast(P)
                                 ).then_inc(c_in, 16)
                sp.sem_inc(qk_used, 1)
                for seg in ("ctx", "lat"):
                    _, n, pr = tokens_of(seg)
                    with sp.Fori(0, n) as i:
                        sp.wait_ge(qk_used, i + (1 + FIRST[seg]))
                        src = rows(net.p, i * P + pr)
                        sp.dma_start(qk[:, 0:384], src[:, 0:384]).then_inc(qk_in, 16)
                        sp.dma_start(qk[:, 384:QK_W], src[:, 512:1024]).then_inc(qk_in, 16)
                        table = ins["k_rope"].rearrange("t (j w) -> t j w", j=2)
                        sp.dma_start(rope[:], table[ds(i * P, P), :, :]).then_inc(qk_in, 16)
                sp.sem_inc(stored, 16)
                for seg, _ in parts:
                    r0, n, _ = tokens_of(seg)
                    with sp.Fori(0, n) as i:
                        k = i + (1 + tiles_before[seg])
                        sp.wait_ge(y_done, k)
                        sp.dma_start(rows(net.y, i * P + r0)[:, 0:512], yo[:]).then_inc(stored, 16)
                sp.wait_ge(stored, (n_tiles + 1) * 16)

            @block.gpsimd
            def _(pool):
                for seg in ("ctx", "lat"):
                    _, n, pr = tokens_of(seg)
                    src = net.p[pr:pr + n * P, :].rearrange("(t p) n -> p t n", p=P)
                    t0 = FIRST[seg]
                    pool.dma_start(V[:, t0:t0 + n, 0:A_KV], src[:, :, 384:512]).then_inc(v_in, 16)
                    pool.dma_start(V[:, t0:t0 + n, A_KV:], src[:, :, 1024:1280]).then_inc(v_in, 16)
                pool.wait_ge(qkt_done, 2 * NT + 2)
                for seg, kt in parts:
                    r0, n, _ = tokens_of(seg)
                    with pool.Fori(0, n) as i:
                        k = i + (1 + tiles_before[seg])
                        pool.wait_ge(scores, (k - 1) * MAPS + 1)
                        pool.tensor_copy(qs[:, 0:2, :], QKT[:, 0:2, ds(i * P + r0, P)]).then_inc(qs_done, 1)
                        pool.tensor_copy(qs[:, 2:4, :], QKT[:, 3:5, ds(i * P + r0, P)]).then_inc(qs_done, 1)

            @block.scalar
            def _(act):
                act.wait_ge(lam_ready, 1)
                act.activation(lam_s[:, 2:4], lam_s[:, 0:2], ACT.Exp).then_inc(lam_exp, 1)
                for seg in ("ctx", "lat"):
                    with act.Fori(0, tokens_of(seg)[1]) as i:
                        k = i + (1 + FIRST[seg])
                        act.wait_ge(mean_done, k)
                        act.activation(small[:, 2, :], small[:, 1, :], ACT.Sqrt).then_inc(root_done, 1)
                        act.wait_ge(qkr_ps, k * 2)
                        act.activation(QKT[:, 4:7, ds(i * P + FIRST[seg] * P, P)],
                                       ps[:, 1, 0:3 * P].rearrange("p (t n) -> p t n", n=P),
                                       ACT.Copy).then_inc(qkt_done, 1)

                act.sem_inc(pT_done, 1)
                act.sem_inc(exp_done, 1)
                for seg, kt in parts:
                    nk = kt * P
                    with act.Fori(0, tokens_of(seg)[1]) as i:
                        k = i + (1 + tiles_before[seg])

                        def exp(m):
                            s = m % 2
                            act.wait_ge(max_done, (k - 1) * MAPS + (PLACE[m] + 1))
                            if m in (0,):
                                act.wait_ge(pT_ps, (k - 1) * HEADS + 1)
                            elif m == 1:
                                act.wait_ge(comb_done, (k - 1) * 4 + 1)
                            elif m < 6:
                                act.wait_ge(pT_ps, (k - 1) * HEADS + (m - 2 + 1) + 1)
                            elif s == 0:
                                act.wait_ge(pT_ps, (k - 1) * HEADS + (4 + (m - 6) // 2 + 1) + 1)
                            else:
                                act.wait_ge(comb_done, (k - 1) * 4 + ((m - 7) // 2 + 1) + 1)
                            scale = (HD if m < 4 else 32) ** -0.5
                            act.activation(p[s][:, 0:nk], SCORE[s][:, 0:nk], ACT.Exp, bias=nm[:, m:m + 1],
                                           scale=scale, accum_out=sums[:, m:m + 1]).then_inc(exp_done, 1)

                        def take(h):
                            s = h % 2 if h < 4 else 0
                            act.wait_ge(pT_ps, (k - 1) * HEADS + (h + 1) + 1)
                            act.wait_ge(pv_done, (k - 1) * HEADS + (h + 1))
                            act.activation(pT[h % 2][:, 0:nk], SCORE[s][:, 0:nk], ACT.Copy).then_inc(pT_done, 1)

                        for step in ("e0 e1 t0 e2 t1 e3 t2 e4 t3 e5 e7 t4 e6 e9 t5 e8 e11 t6 e10 t7").split():
                            (exp if step[0] == "e" else take)(int(step[1:]))
                        act.wait_ge(y_mean, k)
                        act.activation(yst[:, 2, :], yst[:, 1, :], ACT.Sqrt).then_inc(y_root, 1)

            @block.vector
            def _(dve):
                dve.sem_inc(comb_done, 1)
                dve.wait_ge(c_in, 16 * 15)
                dve.tensor_tensor(lam_pr[:], lam_in[:, 0:2, :], lam_in[:, 2:4, :], ALU.mult)
                dve.drain()
                dve.tensor_reduce(lam_s[:, 0:2], lam_pr[:], AX.X, ALU.add).then_inc(lam_ready, 1)
                dve.tensor_scalar(sub_gain[:], sub_gain[:], 1.0 - lam_init, None, ALU.mult)
                dve.wait_ge(lam_exp, 1)
                dve.scalar_tensor_tensor(neg_lam[:], lam_s[:, 3:4], -lam_init, lam_s[:, 2:3],
                                         ALU.add, ALU.subtract)
                for seg in ("ctx", "lat"):
                    with dve.Fori(0, tokens_of(seg)[1]) as i:
                        k = i + (1 + FIRST[seg])
                        A, B = slice(0, 384), slice(384, QK_W)
                        dve.wait_ge(qk_in, k * 48)
                        dve.tensor_tensor(turned[:, A], qk[:, A], qk[:, A], ALU.mult)
                        dve.drain()
                        dve.tensor_reduce(small[:, 0, :], turned[:, A].rearrange("p (h d) -> p h d", d=HD),
                                          AX.X, ALU.add)
                        dve.drain()
                        dve.tensor_scalar(small[:, 1, :], small[:, 0, :], 1.0 / HD, EPS, ALU.mult, ALU.add
                                          ).then_inc(mean_done, 1)
                        dve.wait_ge(root_done, k)
                        dve.reciprocal(small[:, 3, :], small[:, 2, :])
                        dve.drain()
                        heads = qk[:, A].rearrange("p (h d) -> p h d", d=HD)
                        dve.tensor_tensor(heads, heads, small[:, 3, :].unsqueeze(2).broadcast_to([P, 6, HD]), ALU.mult)
                        dve.drain()
                        dve.tensor_tensor(heads, heads, gains[:], ALU.mult)
                        dve.drain()
                        if seg == "lat":
                            for cols, q in ((A, 16), (B, 8)):
                                x4 = qk[:, cols].rearrange("p (b j q) -> p b j q", j=2, q=q)
                                t4 = turned[:, cols].rearrange("p (b j q) -> p b j q", j=2, q=q)
                                s4 = rope[:, 1, cols].rearrange("p (b j q) -> p b j q", j=2, q=q)
                                for j in range(2):
                                    dve.tensor_tensor(t4[:, :, j, :], x4[:, :, 1 - j, :], s4[:, :, j, :], ALU.mult)
                            dve.drain()
                            dve.tensor_tensor(qk[:], qk[:], rope[:, 0, :], ALU.mult)
                            dve.drain()
                            dve.tensor_tensor(qk[:], qk[:], turned[:], ALU.add)
                            dve.drain()
                        dve.tensor_copy(qkr[:, 0:A_Q].rearrange("p (g k d) -> p k g d", g=2, k=2),
                                        qk[:, 0:A_Q].rearrange("p (k g d) -> p k g d", g=2, k=2)).then_inc(qkr_done, 1)
                        dve.tensor_copy(qkr[:, A_Q:], qk[:, A_Q:]).then_inc(qkr_done, 1)
                        dve.wait_ge(qkr_done, k * 2)
                        dve.sem_inc(qk_used, 1)
                        dve.wait_ge(qkr_ps, k * 2)
                        dve.tensor_copy(QKT[:, 0:4, ds(i * P + FIRST[seg] * P, P)],
                                        ps[:, 0, :].rearrange("p (t n) -> p t n", n=P)).then_inc(qkt_done, 1)

                dve.sem_inc(o_used, 1)
                for seg, kt in parts:
                    nk = kt * P
                    with dve.Fori(0, tokens_of(seg)[1]) as i:
                        k = i + (1 + tiles_before[seg])

                        def find_max(m):
                            scale = (HD if m < 4 else 32) ** -0.5
                            dve.wait_ge(scores, (k - 1) * MAPS + (PLACE[m] + 1) + 1)
                            dve.tensor_reduce(mx[:, m:m + 1], SCORE[m % 2][:, 0:nk], AX.X, ALU.max)
                            dve.drain()
                            dve.tensor_scalar(nm[:, m:m + 1], mx[:, m:m + 1], -scale, None, ALU.mult
                                              ).then_inc(max_done, 1)

                        def combine(j):
                            m = 4 + 2 * j
                            dve.wait_ge(exp_done, (k - 1) * MAPS + (max(PLACE[m], PLACE[m + 1]) + 1) + 1)
                            dve.reciprocal(cs[:, 0, j:j + 1], sums[:, m + 1:m + 2])
                            dve.drain()
                            dve.tensor_tensor(cs[:, 1, j:j + 1], cs[:, 0, j:j + 1], sums[:, m:m + 1], ALU.mult)
                            dve.drain()
                            dve.tensor_tensor(cs[:, 2, j:j + 1], cs[:, 1, j:j + 1], neg_lam[:], ALU.mult)
                            dve.drain()
                            dve.scalar_tensor_tensor(p[0][:, 0:nk], p[1][:, 0:nk], cs[:, 2, j:j + 1],
                                                     p[0][:, 0:nk], ALU.mult, ALU.add).then_inc(comb_done, 1)

                        for step in "m0 m1 m2 m3 m4 m5 c0 m7 m6 c1 m9 m8 c2 m11 m10 c3".split():
                            (find_max if step[0] == "m" else combine)(int(step[1:]))
                        dve.reciprocal(rs[:, 0:4], sums[:, 0:4])
                        dve.reciprocal(rs[:, 4:8], sums[:, 4:12:2])
                        dve.drain()
                        dve.wait_ge(pv_done, k * HEADS + 2)
                        o3 = yo[:].rearrange("p (h d) -> p h d", d=HD)
                        dve.wait_ge(stored, k * 16)
                        dve.tensor_tensor(o3, O.rearrange("p (h d) -> p h d", d=HD),
                                          rs[:].unsqueeze(2).broadcast_to([P, HEADS, HD]), ALU.mult).then_inc(o_used, 1)
                        dve.drain()
                        yb = yo[:, 256:512]
                        dve.tensor_tensor(ysq[:], yb, yb, ALU.mult)
                        dve.drain()
                        dve.tensor_reduce(yst[:, 0, :], ysq[:].rearrange("p (h d) -> p h d", d=HD), AX.X, ALU.add)
                        dve.drain()
                        dve.tensor_scalar(yst[:, 1, :], yst[:, 0, :], 1.0 / HD, EPS, ALU.mult, ALU.add
                                          ).then_inc(y_mean, 1)
                        dve.wait_ge(y_root, k)
                        dve.reciprocal(yst[:, 3, :], yst[:, 2, :])
                        dve.drain()
                        dve.tensor_tensor(o3[:, 4:8, :], o3[:, 4:8, :],
                                          yst[:, 3, :].unsqueeze(2).broadcast_to([P, 4, HD]), ALU.mult)
                        dve.drain()
                        dve.tensor_tensor(o3[:, 4:8, :], o3[:, 4:8, :], sub_gain[:], ALU.mult).then_inc(y_done, 1)

            @block.tensor
            def _(pe):
                pe.wait_ge(c_in, 16 * 15)
                pe.sem_inc(qkt_done, 2)
                for seg in ("ctx", "lat"):
                    with pe.Fori(0, tokens_of(seg)[1]) as i:
                        k = i + (1 + FIRST[seg])
                        pe.wait_ge(qkr_done, k * 2)
                        pe.wait_ge(qkt_done, k * 2)
                        for t in range(QB):
                            tr = pe.transpose(ps[:, t // 4, (t % 4) * P:(t % 4 + 1) * P],
                                              qkr[:, t * P:(t + 1) * P], ident[:])
                            if t in (3, QB - 1):
                                tr.then_inc(qkr_ps, 1)

                pe.sem_inc(scores, 1)
                pe.sem_inc(pT_ps, 1)
                pe.sem_inc(pv_done, 2)
                pe.wait_ge(v_in, 64)
                pe.wait_ge(qkt_done, 2 * NT + 2)
                for seg, kt in parts:
                    nk = kt * P
                    with pe.Fori(0, tokens_of(seg)[1]) as i:
                        k = i + (1 + tiles_before[seg])

                        def score(m):
                            s = m % 2
                            if m == 0:
                                pe.wait_ge(pT_done, (k - 1) * HEADS + 1)
                            elif m == 1:
                                pe.wait_ge(exp_done, (k - 1) * MAPS + 1)
                            elif m < 6:
                                pe.wait_ge(pT_done, (k - 1) * HEADS + (m - 2 + 1) + 1)
                            elif s == 0:
                                pe.wait_ge(pT_done, (k - 1) * HEADS + (4 + (m - 6) // 2 + 1) + 1)
                            else:
                                pe.wait_ge(exp_done, (k - 1) * MAPS + (PLACE[m - 2] + 1) + 1)
                            q, kb, p0, n = map_operands(m)
                            for c in range(0, nk, 512):
                                w = min(512, nk - c)
                                mm = pe.matmul(SCORE[s][:, c:c + w], qs[p0:p0 + n, q, :],
                                               QKT[p0:p0 + n, kb, c:c + w], start=True, stop=True)
                            mm.then_inc(scores, 1)

                        def turn(h):
                            s = h % 2 if h < 4 else 0
                            if h < 4:
                                pe.wait_ge(exp_done, (k - 1) * MAPS + (PLACE[h] + 1) + 1)
                            else:
                                pe.wait_ge(comb_done, (k - 1) * 4 + (h - 4 + 1) + 1)
                            for t in range(kt):
                                tr = pe.transpose(SCORE[s][:, t * P:(t + 1) * P], p[s][:, t * P:(t + 1) * P], ident[:])
                            tr.then_inc(pT_ps, 1)

                        def weigh(h):
                            pe.wait_ge(pT_done, (k - 1) * HEADS + (h + 1) + 1)
                            v0 = HD * (h // 2) if h < 4 else A_KV + HD * (h - 4)
                            for t in range(kt):
                                mm = pe.matmul(O[:, h * HD:(h + 1) * HD], pT[h % 2][:, t * P:(t + 1) * P],
                                               V[:, t, v0:v0 + HD], start=(t == 0), stop=(t == kt - 1))
                            mm.then_inc(pv_done, 1)

                        pe.wait_ge(qs_done, k * 2)
                        todo = {"s": score, "t": turn, "w": weigh}
                        for step in ("s0 s1 t0 s2 O w0 t1 s3 w1 t2 s4 w2 t3 s5 w3 s7 t4 s6 w4 s9 t5 s8 w5 "
                                     "s11 t6 s10 w6 t7 w7").split():
                            if step == "O":
                                pe.wait_ge(o_used, k)
                            else:
                                todo[step[0]](int(step[1:]))



SCAN_R, SCAN_V, SCAN_A, SCAN_B, SCAN_K, SCAN_L = 0, CW, 2 * CW, 3 * CW, 5 * CW, 7 * CW
DECAY = float(np.exp(np.float32(-0.5)))


def heads_of(ap, n=CH):
    return ap.rearrange("p (h d) -> p h d", d=HD)


def rwkv_input_phase(nc, net, ps, layer):
    ins = net.ins
    with phase(nc) as (sb, sem):
        ident = sb("ident", [P, P])
        mu = sb("mu", [P, CS])
        w2, a2 = sb("w2", [P, CW]), sb("a2", [P, CW])
        g2 = sb("g2", [P, CW])
        w0, a0 = sb("w0", [P, NZ, CW]), sb("a0", [P, NZ, CW])
        kk_g, ka_g, rk_g = sb("kk_g", [P, CW]), sb("ka_g", [P, CW]), sb("rk_g", [P, CW])
        cur, prev, nxt = sb("cur", [P, CS]), sb("prev", [P, CS]), sb("nxt", [P, CS])
        mix = sb("mix", [P, CS])
        pf = sb("pf", [P, CS])
        lt = sb("lt", [P, 3, P])
        pre = sb("pre", [P, 4, CW])
        kks, sq, kka, rr, kd_sum, rks = (sb(n, [P, CW]) for n in ("kks", "sq", "kka", "rr", "kd_sum", "rks"))
        a_out = sb("a_out", [P, CW])
        b_out, k_out, l_out = sb("b_out", [P, NZ, CW]), sb("k_out", [P, NZ, CW]), sb("l_out", [P, NZ, CW])
        gb = sb("gb", [P, 2, CW])
        st = sb("st", [P, 5, CH])
        c_in, t_in, t_used, pf_done, lt_ps, lt_done = (sem(n) for n in
                                                       ("c_in", "t_in", "t_used", "pf_done", "lt_ps", "lt_done"))
        proj, pre_done, sig_done, ss_done, root_done, outs_done, stored = (
            sem(n) for n in ("proj", "pre_done", "sig_done", "ss_done", "root_done", "outs_done", "stored"))
        pool_done, kd_done, g_done = sem("pool_done"), sem("kd_done"), sem("g_done")
        bc = lambda name: ins[name][layer].partition_broadcast(P)
        R, K, Vv = pf[:, 0:CW], pf[:, CW:2 * CW], pf[:, 2 * CW:3 * CW]
        with nc.Block() as block:
            @block.sync
            def _(sp):
                sp.dma_start(ident[:], ins["k_ident"]).then_inc(c_in, 16)
                sp.dma_start(mu[:], bc("c_mu")).then_inc(c_in, 16)
                sp.dma_start(w2[:], ins["c_w2"][layer].rearrange("z r c -> (z r) c")).then_inc(c_in, 16)
                sp.dma_start(a2[:], ins["c_a2"][layer].rearrange("z r c -> (z r) c")).then_inc(c_in, 16)
                sp.dma_start(g2[:], ins["c_g2"][layer]).then_inc(c_in, 16)
                sp.dma_start(w0[:], bc("c_w0")).then_inc(c_in, 16)
                sp.dma_start(a0[:], bc("c_a0")).then_inc(c_in, 16)
                sp.dma_start(kk_g[:], bc("c_k_k")).then_inc(c_in, 16)
                sp.dma_start(ka_g[:], bc("c_k_a")).then_inc(c_in, 16)
                rk = ins["c_r_k"][layer].rearrange("h d -> (h d)").partition_broadcast(P)
                sp.dma_start(rk_g[:], rk).then_inc(c_in, 16)
                sp.sem_inc(t_used, 1)
                for seg in ("ctx", "lat"):
                    _, n, pr = tokens_of(seg)
                    with sp.Fori(0, n) as i:
                        sp.wait_ge(t_used, i + (1 + FIRST[seg]))
                        for buf, off in ((cur, 0), (prev, -1), (nxt, 1)):
                            sp.dma_start(buf[:], rows(net.p, i * P + (pr + off))[:, ATT:IN_W]).then_inc(t_in, 16)

            @block.gpsimd
            def _(pool):
                pool.wait_ge(c_in, 160)
                for seg in ("ctx", "lat"):
                    with pool.Fori(0, tokens_of(seg)[1]) as i:
                        k = i + (1 + FIRST[seg])
                        pool.wait_ge(pf_done, k)
                        pool.tensor_tensor(kka[:], K, ka_g[:], ALU.mult).then_inc(pool_done, 1)
                        pool.tensor_tensor(rr[:], R, rk_g[:], ALU.mult).then_inc(pool_done, 1)
                        pool.wait_ge(kd_done, k)
                        pool.tensor_tensor(kd_sum[:], k_out[:, 0, :], k_out[:, 1, :], ALU.add).then_inc(pool_done, 1)
                        pool.wait_ge(pool_done, k * 4 - 1)
                        pool.tensor_tensor(rks[:], rr[:], kd_sum[:], ALU.mult).then_inc(pool_done, 1)

            @block.scalar
            def _(act):
                act.sem_inc(stored, 16 * 7)
                for seg in ("ctx", "lat"):
                    r0, n, _ = tokens_of(seg)
                    with act.Fori(0, n) as i:
                        k = i + (1 + FIRST[seg])
                        act.wait_ge(lt_ps, k)
                        act.activation(lt[:, 0, :], ps[:, 0, 0:P], ACT.Tanh).then_inc(lt_done, 1)
                        act.activation(lt[:, 1, :], ps[:, 0, P:2 * P], ACT.Copy).then_inc(lt_done, 1)
                        act.activation(lt[:, 2, :], ps[:, 0, 2 * P:3 * P], ACT.Sigmoid).then_inc(lt_done, 1)
                        act.wait_ge(pre_done, k)
                        act.activation(pre[:], pre[:], ACT.Sigmoid).then_inc(sig_done, 1)
                        act.wait_ge(stored, k * 16 * 7)
                        act.wait_ge(proj, k * 2)
                        act.activation(gb[:, 0, :], ps[:, 5, :], ACT.Copy).then_inc(g_done, 1)
                        act.wait_ge(ss_done, k)
                        act.activation(st[:, 1, :], st[:, 0, :], ACT.Sqrt).then_inc(root_done, 1)
                        act.wait_ge(outs_done, k)
                        act.wait_ge(g_done, k)
                        o = rows(net.scan, i * P + r0)
                        for buf, c0, w in ((R, SCAN_R, CW), (Vv, SCAN_V, CW), (a_out[:], SCAN_A, CW),
                                           (b_out[:].rearrange("p z c -> p (z c)"), SCAN_B, 2 * CW),
                                           (k_out[:].rearrange("p z c -> p (z c)"), SCAN_K, 2 * CW),
                                           (l_out[:].rearrange("p z c -> p (z c)"), SCAN_L, 2 * CW)):
                            act.dma_start(o[:, c0:c0 + w], buf).then_inc(stored, 16)
                        act.dma_start(rows(net.gb, i * P + r0), gb[:].rearrange("p j c -> p (j c)")
                                      ).then_inc(stored, 16)
                act.wait_ge(stored, 16 * 7 * (NT + 1))

            @block.vector
            def _(dve):
                dve.wait_ge(c_in, 160)
                for seg in ("ctx", "lat"):
                    with dve.Fori(0, tokens_of(seg)[1]) as i:
                        k = i + (1 + FIRST[seg])
                        dve.wait_ge(t_in, k * 48)
                        dve.tensor_tensor(mix[:], prev[:], nxt[:], ALU.add)
                        dve.drain()
                        dve.scalar_tensor_tensor(mix[:], mix[:], 0.5, cur[:], ALU.mult, ALU.subtract)
                        dve.drain()
                        dve.tensor_tensor(mix[:], mix[:], mu[:], ALU.mult)
                        dve.drain()
                        dve.wait_ge(stored, k * 16 * 7)
                        dve.tensor_tensor(pf[:], cur[:], mix[:], ALU.add).then_inc(pf_done, 1)
                        dve.drain()
                        dve.sem_inc(t_used, 1)
                        dve.tensor_tensor(kks[:], K, kk_g[:], ALU.mult)
                        dve.drain()
                        dve.tensor_tensor(sq[:], kks[:], kks[:], ALU.mult)
                        dve.drain()
                        dve.tensor_reduce(st[:, 0, :], heads_of(sq[:]), AX.X, ALU.add).then_inc(ss_done, 1)
                        dve.wait_ge(proj, k * 2 - 1)
                        dve.tensor_tensor(pre[:, 0:2, :], ps[:, 1:3, :], w0[:], ALU.add)
                        dve.tensor_tensor(pre[:, 2:4, :], ps[:, 3:5, :], a0[:], ALU.add)
                        dve.drain()
                        dve.sem_inc(pre_done, 1)
                        dve.wait_ge(root_done, k)
                        dve.tensor_scalar(st[:, 2, :], st[:, 1, :], 1e-12, None, ALU.max)
                        dve.drain()
                        dve.reciprocal(st[:, 3, :], st[:, 2, :])
                        dve.drain()
                        dve.tensor_scalar(st[:, 4, :], st[:, 3, :], -1.0, None, ALU.mult)
                        dve.drain()
                        dve.tensor_tensor(heads_of(a_out[:]), heads_of(kks[:]),
                                          st[:, 4, :].unsqueeze(2).broadcast_to([P, CH, HD]), ALU.mult)
                        dve.wait_ge(pool_done, k * 4 - 3)
                        dve.wait_ge(sig_done, k)
                        dve.tensor_scalar(l_out[:], pre[:, 0:2, :], -DECAY, None, ALU.mult)
                        for z in range(NZ):
                            dve.scalar_tensor_tensor(k_out[:, z, :], pre[:, 2 + z, :], 1.0, kka[:],
                                                     ALU.subtract, ALU.mult)
                        dve.drain()
                        for z in range(NZ):
                            dve.tensor_tensor(k_out[:, z, :], k_out[:, z, :], K, ALU.add)
                            dve.scalar_tensor_tensor(b_out[:, z, :], a_out[:], -1.0, pre[:, 2 + z, :],
                                                     ALU.mult, ALU.mult)
                        dve.drain()
                        dve.sem_inc(kd_done, 1)
                        dve.wait_ge(pool_done, k * 4)
                        dve.tensor_reduce(st[:, 0, :], heads_of(rks[:]), AX.X, ALU.add)
                        dve.drain()
                        dve.tensor_tensor(heads_of(gb[:, 1, :]), heads_of(Vv),
                                          st[:, 0, :].unsqueeze(2).broadcast_to([P, CH, HD]), ALU.mult
                                          ).then_inc(outs_done, 1)

            @block.tensor
            def _(pe):
                pe.wait_ge(c_in, 160)
                for seg in ("ctx", "lat"):
                    with pe.Fori(0, tokens_of(seg)[1]) as i:
                        k = i + (1 + FIRST[seg])
                        pe.wait_ge(pf_done, k)
                        for t in range(3):
                            tr = pe.transpose(ps[:, 0, t * P:(t + 1) * P],
                                              pf[:, 3 * CW + t * P:3 * CW + (t + 1) * P], ident[:])
                        tr.then_inc(lt_ps, 1)
                        pe.wait_ge(lt_done, k * 3)
                        for j, w in enumerate((w2, a2)):
                            for z in range(NZ):
                                q = slice(64 * z, 64 * z + 64)
                                mm = pe.matmul(ps[:, 1 + 2 * j + z, :], lt[q, j, :], w[q, :], start=True, stop=True)
                        mm.then_inc(proj, 1)
                        pe.matmul(ps[:, 5, :], lt[:, 2, :], g2[:], start=True, stop=True).then_inc(proj, 1)


def scan_phase(nc, net, ps, layer):
    ins = net.ins
    last = layer == DEPTH - 1
    with phase(nc) as (sb, sem):
        ident = sb("ident", [P, P])
        tri = sb("tri", [C, NZ, 2 * P])
        mask = sb("mask", [P, NZ, P])
        levels = sb("levels", [P, LEVELS, NZ, C])
        ones = sb("ones", [C, 1])
        ra, kb = sb("ra", [P, NZ, CW]), sb("kb", [P, NZ, CW])
        v_raw = sb("v_raw", [C, NZ, CW])
        lw = sb("lw", [C, NZ, CW])
        e_ra, e_kb = sb("e_ra", [P, NZ, CW]), sb("e_kb", [P, NZ, CW])
        e_end = sb("e_end", [C, ST])
        rat, kbt = sb("rat", [P, NZ, CW]), sb("kbt", [P, NZ, CW])
        vu = sb("vu", [P, ST, C])
        rac, kbc = sb("rac", [C, ST, P]), sb("kbc", [C, ST, P])
        G = sb("G", [P, ST, P])
        at = sb("at", [P, 2, ST, C])
        T, TT, YI, X = (sb(n, [P, ST, C]) for n in ("T", "TT", "YI", "X"))
        state = sb("state", [C, ST, C])
        yo = sb("yo", [C, ST, C])
        hi = slice(C, P)
        pe_step, pool_step = sem("pe_step"), sem("pool_step")
        c_in, ones_set, in_sem, in_used, cums, exps, v_done, scaled = (
            sem(n) for n in ("c_in", "ones_set", "in_sem", "in_used", "cums", "exps", "v_done", "scaled"))
        turned, cm_done, g_ps, g_done, at_done, tt0_done = (
            sem(n) for n in ("turned", "cm_done", "g_ps", "g_done", "at_done", "tt0_done"))
        y_ps, yi_done, t_ps, t_done, tt_ps, tt_done = (
            sem(n) for n in ("y_ps", "yi_done", "t_ps", "t_done", "tt_ps", "tt_done"))
        x_ps, x_done, u_ps, u_done, out_ps, out_done, s_ps, s_done, stored = (
            sem(n) for n in ("x_ps", "x_done", "u_ps", "u_done", "out_ps", "out_done", "s_ps", "s_done", "stored"))
        segs = [("ctx", NC_CTX, 0, 0), ("lat", NC_LAT, CTX, NC_CTX)]
        zs = lambda z: slice(CH * z, CH * z + CH)
        stc = lambda t, s: t[:, s // CH, (s % CH) * HD:(s % CH + 1) * HD]
        bank = lambda b, z, part: ps[part, b + z, :].rearrange("p (h c) -> p h c", c=C)
        eye8 = ident[hi, C:P].unsqueeze(1).broadcast_to([C, CH, C])
        with nc.Block() as block:
            @block.sync
            def _(sp):
                sp.dma_start(ident[:], ins["k_ident"]).then_inc(c_in, 16)
                sp.dma_start(tri[:].rearrange("p z n -> p (z n)"), ins["k_tri"]).then_inc(c_in, 16)
                sp.dma_start(mask[:].rearrange("p z n -> p (z n)"), ins["k_mask"]).then_inc(c_in, 16)
                sp.dma_start(levels[hi].rearrange("p l z n -> p (l z n)"), ins["k_levels"]).then_inc(c_in, 16)
                sp.sem_inc(in_used, 1)
                for seg, n, r0, before in segs:
                    with sp.Fori(0, n) as i:
                        sp.wait_ge(in_used, i + (1 + before))
                        for z in range(NZ):
                            at_row = i * C + r0 if z == 0 else i * (-C) + (r0 + (n - 1) * C)
                            src = net.scan[ds(at_row, C), :]
                            for dst, c0 in ((lw[:, z, :], SCAN_L + z * CW), (ra[0:C, z, :], SCAN_R),
                                            (ra[hi, z, :], SCAN_A), (kb[0:C, z, :], SCAN_K + z * CW),
                                            (kb[hi, z, :], SCAN_B + z * CW), (v_raw[:, z, :], SCAN_V)):
                                sp.dma_start(dst, src[:, c0:c0 + CW]).then_inc(in_sem, 16)

            @block.gpsimd
            def _(pool):
                pool.memset(ones[:], 1.0).then_inc(ones_set, 1)
                pool.memset(state[:], 0.0).then_inc(ones_set, 1)
                pool.wait_ge(c_in, 64)
                for seg, n, r0, before in segs:
                    with pool.Fori(0, n) as i:
                        k = i + (1 + before)
                        pool.wait_ge(in_sem, k * 192)
                        pool.wait_ge(s_done, k)
                        pool.sem_inc(pool_step, 1)
                        pool.tensor_copy(vu[0:C].rearrange("p (z h) d -> p z (h d)", z=NZ), v_raw[:]).then_inc(v_done, 1)
                        for l in range(LEVELS):
                            pool.wait_ge(g_done, k * 2)
                            if l >= 2:
                                pool.wait_ge(y_ps, (k - 1) * 12 + 2 * (l - 1))
                            if l == 2:
                                pool.wait_ge(tt0_done, k * 2)
                            for z in range(NZ):
                                pool.tensor_tensor(at[hi, l % 2, zs(z), :], G[hi, zs(z), C:P],
                                                   levels[hi, l, z, :].unsqueeze(1).broadcast_to([C, CH, C]),
                                                   ALU.mult).then_inc(at_done, 1)

            @block.scalar
            def _(act):
                act.sem_inc(stored, 32)
                for seg, n, r0, before in segs:
                    emit = not (last and seg == "ctx")
                    with act.Fori(0, n) as i:
                        k = i + (1 + before)
                        act.wait_ge(cums, k)
                        act.activation(e_ra[:], ps[:, 0:2, :], ACT.Exp).then_inc(exps, 1)
                        act.activation(e_kb[:], ps[:, 2:4, :], ACT.Exp).then_inc(exps, 1)
                        act.activation(e_end[:], ps[0:C, 4, 0:ST], ACT.Exp).then_inc(exps, 1)
                        act.wait_ge(turned, k * 2 - 1)
                        act.activation(rac[:].rearrange("p s c -> p (s c)"),
                                       ps[0:C, 0:4, :].rearrange("p b n -> p (b n)"), ACT.Copy).then_inc(cm_done, 1)
                        for l in range(1, LEVELS):
                            for z in range(NZ):
                                if l < LEVELS - 1:
                                    act.wait_ge(t_ps, (k - 1) * 8 + (2 * (l - 1) + z + 1))
                                    act.activation(T[hi, zs(z), :], bank(6, z, hi), ACT.Copy).then_inc(t_done, 1)
                            for z in range(NZ):
                                act.wait_ge(tt_ps, (k - 1) * 10 + (2 * (l - 1) + z + 1))
                                act.activation(TT[hi, zs(z), :], bank(0, z, hi), ACT.Copy).then_inc(tt_done, 1)
                        for z in range(NZ):
                            act.wait_ge(x_ps, (k - 1) * 2 + (z + 1))
                            act.activation(X[hi, zs(z), :], bank(2, z, hi), ACT.Copy).then_inc(x_done, 1)
                        for z in range(NZ):
                            act.wait_ge(u_ps, (k - 1) * 2 + (z + 1))
                            act.activation(vu[hi, zs(z), :], bank(4, z, hi), ACT.Copy).then_inc(u_done, 1)
                        if emit:
                            act.wait_ge(out_ps, k - (NC_CTX if last else 0))
                            act.wait_ge(stored, (k - (NC_CTX if last else 0)) * 32)
                            act.activation(yo[:].rearrange("p (z h) c -> p z (h c)", z=NZ), ps[0:C, 6:8, :], ACT.Copy
                                           ).then_inc(out_done, 1)
                            act.wait_ge(out_done, k + (1 - (NC_CTX if last else 0)))
                            for z in range(NZ):
                                at_row = i * C + r0 if z == 0 else i * (-C) + (r0 + (n - 1) * C)
                                act.dma_start(net.yd[z][ds(at_row, C), :],
                                              yo[:, zs(z), :].rearrange("p h c -> p (h c)")).then_inc(stored, 16)
                act.wait_ge(stored, 32 * (NC_LAT + (0 if last else NC_CTX) + 1))

            @block.vector
            def _(dve):
                dve.wait_ge(c_in, 64)
                dve.wait_ge(ones_set, 2)
                dve.sem_inc(s_done, 1)
                for seg, n, r0, before in segs:
                    with dve.Fori(0, n) as i:
                        k = i + (1 + before)
                        dve.wait_ge(in_sem, k * 192)
                        dve.wait_ge(exps, k * 3 - 2)
                        dve.tensor_tensor(rat[:], ra[:], e_ra[:], ALU.mult).then_inc(scaled, 1)
                        dve.wait_ge(exps, k * 3 - 1)
                        dve.tensor_tensor(kbt[:], kb[:], e_kb[:], ALU.mult).then_inc(scaled, 1)
                        dve.wait_ge(v_done, k)
                        dve.wait_ge(scaled, k * 2)
                        dve.sem_inc(in_used, 1)
                        dve.wait_ge(turned, k * 2)
                        dve.tensor_copy(kbc[:].rearrange("p s c -> p (s c)"),
                                        ps[0:C, 4:8, :].rearrange("p b n -> p (b n)")).then_inc(cm_done, 1)
                        for z in range(NZ):
                            dve.wait_ge(g_ps, (k - 1) * 2 + (z + 1))
                            dve.tensor_tensor(G[:, zs(z), :],
                                              ps[:, 2 * z:2 * z + 2, :].rearrange("p b (s n) -> p (b s) n", n=P),
                                              mask[:, z, :].unsqueeze(1).broadcast_to([P, CH, P]), ALU.mult
                                              ).then_inc(g_done, 1)
                        for z in range(NZ):
                            dve.wait_ge(at_done, (k - 1) * 12 + (z + 1))
                            dve.tensor_tensor(TT[hi, zs(z), :], at[hi, 0, zs(z), :], eye8, ALU.add
                                              ).then_inc(tt0_done, 1)
                        for l in range(LEVELS):
                            dst = T if l == 0 else YI
                            for z in range(NZ):
                                dve.wait_ge(y_ps, (k - 1) * 12 + (2 * l + z + 1))
                                dve.tensor_tensor(dst[hi, zs(z), :], bank(4, z, hi), eye8, ALU.add
                                                  ).then_inc(yi_done, 1)
                        dve.wait_ge(s_ps, k)
                        dve.tensor_tensor(state[:].rearrange("p (z h) c -> p z (h c)", z=NZ),
                                          state[:].rearrange("p (z h) c -> p z (h c)", z=NZ),
                                          ps[0:C, 0:2, :], ALU.add)
                        dve.drain()
                        dve.tensor_tensor(state[:], state[:], e_end[:].unsqueeze(2).broadcast_to([C, ST, C]),
                                          ALU.mult).then_inc(s_done, 1)

            @block.tensor
            def _(pe):
                pe.wait_ge(c_in, 64)
                pe.sem_inc(out_done, 1)
                for seg, n, r0, before in segs:
                    emit = not (last and seg == "ctx")
                    with pe.Fori(0, n) as i:
                        k = i + (1 + before)
                        pe.wait_ge(in_sem, k * 192)
                        pe.wait_ge(s_done, k)
                        if emit:
                            pe.wait_ge(out_done, k - (NC_CTX if last else 0))
                        for z in range(NZ):
                            pe.matmul(ps[:, z, :], tri[:, z, 0:P], lw[:, z, :], start=True, stop=True)
                            pe.matmul(ps[:, 2 + z, :], tri[:, z, P:2 * P], lw[:, z, :], start=True, stop=True)
                        for s in range(ST):
                            mm = pe.matmul(ps[0:C, 4, s:s + 1], stc(lw, s), ones[:], start=True, stop=True)
                        mm.then_inc(cums, 1)
                        pe.wait_ge(exps, k * 3)
                        for j, src in enumerate((rat, kbt)):
                            pe.wait_ge(scaled, k * 2 - 1 + j)
                            pe.sem_inc(pe_step, 1)
                            for s in range(ST):
                                tr = pe.transpose(ps[0:C, 4 * j + s // 4, (s % 4) * P:(s % 4 + 1) * P],
                                                  stc(src, s), ident[:])
                            tr.then_inc(turned, 1)
                        pe.wait_ge(cm_done, k * 2)
                        for s in range(ST):
                            mm = pe.matmul(ps[:, s // 4, (s % 4) * P:(s % 4 + 1) * P], kbc[:, s, :], rac[:, s, :],
                                           start=True, stop=True)
                            if s % CH == CH - 1:
                                mm.then_inc(g_ps, 1)
                        for l in range(LEVELS):
                            for z in range(NZ):
                                pe.wait_ge(at_done, (k - 1) * 12 + (2 * l + z + 1))
                                if l == 1:
                                    pe.wait_ge(yi_done, (k - 1) * 12 + (z + 1))
                                elif l > 1:
                                    pe.wait_ge(t_done, (k - 1) * 8 + (2 * (l - 2) + z + 1))
                                pe.sem_inc(pe_step, 1)
                                for h in range(CH):
                                    s = CH * z + h
                                    rhs = ident[hi, C:P] if l == 0 else T[hi, s, :]
                                    mm = pe.matmul(bank(4, z, hi)[:, h, :], at[hi, l % 2, s, :], rhs,
                                                   start=True, stop=True)
                                mm.then_inc(y_ps, 1)
                            if l == 0:
                                continue
                            if l < LEVELS - 1:
                                for z in range(NZ):
                                    pe.wait_ge(yi_done, (k - 1) * 12 + (2 * l + z + 1))
                                    if l == 1:
                                        pe.wait_ge(tt0_done, (k - 1) * 2 + (z + 1))
                                    else:
                                        pe.wait_ge(tt_done, (k - 1) * 10 + (2 * (l - 2) + z + 1))
                                    pe.sem_inc(pe_step, 1)
                                    for h in range(CH):
                                        s = CH * z + h
                                        mm = pe.matmul(bank(6, z, hi)[:, h, :], TT[hi, s, :], YI[hi, s, :],
                                                       start=True, stop=True)
                                    mm.then_inc(t_ps, 1)
                            for z in range(NZ):
                                pe.wait_ge(yi_done, (k - 1) * 12 + (2 * l + z + 1))
                                if l > 1:
                                    pe.wait_ge(tt_done, (k - 1) * 10 + (2 * (l - 2) + z + 1))
                                pe.sem_inc(pe_step, 1)
                                for h in range(CH):
                                    s = CH * z + h
                                    mm = pe.matmul(bank(0, z, hi)[:, h, :], YI[hi, s, :], TT[hi, s, :],
                                                   start=True, stop=True)
                                mm.then_inc(tt_ps, 1)
                        pe.wait_ge(v_done, k)
                        pe.sem_inc(pe_step, 1)
                        for z in range(NZ):
                            for h in range(CH):
                                s = CH * z + h
                                pe.matmul(bank(2, z, hi)[:, h, :], rac[:, s, C:P], state[:, s, :],
                                          start=True, stop=False)
                                mm = pe.matmul(bank(2, z, hi)[:, h, :], G[0:C, s, C:P], vu[0:C, s, :],
                                               start=False, stop=True)
                            mm.then_inc(x_ps, 1)
                        for z in range(NZ):
                            pe.wait_ge(x_done, (k - 1) * 2 + (z + 1))
                            pe.wait_ge(tt_done, k * 10 - 1 + z)
                            pe.sem_inc(pe_step, 1)
                            for h in range(CH):
                                s = CH * z + h
                                mm = pe.matmul(bank(4, z, hi)[:, h, :], TT[hi, s, :], X[hi, s, :],
                                               start=True, stop=True)
                            mm.then_inc(u_ps, 1)
                        pe.wait_ge(u_done, k * 2)
                        pe.sem_inc(pe_step, 1)
                        if emit:
                            for s in range(ST):
                                y = bank(6, s // CH, slice(0, C))[:, s % CH, :]
                                pe.matmul(y, rac[:, s, 0:C], state[:, s, :], start=True, stop=False)
                                mm = pe.matmul(y, G[:, s, 0:C], vu[:, s, :], start=False, stop=True)
                            mm.then_inc(out_ps, 1)
                        for s in range(ST):
                            mm = pe.matmul(bank(0, s // CH, slice(0, C))[:, s % CH, :], stc(kbt, s), vu[:, s, :],
                                           start=True, stop=True)
                        mm.then_inc(s_ps, 1)



def mix_output_phase(nc, net, ps, layer):
    ins = net.ins
    last = layer == DEPTH - 1
    segs = [("lat", 0)] if last else [("ctx", 0), ("lat", CT)]
    n_all = LT if last else NT
    RW = NG + NE
    BIG = 1e30
    with phase(nc) as (sb, sem):
        ident = sb("ident", [P, P])
        w = sb("w", [P, DT, D])
        wr = sb("wr", [P, DT, RW])
        br = sb("br", [P, RW])
        rev = sb("rev", [P, RW])
        lnw, lnb = sb("lnw", [P, CW]), sb("lnb", [P, CW])
        gain = sb("gain", [P, D])
        GA, G, S = sb("GA", [P, 2, D]), sb("G", [P, 2, D]), sb("S", [P, 2, D])
        y = sb("y", [P, D])
        y2 = sb("y2", [P, CW])
        gb = sb("gb", [P, 2, CW])
        ysq = sb("ysq", [P, CW])
        st = sb("st", [P, 6, CH])
        yT, fT = sb("yT", [P, DT, P]), sb("fT", [P, DT, P])
        x, f, fs = sb("x", [P, D]), sb("f", [P, D]), sb("fs", [P, D])
        small = sb("small", [P, 4])
        lg = sb("lg", [P, RW])
        sel = sb("sel", [P, 4, RW])
        r1 = sb("r1", [P, 16])
        ex = sb("ex", [P, 2, NG + 1])
        c_in, c_ready, y_in, y_used, x_in, x_used, x_stored = (
            sem(n) for n in ("c_in", "c_ready", "y_in", "y_used", "x_in", "x_used", "x_stored"))
        var_done, root_done, y_done, y_ps, yT_done, prod = (
            sem(n) for n in ("var_done", "root_done", "y_done", "y_ps", "yT_done", "prod"))
        x_done, f_var, f_root, f_done, f_ps, fT_done, lg_ps, f_stored = (
            sem(n) for n in ("x_done", "f_var", "f_root", "f_done", "f_ps", "fT_done", "lg_ps", "f_stored"))
        diff_done, exp_done = sem("diff_done"), sem("exp_done")
        NCON = 16
        with nc.Block() as block:
            @block.sync
            def _(sp):
                bc = lambda ap: ap.partition_broadcast(P)
                sp.dma_start(ident[:], ins["k_ident"]).then_inc(c_in, 16)
                sp.dma_start(w[:], ins["w_out"][layer].rearrange("(t p) n -> p t n", p=P)).then_inc(c_in, 16)
                sp.dma_start(wr[:, :, 0:NG], ins["r_w_group"][layer].rearrange("(t p) n -> p t n", p=P)
                             ).then_inc(c_in, 16)
                sp.dma_start(wr[:, :, NG:], ins["r_w_expert"][layer].rearrange("(t p) n -> p t n", p=P)
                             ).then_inc(c_in, 16)
                sp.dma_start(br[:, 0:NG], bc(ins["r_b_group"][layer])).then_inc(c_in, 16)
                sp.dma_start(br[:, NG:], bc(ins["r_b_expert"][layer])).then_inc(c_in, 16)
                sp.dma_start(rev[:], bc(ins["k_rev"])).then_inc(c_in, 16)
                sp.dma_start(lnw[:], bc(ins["c_ln_w"][layer])).then_inc(c_in, 16)
                sp.dma_start(lnb[:], bc(ins["c_ln_b"][layer])).then_inc(c_in, 16)
                sp.dma_start(gain[:], bc(ins["g_ffn"][layer])).then_inc(c_in, 16)
                for j in range(2):
                    m = net.mod[layer][j]
                    sp.dma_start(GA[:, j, :], bc(m[2 * D:3 * D])).then_inc(c_in, 16)
                    sp.dma_start(S[:, j, :], bc(m[3 * D:4 * D])).then_inc(c_in, 16)
                    sp.dma_start(G[:, j, :], bc(m[4 * D:5 * D])).then_inc(c_in, 16)
                sp.sem_inc(y_used, 1)
                sp.sem_inc(x_stored, 16)
                for seg, before in segs:
                    r0, n, _ = tokens_of(seg)
                    with sp.Fori(0, n) as i:
                        k = i + (1 + before)
                        r = i * P + r0
                        sp.wait_ge(y_used, k)
                        sp.dma_start(y[:, 0:CW], rows(net.y, r)[:, 0:CW]).then_inc(y_in, 16)
                        sp.dma_start(y[:, CW:D], rows(net.yd[0], r)).then_inc(y_in, 16)
                        sp.dma_start(y2[:], rows(net.yd[1], r)).then_inc(y_in, 16)
                        sp.dma_start(gb[:].rearrange("p j c -> p (j c)"), rows(net.gb, r)).then_inc(y_in, 16)
                        sp.wait_ge(x_stored, k * 16)
                        sp.wait_ge(x_used, k)
                        sp.dma_start(x[:], rows(net.x, r)).then_inc(x_in, 16)

            @block.scalar
            def _(act):
                act.sem_inc(f_stored, 16)
                for seg, before in segs:
                    r0, n, _ = tokens_of(seg)
                    with act.Fori(0, n) as i:
                        k = i + (1 + before)
                        act.wait_ge(var_done, k)
                        act.activation(st[:, 3, :], st[:, 2, :], ACT.Sqrt).then_inc(root_done, 1)
                        act.wait_ge(y_ps, k * 2)
                        act.activation(yT[:, 4:8, :], ps[:, 1, :].rearrange("p (t n) -> p t n", n=P),
                                       ACT.Copy).then_inc(yT_done, 1)
                        act.wait_ge(x_done, k)
                        act.dma_start(rows(net.x, i * P + r0), x[:]).then_inc(x_stored, 16)
                        act.wait_ge(f_var, k)
                        act.activation(small[:, 2:3], small[:, 1:2], ACT.Sqrt).then_inc(f_root, 1)
                        act.wait_ge(f_ps, k * 2)
                        act.activation(fT[:, 4:8, :], ps[:, 5, :].rearrange("p (t n) -> p t n", n=P),
                                       ACT.Copy).then_inc(fT_done, 1)
                        act.dma_start(rows(net.f, i * P + r0), f[:]).then_inc(f_stored, 16)
                        act.wait_ge(diff_done, k)
                        act.activation(ex[:, 1, :], ex[:, 0, :], ACT.Exp).then_inc(exp_done, 1)
                act.wait_ge(f_stored, 16 * (n_all + 1))
                act.wait_ge(x_stored, 16 * (n_all + 1))

            @block.vector
            def _(dve):
                dve.wait_ge(c_in, 16 * NCON)
                for j in range(2):
                    dve.scalar_tensor_tensor(G[:, j, :], G[:, j, :], 1.0, gain[:], ALU.add, ALU.mult)
                dve.sem_inc(x_used, 1)
                for seg, before in segs:
                    r0, n, _ = tokens_of(seg)
                    j = 1 if seg == "ctx" else 0
                    with dve.Fori(0, n) as i:
                        k = i + (1 + before)
                        tile = i + r0 // P
                        yc = y[:, CW:D]
                        b8 = lambda q: st[:, q, :].unsqueeze(2).broadcast_to([P, CH, HD])
                        dve.wait_ge(y_in, k * 64)
                        dve.tensor_tensor(yc, yc, y2[:], ALU.add)
                        dve.drain()
                        dve.tensor_reduce(st[:, 0, :], heads_of(yc), AX.X, ALU.add)
                        dve.drain()
                        dve.tensor_scalar(st[:, 1, :], st[:, 0, :], -1.0 / HD, None, ALU.mult)
                        dve.drain()
                        dve.tensor_tensor(heads_of(yc), heads_of(yc), b8(1), ALU.add)
                        dve.drain()
                        dve.tensor_tensor(ysq[:], yc, yc, ALU.mult)
                        dve.drain()
                        dve.tensor_reduce(st[:, 0, :], heads_of(ysq[:]), AX.X, ALU.add)
                        dve.drain()
                        dve.tensor_scalar(st[:, 2, :], st[:, 0, :], 1.0 / HD, GN_EPS, ALU.mult, ALU.add
                                          ).then_inc(var_done, 1)
                        dve.wait_ge(root_done, k)
                        dve.reciprocal(st[:, 4, :], st[:, 3, :])
                        dve.drain()
                        dve.tensor_tensor(heads_of(yc), heads_of(yc), b8(4), ALU.mult)
                        dve.drain()
                        dve.tensor_tensor(yc, yc, lnw[:], ALU.mult)
                        dve.drain()
                        dve.tensor_tensor(yc, yc, lnb[:], ALU.add)
                        dve.drain()
                        dve.tensor_tensor(yc, yc, gb[:, 1, :], ALU.add)
                        dve.drain()
                        dve.tensor_tensor(yc, yc, gb[:, 0, :], ALU.mult).then_inc(y_done, 1)
                        dve.wait_ge(y_ps, k * 2)
                        dve.tensor_copy(yT[:, 0:4, :], ps[:, 0, :].rearrange("p (t n) -> p t n", n=P)
                                        ).then_inc(yT_done, 1)
                        dve.sem_inc(y_used, 1)
                        dve.wait_ge(prod, k)
                        dve.tensor_tensor(fs[:], ps[:, 2:4, :], GA[:, j, :].rearrange("p (a n) -> p a n", a=2), ALU.mult)
                        dve.drain()
                        dve.wait_ge(x_in, k * 16)
                        dve.tensor_tensor(x[:], x[:], fs[:], ALU.add).then_inc(x_done, 1)
                        dve.drain()
                        dve.scalar_tensor_tensor(fs[:], x[:], 1.0, x[:], ALU.mult, ALU.mult, accum_out=small[:, 0:1])
                        dve.drain()
                        dve.tensor_scalar(small[:, 1:2], small[:, 0:1], 1.0 / D, EPS, ALU.mult, ALU.add
                                          ).then_inc(f_var, 1)
                        dve.wait_ge(f_root, k)
                        dve.reciprocal(small[:, 3:4], small[:, 2:3])
                        dve.drain()
                        dve.scalar_tensor_tensor(fs[:], x[:], small[:, 3:4], G[:, j, :], ALU.mult, ALU.mult)
                        dve.drain()
                        dve.wait_ge(f_stored, k * 16)
                        dve.tensor_tensor(f[:], fs[:], S[:, j, :], ALU.add).then_inc(f_done, 1)
                        dve.sem_inc(x_used, 1)
                        dve.wait_ge(f_ps, k * 2 - 1)
                        dve.tensor_copy(fT[:, 0:4, :], ps[:, 4, :].rearrange("p (t n) -> p t n", n=P)
                                        ).then_inc(fT_done, 1)
                        dve.wait_ge(lg_ps, k)
                        dve.tensor_tensor(lg[:], ps[:, 6, 0:RW], br[:], ALU.add)
                        dve.drain()
                        gl, el = lg[:, 0:NG], lg[:, NG:]
                        el3 = el.rearrange("p (g e) -> p g e", g=NG)

                        def first_largest(v, r, top, out, at):
                            w_ = v.shape[-1]
                            dve.tensor_reduce(r1[:, top:top + 1], v, AX.X, ALU.max)
                            dve.drain()
                            c_ = sel[:, at, 0:w_]
                            dve.scalar_tensor_tensor(c_, v, r1[:, top:top + 1], r, ALU.is_equal, ALU.mult)
                            dve.drain()
                            dve.tensor_reduce(r1[:, top + 1:top + 2], c_, AX.X, ALU.max)
                            dve.drain()
                            dve.tensor_scalar(out, c_, r1[:, top + 1:top + 2], None, ALU.is_equal)
                            dve.drain()

                        pick = sel[:, 1, 0:NG]
                        first_largest(gl, rev[:, 0:NG], 0, pick, 0)
                        dve.tensor_scalar(ex[:, 0, 0:NG], gl, r1[:, 0:1], None, ALU.subtract)
                        dve.tensor_scalar(sel[:, 2, 0:NG], pick, 1.0, BIG, ALU.subtract, ALU.mult)
                        dve.drain()
                        dve.tensor_tensor(el3, el3, sel[:, 2, 0:NG].unsqueeze(2).broadcast_to([P, NG, EPG]), ALU.add)
                        dve.drain()
                        one, two = sel[:, 1, 0:NE], sel[:, 3, 0:NE]
                        first_largest(el, rev[:, NG:], 2, one, 0)
                        dve.tensor_copy(net.chosen[:, ds(tile, 1), 0, :], one.unsqueeze(1))
                        dve.scalar_tensor_tensor(el, one, -2.0 * BIG, el, ALU.mult, ALU.add)
                        dve.drain()
                        first_largest(el, rev[:, NG:], 4, two, 0)
                        dve.tensor_copy(net.chosen[:, ds(tile, 1), 1, :], two.unsqueeze(1))
                        dve.tensor_tensor(ex[:, 0, NG:NG + 1], r1[:, 4:5], r1[:, 2:3], ALU.subtract
                                          ).then_inc(diff_done, 1)
                        dve.wait_ge(exp_done, k)
                        dve.tensor_reduce(r1[:, 8:9], ex[:, 1, 0:NG], AX.X, ALU.add)
                        dve.tensor_scalar(r1[:, 9:10], ex[:, 1, NG:NG + 1], 1.0, None, ALU.add)
                        dve.drain()
                        dve.tensor_tensor(r1[:, 10:11], r1[:, 8:9], r1[:, 9:10], ALU.mult)
                        dve.drain()
                        dve.reciprocal(r1[:, 11:12], r1[:, 10:11])
                        dve.drain()
                        dve.tensor_tensor(r1[:, 12:13], r1[:, 11:12], ex[:, 1, NG:NG + 1], ALU.mult)
                        dve.drain()
                        dve.tensor_copy(net.gate[:, ds(tile, 1), :], r1[:, 11:13].unsqueeze(1))
                        dve.drain()

            @block.tensor
            def _(pe):
                pe.wait_ge(c_in, 16 * NCON)
                for seg, before in segs:
                    with pe.Fori(0, tokens_of(seg)[1]) as i:
                        k = i + (1 + before)
                        pe.wait_ge(y_done, k)
                        for t in range(DT):
                            tr = pe.transpose(ps[:, t // 4, (t % 4) * P:(t % 4 + 1) * P], y[:, t * P:(t + 1) * P], ident[:])
                            if t % 4 == 3:
                                tr.then_inc(y_ps, 1)
                        pe.wait_ge(yT_done, k * 2)
                        for c in range(2):
                            for t in range(DT):
                                mm = pe.matmul(ps[:, 2 + c, :], yT[:, t, :], w[:, t, c * 512:(c + 1) * 512],
                                               start=(t == 0), stop=(t == DT - 1))
                        mm.then_inc(prod, 1)
                        pe.wait_ge(f_done, k)
                        for t in range(DT):
                            tr = pe.transpose(ps[:, 4 + t // 4, (t % 4) * P:(t % 4 + 1) * P],
                                              f[:, t * P:(t + 1) * P], ident[:])
                            if t % 4 == 3:
                                tr.then_inc(f_ps, 1)
                        pe.wait_ge(fT_done, k * 2)
                        for t in range(DT):
                            mm = pe.matmul(ps[:, 6, 0:RW], fT[:, t, :], wr[:, t, :], start=(t == 0), stop=(t == DT - 1))
                        mm.then_inc(lg_ps, 1)


def placement_phase(nc, net, ps, layer):
    ins = net.ins
    t0 = CT if layer == DEPTH - 1 else 0
    n = NT - t0
    with phase(nc) as (sb, sem):
        ident, before, ones = sb("ident", [P, P]), sb("before", [P, P]), sb("ones", [P, P])
        before_e = sb("before_e", [NE, NE])
        e_row = sb("e_row", [P, NE])
        j_row = sb("j_row", [1, OVER])
        both = sb("both", [P, NT, NE])
        rank, place, w = sb("rank", [P, NT, NE]), sb("place", [P, NT, NE]), sb("w", [P, NT, NE])
        count, nov, shift = sb("count", [P, NE]), sb("nov", [P, NE]), sb("shift", [P, NE])
        novT = sb("novT", [NE, P])
        end = sb("end", [P, NE])
        cmp = sb("cmp", [1, OVER, NE])
        blk = sb("blk", [1, OVER + 1])
        rowf = sb("rowf", [P, NT, 2])
        token = sb("token", [P, NT], I32)
        zero = sb("zero", [P, NB], I32)
        c_in, both_done, rank_ps, nov_done, novT_ps, novT_done, ov_ps, rows_done, cleared, scattered, pool_c = (
            sem(s) for s in ("c_in", "both_done", "rank_ps", "nov_done", "novT_ps", "novT_done", "ov_ps",
                             "rows_done", "cleared", "scattered", "pool_c"))
        with nc.Block() as block:
            @block.sync
            def _(sp):
                sp.dma_start(ident[:], ins["k_ident"]).then_inc(c_in, 16)
                sp.dma_start(before[:], ins["k_before"]).then_inc(c_in, 16)
                sp.dma_start(before_e[:], ins["k_before_e"]).then_inc(c_in, 16)
                sp.dma_start(e_row[:], ins["k_e_row"].partition_broadcast(P)).then_inc(c_in, 16)
                sp.dma_start(j_row[:], ins["k_j_row"].partition_broadcast(1)).then_inc(c_in, 16)
                sp.wait_ge(pool_c, 3)
                sp.dma_start(net.table.rearrange("(p b) o -> p (b o)", p=P), zero[:]).then_inc(cleared, 16)

            @block.gpsimd
            def _(pool):
                pool.memset(ones[:], 1.0).then_inc(pool_c, 1)
                pool.memset(zero[:], 0).then_inc(pool_c, 1)
                pool.iota(token[:], pattern=[[P, NT]], base=0, channel_multiplier=1).then_inc(pool_c, 1)
                pool.wait_ge(pool_c, 3)
                pool.wait_ge(cleared, 16)
                pool.wait_ge(rows_done, 1)
                for t in range(t0, NT):
                    for j in range(2):
                        pool.indirect_dma_start(net.table, bass.IndirectOffsetOnAxis(net.row[:, t, j:j + 1], 0),
                                                token[:, t:t + 1], None).then_inc(scattered, 16)
                pool.wait_ge(scattered, 16 * 2 * n)

            @block.vector
            def _(dve):
                T = slice(t0, NT)
                dve.tensor_tensor(both[:, T], net.chosen[:, T, 0, :], net.chosen[:, T, 1, :], ALU.add
                                  ).then_inc(both_done, 1)
                dve.wait_ge(rank_ps, 1)
                dve.tensor_copy(rank[:, T], ps[:, 0, 0:n * NE].rearrange("p (t e) -> p t e", e=NE))
                dve.tensor_copy(count[:], ps[:, 1, 0:NE])
                dve.drain()
                dve.tensor_scalar(nov[:], count[:], float(P), None, ALU.is_gt)
                for m in range(2, NT):
                    dve.drain()
                    dve.scalar_tensor_tensor(nov[:], count[:], float(P * m), nov[:], ALU.is_gt, ALU.add)
                dve.drain()
                dve.sem_inc(nov_done, 1)
                dve.wait_ge(novT_ps, 1)
                dve.tensor_copy(novT[:], ps[0:NE, 2, 0:P]).then_inc(novT_done, 1)
                dve.wait_ge(ov_ps, 1)
                dve.tensor_scalar(shift[:], ps[:, 3, 0:NE], float(P), float((NE - 1) * P), ALU.mult, ALU.add)
                dve.tensor_tensor(end[:], ps[:, 3, 0:NE], nov[:], ALU.add)
                dve.drain()
                dve.wait_ge(c_in, 80)
                dve.tensor_tensor(shift[:], shift[:], e_row[:], ALU.subtract)
                dve.tensor_scalar(w[:, T], rank[:, T], float(P), None, ALU.is_ge)
                dve.tensor_tensor(place[:, T], rank[:, T], e_row[:].unsqueeze(1).broadcast_to([P, n, NE]), ALU.add)
                dve.drain()
                dve.tensor_tensor(w[:, T], w[:, T], shift[:].unsqueeze(1).broadcast_to([P, n, NE]), ALU.mult)
                dve.drain()
                dve.tensor_tensor(place[:, T], place[:, T], w[:, T], ALU.add)
                for j in range(2):
                    dve.drain()
                    dve.tensor_tensor(w[:, T], place[:, T], net.chosen[:, T, j, :], ALU.mult)
                    dve.drain()
                    dve.tensor_reduce(rowf[:, T, j], w[:, T], AX.X, ALU.add)
                dve.drain()
                dve.tensor_copy(net.row[:, T, :], rowf[:, T, :])
                e3 = end[0:1, :].unsqueeze(1).broadcast_to([1, OVER, NE])
                dve.tensor_tensor(cmp[:], e3, j_row[:].unsqueeze(2).broadcast_to([1, OVER, NE]), ALU.is_le)
                dve.drain()
                dve.tensor_reduce(blk[:, 0:OVER], cmp[:], AX.X, ALU.add)
                dve.tensor_copy(blk[:, OVER:OVER + 1], end[0:1, NE - 1:NE])
                dve.drain()
                dve.tensor_scalar(blk[:, 0:OVER], blk[:, 0:OVER], float(NE - 1), None, ALU.min)
                dve.drain()
                dve.tensor_copy(net.blocks[:], blk[:])
                dve.drain()
                dve.sem_inc(rows_done, 1)

            @block.tensor
            def _(pe):
                pe.wait_ge(c_in, 80)
                pe.wait_ge(pool_c, 3)
                pe.wait_ge(both_done, 1)
                for t in range(t0, NT):
                    o = ps[:, 0, (t - t0) * NE:(t - t0 + 1) * NE]
                    for u in range(t0, t):
                        pe.matmul(o, ones[:], both[:, u, :], start=(u == t0), stop=False)
                    mm = pe.matmul(o, before[:], both[:, t, :], start=(t == t0), stop=True)
                for t in range(t0, NT):
                    mm = pe.matmul(ps[:, 1, 0:NE], ones[:], both[:, t, :], start=(t == t0), stop=(t == NT - 1))
                mm.then_inc(rank_ps, 1)
                pe.wait_ge(nov_done, 1)
                pe.transpose(ps[0:NE, 2, 0:P], nov[:], ident[:]).then_inc(novT_ps, 1)
                pe.wait_ge(novT_done, 1)
                pe.matmul(ps[:, 3, 0:NE], novT[:], before_e[:], start=True, stop=True).then_inc(ov_ps, 1)


def expert_phase(nc, net, ps, layer):
    ins = net.ins
    HF = FF // P
    with phase(nc) as (sb, sem):
        ident = sb("ident", [P, P])
        w1 = [sb(f"w1{b}", [P, DT, FF]) for b in range(2)]
        w3 = [sb(f"w3{b}", [P, DT, FF]) for b in range(2)]
        w2 = [sb(f"w2{b}", [P, HF, D]) for b in range(2)]
        idx = [sb(f"idx{b}", [P, 1], I32) for b in range(2)]
        xg = [sb(f"xg{b}", [P, D]) for b in range(2)]
        xT = [sb(f"xT{b}", [P, DT, P]) for b in range(2)]
        sg = [sb(f"sg{b}", [P, FF]) for b in range(2)]
        h = [sb(f"h{b}", [P, FF]) for b in range(2)]
        hT = [sb(f"hT{b}", [P, HF, P]) for b in range(2)]
        yo = [sb(f"yo{b}", [P, D]) for b in range(2)]
        c_in, pool_step = sem("c_in"), sem("pool_step")
        w13_in = [sem(f"w13_in{b}") for b in range(2)]
        w2_in = [sem(f"w2_in{b}") for b in range(2)]
        idx_in = [sem(f"idx_in{b}") for b in range(2)]
        x_in = [sem(f"x_in{b}") for b in range(2)]
        stored = [sem(f"stored{b}") for b in range(2)]
        x_ps, xT_done, up, sig, h_done, h_ps, hT_done, down, y_done = (
            sem(n) for n in ("x_ps", "xT_done", "up", "sig", "h_done", "h_ps", "hT_done", "down", "y_done"))
        loops = [("first", NE // 2, 0), ("over", OVER // 2, NE)]
        UP = lambda b: 2 + 2 * b
        with nc.Block() as block:
            @block.sync
            def _(sp):
                sp.dma_start(ident[:], ins["k_ident"]).then_inc(c_in, 16)
                sp.sem_inc(up, 2)
                sp.sem_inc(down, 2)
                used = sp.value_load(net.blocks[0:1, OVER:OVER + 1], min_val=0, max_val=OVER)
                for kind, n, before in loops:
                    with sp.Fori(0, n) as i:
                        for b in range(2):
                            q = i * 2 + (b + before + 1)
                            if kind == "first":
                                e, cond = i * 2 + b, None
                            else:
                                e = sp.value_load(net.blocks[0:1, ds(i * 2 + b, 1)], min_val=0, max_val=NE - 1)
                                cond = (i * 2 + b) < used
                            sp.wait_ge(up, q)
                            for w, name in ((w1[b], "e_w1"), (w3[b], "e_w3")):
                                src = ins[name][layer].rearrange("e (p t) f -> e p (t f)", p=P)[ds(e, 1)]
                                sp.dma_start(w[:].rearrange("p t f -> p (t f)"), src.rearrange("o p n -> (o p) n"),
                                             cond=cond).then_inc(w13_in[b], 16)
                            sp.wait_ge(down, q)
                            src = ins["e_w2"][layer].rearrange("e (p t) f -> e p (t f)", p=P)[ds(e, 1)]
                            sp.dma_start(w2[b][:].rearrange("p t f -> p (t f)"), src.rearrange("o p n -> (o p) n"),
                                         cond=cond).then_inc(w2_in[b], 16)

            @block.gpsimd
            def _(pool):
                pool.sem_inc(x_ps, 2)
                for kind, n, before in loops:
                    with pool.Fori(0, n) as i:
                        for b in range(2):
                            q = i * 2 + (b + before + 1)
                            m = i + (1 + before // 2)
                            pool.wait_ge(x_ps, q)
                            pool.sem_inc(pool_step, 1)
                            pool.dma_start(idx[b][:], net.table[ds((i * 2 + (b + before)) * P, P), :]
                                           ).then_inc(idx_in[b], 16)
                            pool.wait_ge(idx_in[b], m * 16)
                            pool.sem_inc(pool_step, 1)
                            pool.indirect_dma_start(xg[b][:], None, net.f, bass.IndirectOffsetOnAxis(idx[b][:, 0:1], 0)
                                                    ).then_inc(x_in[b], 16)

            @block.scalar
            def _(act):
                for b in range(2):
                    act.sem_inc(stored[b], 16)
                for kind, n, before in loops:
                    with act.Fori(0, n) as i:
                        m = i + (1 + before // 2)
                        for b in range(2):
                            q = i * 2 + (b + before + 1)
                            act.wait_ge(x_ps, q + 2)
                            act.activation(xT[b][:, 4:8, :], ps[:, 1, :].rearrange("p (t n) -> p t n", n=P), ACT.Copy
                                           ).then_inc(xT_done, 1)
                            act.wait_ge(up, q + 2)
                            act.activation(sg[b][:], ps[:, UP(b), :], ACT.Sigmoid).then_inc(sig, 1)
                        for b in range(2):
                            q = i * 2 + (b + before + 1)
                            act.wait_ge(h_ps, q)
                            act.activation(hT[b][:], ps[:, 6 + b, :].rearrange("p (t n) -> p t n", n=P), ACT.Copy
                                           ).then_inc(hT_done, 1)
                            act.wait_ge(down, q + 2)
                            act.wait_ge(stored[b], m * 16)
                            act.activation(yo[b][:], ps[:, UP(b):UP(b) + 2, :], ACT.Copy).then_inc(y_done, 1)
                            act.wait_ge(y_done, q + 2)
                            act.dma_start(rows(net.ye, (i * 2 + (b + before)) * P), yo[b][:]).then_inc(stored[b], 16)
                for b in range(2):
                    act.wait_ge(stored[b], 16 * (NB // 2 + 1))

            @block.vector
            def _(dve):
                for kind, n, before in loops:
                    with dve.Fori(0, n) as i:
                        for b in range(2):
                            q = i * 2 + (b + before + 1)
                            dve.wait_ge(x_ps, q + 2)
                            dve.tensor_copy(xT[b][:, 0:4, :], ps[:, 0, :].rearrange("p (t n) -> p t n", n=P)
                                            ).then_inc(xT_done, 1)
                            dve.wait_ge(sig, q)
                            dve.tensor_tensor(sg[b][:], sg[b][:], ps[:, UP(b), :], ALU.mult)
                            dve.drain()
                            dve.tensor_tensor(h[b][:], sg[b][:], ps[:, UP(b) + 1, :], ALU.mult).then_inc(h_done, 1)

            @block.tensor
            def _(pe):
                pe.wait_ge(c_in, 16)
                pe.sem_inc(y_done, 2)
                for kind, n, before in loops:
                    with pe.Fori(0, n) as i:
                        m = i + (1 + before // 2)
                        for b in range(2):
                            q = i * 2 + (b + before + 1)
                            pe.wait_ge(x_in[b], m * 16)
                            if b == 1:
                                pe.wait_ge(xT_done, q * 2 - 2)
                            for t in range(DT):
                                tr = pe.transpose(ps[:, t // 4, (t % 4) * P:(t % 4 + 1) * P], xg[b][:, t:D:DT], ident[:])
                            tr.then_inc(x_ps, 1)
                            pe.wait_ge(xT_done, q * 2)
                            pe.wait_ge(w13_in[b], m * 32)
                            pe.wait_ge(y_done, q)
                            for j, w in enumerate((w1[b], w3[b])):
                                for t in range(DT):
                                    mm = pe.matmul(ps[:, UP(b) + j, :], xT[b][:, t, :], w[:, t, :],
                                                   start=(t == 0), stop=(t == DT - 1))
                            mm.then_inc(up, 1)
                        for b in range(2):
                            q = i * 2 + (b + before + 1)
                            pe.wait_ge(h_done, q)
                            for t in range(HF):
                                tr = pe.transpose(ps[:, 6 + b, t * P:(t + 1) * P], h[b][:, t:FF:HF], ident[:])
                            tr.then_inc(h_ps, 1)
                            pe.wait_ge(hT_done, q)
                            pe.wait_ge(w2_in[b], m * 16)
                            for c in range(2):
                                for t in range(HF):
                                    mm = pe.matmul(ps[:, UP(b) + c, :], hT[b][:, t, :], w2[b][:, t, c * 512:(c + 1) * 512],
                                                   start=(t == 0), stop=(t == HF - 1))
                            mm.then_inc(down, 1)


def combine_phase(nc, net, ps, layer):
    ins = net.ins
    last = layer == DEPTH - 1
    segs = [("lat", 0)] if last else [("ctx", 0), ("lat", CT)]
    n_all = LT if last else NT
    with phase(nc) as (sb, sem):
        GA = sb("GA", [P, 2, D])
        gain = sb("gain", [P, D])
        x, mix, o = sb("x", [P, D]), sb("mix", [P, D]), sb("o", [P, D])
        y = [sb(f"y{j}", [P, D]) for j in range(2)]
        idx = [sb(f"idx{j}", [P, 1], U32) for j in range(2)]
        gate = sb("gate", [P, 2])
        small = sb("small", [P, 4])
        c_in, x_in, used, idx_done, y_in, mean_done, root_done, o_done, stored, pool_step = (
            sem(n) for n in ("c_in", "x_in", "used", "idx_done", "y_in", "mean_done", "root_done", "o_done",
                             "stored", "pool_step"))
        with nc.Block() as block:
            @block.sync
            def _(sp):
                for j in range(2):
                    sp.dma_start(GA[:, j, :], net.mod[layer][j][5 * D:6 * D].partition_broadcast(P)).then_inc(c_in, 16)
                sp.dma_start(gain[:], ins["g_final"].partition_broadcast(P)).then_inc(c_in, 16)
                sp.sem_inc(used, 1)
                for seg, before in segs:
                    r0, n, _ = tokens_of(seg)
                    with sp.Fori(0, n) as i:
                        sp.wait_ge(used, i + (1 + before))
                        sp.dma_start(x[:], rows(net.x, i * P + r0)).then_inc(x_in, 16)

            @block.gpsimd
            def _(pool):
                for seg, before in segs:
                    r0, n, _ = tokens_of(seg)
                    with pool.Fori(0, n) as i:
                        k = i + (1 + before)
                        pool.wait_ge(idx_done, k)
                        pool.sem_inc(pool_step, 1)
                        for j in range(2):
                            pool.indirect_dma_start(y[j][:], None, net.ye, bass.IndirectOffsetOnAxis(idx[j][:, 0:1], 0)
                                                    ).then_inc(y_in, 16)

            @block.scalar
            def _(act):
                act.sem_inc(stored, 16)
                for seg, before in segs:
                    r0, n, _ = tokens_of(seg)
                    with act.Fori(0, n) as i:
                        k = i + (1 + before)
                        if last:
                            act.wait_ge(mean_done, k)
                            act.activation(small[:, 2:3], small[:, 1:2], ACT.Sqrt).then_inc(root_done, 1)
                        act.wait_ge(o_done, k)
                        dst = rows(net.out[0], i * P) if last else rows(net.x, i * P + r0)
                        act.dma_start(dst, o[:]).then_inc(stored, 16)
                act.wait_ge(stored, 16 * (n_all + 1))

            @block.vector
            def _(dve):
                dve.wait_ge(c_in, 48)
                for seg, before in segs:
                    r0, n, _ = tokens_of(seg)
                    j = 1 if seg == "ctx" else 0
                    with dve.Fori(0, n) as i:
                        k = i + (1 + before)
                        tile = i + r0 // P
                        for q in range(2):
                            dve.tensor_copy(idx[q][:].unsqueeze(1), net.row[:, ds(tile, 1), q:q + 1])
                        dve.tensor_copy(gate[:].unsqueeze(1), net.gate[:, ds(tile, 1), :])
                        dve.drain()
                        dve.sem_inc(idx_done, 1)
                        dve.wait_ge(y_in, k * 32)
                        dve.tensor_scalar(mix[:], y[0][:], gate[:, 0:1], None, ALU.mult)
                        dve.drain()
                        dve.scalar_tensor_tensor(mix[:], y[1][:], gate[:, 1:2], mix[:], ALU.mult, ALU.add)
                        dve.drain()
                        dve.tensor_tensor(mix[:], mix[:], GA[:, j, :], ALU.mult)
                        dve.drain()
                        dve.wait_ge(x_in, k * 16)
                        dve.wait_ge(stored, k * 16)
                        if not last:
                            dve.tensor_tensor(o[:], x[:], mix[:], ALU.add).then_inc(o_done, 1)
                            dve.drain()
                            dve.sem_inc(used, 1)
                            continue
                        dve.tensor_tensor(x[:], x[:], mix[:], ALU.add)
                        dve.drain()
                        dve.scalar_tensor_tensor(mix[:], x[:], 1.0, x[:], ALU.mult, ALU.mult, accum_out=small[:, 0:1])
                        dve.drain()
                        dve.tensor_scalar(small[:, 1:2], small[:, 0:1], 1.0 / D, EPS, ALU.mult, ALU.add
                                          ).then_inc(mean_done, 1)
                        dve.wait_ge(root_done, k)
                        dve.reciprocal(small[:, 3:4], small[:, 2:3])
                        dve.drain()
                        dve.scalar_tensor_tensor(o[:], x[:], small[:, 3:4], gain[:], ALU.mult, ALU.mult
                                                 ).then_inc(o_done, 1)
                        dve.drain()
                        dve.sem_inc(used, 1)


INPUTS = ["x", "c", "ctx", "c_ctx", "w_mod", "b_mod", "g_mix", "g_ffn", "w_in", "a_q_gain", "a_k_gain",
          "b_lq1", "b_lk1", "b_lq2", "b_lk2", "b_subln", "c_mu", "c_w0", "c_w2", "c_a0", "c_a2", "c_g2",
          "c_k_k", "c_k_a", "c_r_k", "c_ln_w", "c_ln_b", "w_out", "r_w_group", "r_b_group",
          "r_w_expert", "r_b_expert", "e_w1", "e_w3", "e_w2", "g_final"]


def constants():
    tri, mask, levels = scan_constants()
    i = np.arange(P)
    return {
        "k_ident": np.eye(P, dtype=np.float32),
        "k_rope": rope_tables(),
        "k_tri": tri, "k_mask": mask, "k_levels": levels,
        "k_before": (i[:, None] < i[None, :]).astype(np.float32),
        "k_rev": np.concatenate([NG - np.arange(NG), NE - np.arange(NE)]).astype(np.float32),
        "k_e_row": (P * np.arange(NE)).astype(np.float32),
        "k_j_row": np.arange(OVER).astype(np.float32),
        "k_before_e": (np.arange(NE)[:, None] < np.arange(NE)[None, :]).astype(np.float32),
    }




def build(nc, ins, out):
    net = Net(nc, ins, out)
    with (nc.psum_tensor("ps", [P, 8, 512], F32) as ps_t, nc.sbuf_tensor("chosen", [P, NT, 2, NE], F32) as chosen,
          nc.sbuf_tensor("gate", [P, NT, 2], F32) as gate, nc.sbuf_tensor("row", [P, NT, 2], U32) as row,
          nc.sbuf_tensor("blocks", [1, OVER + 1], I32) as blocks):
        ps = ps_t[:]
        net.chosen, net.gate, net.row, net.blocks = chosen, gate, row, blocks
        steps = [lambda: modulation_phase(nc, net, ps)]
        for layer in range(DEPTH):
            for f in LAYER_PHASES:
                steps.append(lambda f=f, layer=layer: f(nc, net, ps, layer))
        for s in steps:
            s()


LAYER_PHASES = [input_projection_phase, attention_phase, rwkv_input_phase, scan_phase,
                mix_output_phase, placement_phase, expert_phase, combine_phase]


def kernel(**inputs):
    import concourse.bacc as bacc
    from concourse.bass_utils import run_bass_kernel_spmd

    nc = bacc.Bacc("TRN2", target_bir_lowering=False, num_devices=1)
    arrays, ins = {}, {}
    for name, a in {**{n: inputs[n] for n in INPUTS}, **constants()}.items():
        a = np.ascontiguousarray(a)
        arrays[f"in_{name}"] = a
        ins[name] = nc.dram_tensor(f"in_{name}", a.shape, mybir.dt.from_np(a.dtype), kind="ExternalInput").ap()
    out = nc.dram_tensor("out_0", (1, SEQ, D), F32, kind="ExternalOutput").ap()
    build(nc, ins, out)
    return run_bass_kernel_spmd(nc, [arrays], core_ids=[0]).results[0]["out_0"]
```

```python
from contextlib import ExitStack, contextmanager

import numpy as np

import concourse.bass as bass
from concourse import mybir

F32 = mybir.dt.float32
I32 = mybir.dt.int32
U32 = mybir.dt.uint32
ALU = mybir.AluOpType
ACT = mybir.ActivationFunctionType
AX = mybir.AxisListType
ds = bass.ds

P = 128
D = 1024
DT = D // P
DEPTH = 2
SEQ = 1024
CTX = 256
TOK = SEQ + CTX
NT = TOK // P
CT = CTX // P
LT = SEQ // P
GRID_W = 64
EPS = 1e-6
HD = 64
A_Q, A_KV, B_Q, B_V = 256, 128, 256, 256
ATT = A_Q + 2 * A_KV + 2 * B_Q + B_V
CW = 512
CH = 8
LORA = 384
CS = 3 * CW + LORA
IN_W = ATT + CS
GN_EPS = 64e-5
NG, EPG, NE, FF = 4, 8, 32, 512
SLOTS = TOK * 2
OVER = 2 * ((SLOTS - 1) // P // 2 + 1)
NB = NE + OVER
C = 64
NC_CTX = CTX // C
NC_LAT = SEQ // C
NZ = 2
ST = NZ * CH

PAD_ROWS = TOK + 3
SEGMENTS = {"ctx": (0, CT, 1), "lat": (CTX, LT, CTX + 2)}


def tokens_of(seg):
    return SEGMENTS[seg]


@contextmanager
def phase(nc):
    sems = []
    with ExitStack() as ctx:
        def sb(name, shape, dt=F32):
            return ctx.enter_context(nc.sbuf_tensor(nc_name(name), shape, dt))

        def sem(name):
            s = nc.alloc_semaphore(nc_name(name))
            sems.append(s)
            return s

        yield sb, sem
        nc.clear_and_free_semaphores(sems)
        nc.all_engine_barrier()


_names = {}


def nc_name(name):
    _names[name] = _names.get(name, 0) + 1
    return f"{name}_{_names[name]}"


def rows(ap, start, n=P):
    return ap[ds(start, n), :]


def rope_tables():
    def table(dim):
        half = dim // 2
        inv = np.float32(10000.0) ** (-np.arange(0, half, 2, dtype=np.float32) / np.float32(half))
        t = np.arange(SEQ)
        ar = (t // GRID_W).astype(np.float32)[:, None] * inv.astype(np.float32)
        ac = (t % GRID_W).astype(np.float32)[:, None] * inv.astype(np.float32)
        ang = np.concatenate([ar, ar, ac, ac], -1).astype(np.float32)
        q = dim // 4
        sign = np.tile(np.concatenate([-np.ones(q), np.ones(q)]), 2).astype(np.float32)
        return np.cos(ang).astype(np.float32), (np.sin(ang) * sign).astype(np.float32)
    ca, sa = table(64)
    cb, sb = table(32)
    return np.concatenate([np.tile(ca, 6), np.tile(cb, 16), np.tile(sa, 6), np.tile(sb, 16)], -1)


ROPE_W = 6 * 64 + 16 * 32


def scan_constants():
    i = np.arange(C)
    before = [i[:, None] < i[None, :], i[:, None] > i[None, :]]
    eye = np.eye(C, dtype=bool)
    tri = np.zeros((C, NZ, 2 * P), np.float32)
    mask = np.zeros((P, NZ, P), np.float32)
    for z in range(NZ):
        incl = (before[z] | eye).astype(np.float32)
        excl = before[z].astype(np.float32)
        tri[:, z] = np.concatenate([incl, excl, -incl, -incl], 1)
        half = np.concatenate([incl, excl], 1)
        mask[:, z] = np.concatenate([half, half], 0)
    levels = []
    n = 1
    while n < C:
        up = (i[:, None] // (2 * n) == i[None, :] // (2 * n)) & (i[:, None] // n != i[None, :] // n)
        levels.append(np.stack([(up & before[z]).astype(np.float32) for z in range(NZ)], 1))
        n *= 2
    lv = np.stack(levels, 1).reshape(C, -1)
    return tri.reshape(C, -1), mask.reshape(P, -1), lv


LEVELS = 6


class Net:

    def __init__(self, nc, ins, out):
        self.ins = ins
        self.out = out
        self.x = nc.dram_tensor("s_x", [TOK, D], F32).ap()
        self.mod = nc.dram_tensor("s_mod", [DEPTH, 2, 6 * D], F32).ap()
        self.p = nc.dram_tensor("s_p", [PAD_ROWS, IN_W], F32).ap()
        self.y = nc.dram_tensor("s_y", [TOK, D], F32).ap()
        self.scan = nc.dram_tensor("s_scan", [TOK, 9 * CW], F32).ap()
        self.gb = nc.dram_tensor("s_gb", [TOK, 2 * CW], F32).ap()
        self.yd = nc.dram_tensor("s_yd", [NZ, TOK, CW], F32).ap()
        self.f = nc.dram_tensor("s_f", [TOK, D], F32).ap()
        self.table = nc.dram_tensor("s_table", [NB * P, 1], I32).ap()
        self.ye = nc.dram_tensor("s_ye", [NB * P, D], F32).ap()


def modulation_phase(nc, net, ps):
    NW = 512
    NCH = 6 * D // NW
    ins = net.ins
    with phase(nc) as (sb, sem):
        cond = sb("cond", [P, 2, DT])
        sig = sb("sig", [P, 2, DT])
        act = sb("act", [P, DT, 2])
        wt = [sb(f"wt{b}", [P, DT, NW]) for b in range(2)]
        bias = [sb(f"bias{b}", [2, NW]) for b in range(2)]
        res = [sb(f"res{b}", [2, NW]) for b in range(2)]
        zrow = sb("zrow", [1, CS])
        cond_in, sig_done, act_done = sem("cond_in"), sem("sig_done"), sem("act_done")
        w_in = [sem(f"w_in{b}") for b in range(2)]
        w_used, sums, added, stored, zeroed, side = (sem(n) for n in
                                                     ("w_used", "sums", "added", "stored", "zeroed", "side"))
        with nc.Block() as block:
            @block.sync
            def _(sp):
                sp.dma_start(cond[:, 0, :], ins["c"].rearrange("o (p t) -> p (o t)", t=DT)).then_inc(cond_in, 16)
                sp.dma_start(cond[:, 1, :], ins["c_ctx"].rearrange("(p t) -> p t", t=DT)).then_inc(cond_in, 16)
                sp.sem_inc(w_used, 2)
                for layer in range(DEPTH):
                    w = ins["w_mod"][layer].rearrange("(p t) n -> p t n", t=DT)
                    with sp.Fori(0, NCH // 2) as i:
                        for b in range(2):
                            n = (i * 2 + b)
                            sp.wait_ge(w_used, n + (1 + layer * NCH))
                            sp.dma_start(wt[b][:], w[:, :, ds(n * NW, NW)]).then_inc(w_in[b], 16)
                            src = ins["b_mod"][layer][ds(n * NW, NW)].partition_broadcast(2)
                            sp.dma_start(bias[b][:], src).then_inc(w_in[b], 16)

            @block.gpsimd
            def _(pool):
                pool.memset(zrow[:], 0.0).then_inc(zeroed, 1)

            @block.scalar
            def _(act_e):
                act_e.wait_ge(cond_in, 32)
                act_e.activation(sig[:], cond[:], ACT.Sigmoid).then_inc(sig_done, 1)
                act_e.dma_start(net.x[0:CTX, :], ins["ctx"][0]).then_inc(side, 16)
                act_e.dma_start(net.x[CTX:TOK, :], ins["x"][0]).then_inc(side, 16)
                act_e.wait_ge(zeroed, 1)
                for r in (0, CTX + 1, PAD_ROWS - 1):
                    act_e.dma_start(net.p[r:r + 1, ATT:IN_W], zrow[:]).then_inc(side, 16)
                act_e.wait_ge(side, 5 * 16)
                for layer in range(DEPTH):
                    with act_e.Fori(0, NCH // 2) as i:
                        for b in range(2):
                            n = (i * 2 + b)
                            act_e.wait_ge(added, n + (1 + layer * NCH))
                            act_e.dma_start(net.mod[layer][:, ds(n * NW, NW)], res[b][:]).then_inc(stored, 16)
                            act_e.wait_ge(stored, (n + (3 + layer * NCH)) * 16)

            @block.vector
            def _(dve):
                dve.wait_ge(sig_done, 1)
                dve.tensor_tensor(act[:].rearrange("p t j -> p j t"), cond[:], sig[:], ALU.mult).then_inc(act_done, 1)
                dve.sem_inc(stored, 32)
                for layer in range(DEPTH):
                    with dve.Fori(0, NCH // 2) as i:
                        for b in range(2):
                            n = (i * 2 + b)
                            dve.wait_ge(sums, n + (1 + layer * NCH))
                            dve.wait_ge(stored, (n + (1 + layer * NCH)) * 16)
                            dve.tensor_tensor(res[b][:], ps[0:2, b, :], bias[b][:], ALU.add).then_inc(added, 1)

            @block.tensor
            def _(pe):
                pe.wait_ge(act_done, 1)
                for layer in range(DEPTH):
                    with pe.Fori(0, NCH // 2) as i:
                        for b in range(2):
                            n = (i * 2 + b)
                            pe.wait_ge(w_in[b], (i + 1 + layer * NCH // 2) * 32)
                            if b == 0 and layer == 0:
                                pass
                            for t in range(DT):
                                mm = pe.matmul(ps[0:2, b, :], act[:, t, :], wt[b][:, t, :],
                                               start=(t == 0), stop=(t == DT - 1))
                            mm.then_inc(sums, 1)
                            pe.wait_ge(added, n + (1 + layer * NCH))
                            pe.sem_inc(w_used, 1)



NCK = [(n, min(512, IN_W - n)) for n in range(0, IN_W, 512)]
FIRST = {"ctx": 0, "lat": CT}


def input_projection_phase(nc, net, ps, layer):
    ins = net.ins
    with phase(nc) as (sb, sem):
        w = sb("w", [P, DT, IN_W])
        ident = sb("ident", [P, P])
        gain = sb("gain", [P, D])
        G = sb("G", [P, 2, D])
        S = sb("S", [P, 2, D])
        x = sb("x", [P, D])
        h = sb("h", [P, D])
        hT = sb("hT", [P, DT, P])
        small = sb("small", [P, 4])
        minus_half = sb("minus_half", [P, 1])
        po = sb("po", [P, IN_W])
        zero = sb("zero", [P, D])
        ye_clear = sem("ye_clear")
        const_set = sem("const_set")
        w_in, c_in, x_in, x_used = sem("w_in"), sem("c_in"), sem("x_in"), sem("x_used")
        mean_done, root_done, h_done = sem("mean_done"), sem("root_done"), sem("h_done")
        hT_ps, hT_done, prod, out_done, stored = (sem(n) for n in ("hT_ps", "hT_done", "prod", "out_done", "stored"))
        with nc.Block() as block:
            @block.sync
            def _(sp):
                sp.dma_start(ident[:], ins["k_ident"]).then_inc(c_in, 16)
                sp.dma_start(gain[:], ins["g_mix"][layer].partition_broadcast(P)).then_inc(c_in, 16)
                for j in range(2):
                    m = net.mod[layer][j]
                    sp.dma_start(S[:, j, :], m[0:D].partition_broadcast(P)).then_inc(c_in, 16)
                    sp.dma_start(G[:, j, :], m[D:2 * D].partition_broadcast(P)).then_inc(c_in, 16)
                sp.sem_inc(x_used, 1)
                for seg in ("ctx", "lat"):
                    r0, n, _ = tokens_of(seg)
                    with sp.Fori(0, n) as i:
                        sp.wait_ge(x_used, i + (1 + FIRST[seg]))
                        sp.dma_start(x[:], rows(net.x, i * P + r0)).then_inc(x_in, 16)

            @block.gpsimd
            def _(pool):
                pool.memset(minus_half[:], -0.5).then_inc(const_set, 1)
                pool.memset(zero[:], 0.0).then_inc(const_set, 1)
                pool.wait_ge(const_set, 2)
                if layer == 0:
                    pool.dma_start(net.ye[NE * P:].rearrange("(b p) n -> p b n", p=P),
                                   zero[:].unsqueeze(1).broadcast_to([P, OVER, D])).then_inc(ye_clear, 16)
                    pool.wait_ge(ye_clear, 16)
                for seg in ("ctx", "lat"):
                    with pool.Fori(0, tokens_of(seg)[1]) as i:
                        pool.wait_ge(mean_done, i + (1 + FIRST[seg]))
                        pool.tensor_tensor(small[:, 3:4], small[:, 1:2], minus_half[:], ALU.pow).then_inc(root_done, 1)

            @block.scalar
            def _(act):
                for t in range(DT):
                    act.dma_start(w[:, t, :], ins["w_in"][layer][t * P:(t + 1) * P, :]).then_inc(w_in, 16)
                act.sem_inc(out_done, 6)
                act.sem_inc(stored, 16)
                for seg in ("ctx", "lat"):
                    _, n, pr = tokens_of(seg)
                    with act.Fori(0, n) as i:
                        k = i + (1 + FIRST[seg])
                        act.wait_ge(hT_ps, k * 2 + 2)
                        act.wait_ge(prod, (k - 1) * len(NCK) + 1)
                        act.activation(hT[:, 4:8, :], ps[:, 1, :].rearrange("p (t n) -> p t n", n=P),
                                       ACT.Copy).then_inc(hT_done, 1)
                        act.wait_ge(stored, k * 16)
                        for c, (c0, cn) in enumerate(NCK):
                            act.wait_ge(prod, (k - 1) * len(NCK) + (c + 2))
                            act.activation(po[:, c0:c0 + cn], ps[:, 2 + c % 6, 0:cn], ACT.Copy).then_inc(out_done, 1)
                        act.wait_ge(out_done, k * len(NCK) + 6)
                        act.dma_start(rows(net.p, i * P + pr), po[:]).then_inc(stored, 16)
                act.wait_ge(stored, 16 * (NT + 1))

            @block.vector
            def _(dve):
                dve.wait_ge(c_in, 16 * 6)
                for j in range(2):
                    dve.scalar_tensor_tensor(G[:, j, :], G[:, j, :], 1.0, gain[:], ALU.add, ALU.mult)
                dve.sem_inc(hT_ps, 2)
                dve.drain()
                for seg in ("ctx", "lat"):
                    _, n, _ = tokens_of(seg)
                    j = 1 if seg == "ctx" else 0
                    with dve.Fori(0, n) as i:
                        k = i + (1 + FIRST[seg])
                        dve.wait_ge(x_in, k * 16)
                        dve.wait_ge(hT_ps, (k - 1) * 2 + 2)
                        dve.scalar_tensor_tensor(h[:], x[:], 1.0, x[:], ALU.mult, ALU.mult, accum_out=small[:, 0:1])
                        dve.drain()
                        dve.tensor_scalar(small[:, 1:2], small[:, 0:1], 1.0 / D, EPS, ALU.mult, ALU.add
                                          ).then_inc(mean_done, 1)
                        dve.wait_ge(root_done, k)
                        dve.scalar_tensor_tensor(h[:], x[:], small[:, 3:4], G[:, j, :], ALU.mult, ALU.mult
                                                 ).then_inc(x_used, 1)
                        dve.drain()
                        dve.tensor_tensor(h[:], h[:], S[:, j, :], ALU.add).then_inc(h_done, 1)
                        dve.wait_ge(hT_ps, k * 2 + 1)
                        dve.wait_ge(prod, (k - 1) * len(NCK) + 1)
                        dve.tensor_copy(hT[:, 0:4, :], ps[:, 0, :].rearrange("p (t n) -> p t n", n=P)
                                        ).then_inc(hT_done, 1)

            @block.tensor
            def _(pe):
                pe.sem_inc(prod, 1)
                pe.wait_ge(c_in, 16 * 6)
                for seg in ("ctx", "lat"):
                    _, n, _ = tokens_of(seg)
                    with pe.Fori(0, n) as i:
                        k = i + (1 + FIRST[seg])
                        pe.wait_ge(h_done, k)
                        for t in range(DT):
                            tr = pe.transpose(ps[:, t // 4, (t % 4) * P:(t % 4 + 1) * P],
                                              h[:, t * P:(t + 1) * P], ident[:])
                            if t % 4 == 3:
                                tr.then_inc(hT_ps, 1)
                        pe.wait_ge(hT_done, k * 2)
                        pe.wait_ge(w_in, 16 * DT)
                        for c, (c0, cn) in enumerate(NCK):
                            pe.wait_ge(out_done, (k - 1) * len(NCK) + (c + 1))
                            for t in range(DT):
                                mm = pe.matmul(ps[:, 2 + c % 6, 0:cn], hT[:, t, :], w[:, t, c0:c0 + cn],
                                               start=(t == 0), stop=(t == DT - 1))
                            mm.then_inc(prod, 1)



QK_W = A_Q + A_KV + 2 * B_Q
QB = QK_W // P
MAPS = 12
HEADS = 8
ORDER = [m for j in range(4) for m in (j, 4 + 2 * j, 5 + 2 * j)]
PLACE = [ORDER.index(m) for m in range(MAPS)]
HEAD_ORDER = [0, 4, 1, 5, 2, 6, 3, 7]
TURN = [HEAD_ORDER.index(h) for h in range(HEADS)]


def map_operands(m):
    return m, 2 if m < 4 else 5 + (m - 4) // 4


def attention_phase(nc, net, ps, layer):
    ins = net.ins
    lam_init = 0.8 - 0.6 * float(np.exp(-0.3 * layer))
    parts = [("ctx", CT)] * (layer < DEPTH - 1) + [("lat", NT)]
    tiles_before = {"ctx": 0, "lat": CT if layer < DEPTH - 1 else 0}
    n_tiles = tiles_before["lat"] + LT
    chunks_before = {"ctx": 0, "lat": tiles_before["lat"] * HEADS}
    with phase(nc) as (sb, sem):
        ident = sb("ident", [P, P])
        QKT = sb("QKT", [P, QB, TOK])
        V = sb("V", [P, NT, A_KV + B_V])
        gains = sb("gains", [P, 6, HD])
        sub_gain = sb("sub_gain", [P, 4, HD])
        lam_in = sb("lam_in", [P, 4, 32])
        lam_pr = sb("lam_pr", [P, 2, 32])
        lam_s = sb("lam_s", [P, 4])
        neg_lam = sb("neg_lam", [P, 1])
        qk = sb("qk", [P, QK_W])
        rope = sb("rope", [P, 2, ROPE_W])
        turned = sb("turned", [P, QK_W])
        qkr = sb("qkr", [P, QK_W])
        small = sb("small", [P, 4, 6])
        qs = sb("qs", [P, MAPS, P])
        p_a, p_b1 = sb("p_a", [P, TOK]), sb("p_b1", [P, TOK])
        p_b0 = [sb(f"p_b0_{n}", [P, TOK]) for n in range(2)]
        weights = lambda h: p_a if h < 4 else p_b0[h % 2]
        pT = [sb(f"pT{s}", [P, TOK]) for s in range(2)]
        mx = sb("mx", [P, MAPS])
        nm = sb("nm", [P, MAPS])
        sums = sb("sums", [P, MAPS])
        cs = sb("cs", [P, 3, 4])
        rs = sb("rs", [P, HEADS])
        yo = sb("yo", [P, HEADS * HD])
        ysq = sb("ysq", [P, 4 * HD])
        yst = sb("yst", [P, 4, 4])
        c_in, v_in, lam_ready, lam_exp = sem("c_in"), sem("v_in"), sem("lam_ready"), sem("lam_exp")
        qk_in, qk_used, mean_done, root_done, qkr_done, qkr_ps, qkt_done = (
            sem(n) for n in ("qk_in", "qk_used", "mean_done", "root_done", "qkr_done", "qkr_ps", "qkt_done"))
        qs_clear, pool_step = sem("qs_clear"), sem("pool_step")
        qs_done, scores, max_done, exp_done, comb_done = (
            sem(n) for n in ("qs_done", "scores", "max_done", "exp_done", "comb_done"))
        chunk_ps, pT_done, pv_done, o_used = sem("chunk_ps"), sem("pT_done"), sem("pv_done"), sem("o_used")
        y_mean, y_root, y_done, stored = sem("y_mean"), sem("y_root"), sem("y_done"), sem("stored")
        SCORE = [ps[:, 3 * s:3 * s + 3, :].rearrange("p b n -> p (b n)") for s in range(2)]

        def turn_chunks(kt):
            return [(t, min(4, kt - t)) for t in range(0, kt, 4)]
        O = ps[:, 7, :]
        with nc.Block() as block:
            @block.sync
            def _(sp):
                sp.dma_start(ident[:], ins["k_ident"]).then_inc(c_in, 16)
                for g, (src, n) in enumerate((("a_q_gain", 4), ("a_k_gain", 2))):
                    for h in range(n):
                        sp.dma_start(gains[:, 4 * g + h, :], ins[src][layer].partition_broadcast(P)
                                     ).then_inc(c_in, 16)
                for j, src in enumerate(("b_lq1", "b_lq2", "b_lk1", "b_lk2")):
                    sp.dma_start(lam_in[:, j, :], ins[src][layer].partition_broadcast(P)).then_inc(c_in, 16)
                for j in range(4):
                    sp.dma_start(sub_gain[:, j, :], ins["b_subln"][layer].partition_broadcast(P)
                                 ).then_inc(c_in, 16)
                sp.sem_inc(qk_used, 1)
                for seg in ("ctx", "lat"):
                    _, n, pr = tokens_of(seg)
                    with sp.Fori(0, n) as i:
                        sp.wait_ge(qk_used, i + (1 + FIRST[seg]))
                        src = rows(net.p, i * P + pr)
                        sp.dma_start(qk[:, 0:384], src[:, 0:384]).then_inc(qk_in, 16)
                        sp.dma_start(qk[:, 384:QK_W], src[:, 512:1024]).then_inc(qk_in, 16)
                        table = ins["k_rope"].rearrange("t (j w) -> t j w", j=2)
                        sp.dma_start(rope[:], table[ds(i * P, P), :, :]).then_inc(qk_in, 16)
                sp.sem_inc(stored, 16)
                for seg, _ in parts:
                    r0, n, _ = tokens_of(seg)
                    with sp.Fori(0, n) as i:
                        k = i + (1 + tiles_before[seg])
                        sp.wait_ge(y_done, k)
                        sp.dma_start(rows(net.y, i * P + r0)[:, 0:512], yo[:]).then_inc(stored, 16)
                sp.wait_ge(stored, (n_tiles + 1) * 16)

            @block.gpsimd
            def _(pool):
                for seg in ("ctx", "lat"):
                    _, n, pr = tokens_of(seg)
                    src = net.p[pr:pr + n * P, :].rearrange("(t p) n -> p t n", p=P)
                    t0 = FIRST[seg]
                    pool.dma_start(V[:, t0:t0 + n, 0:A_KV], src[:, :, 384:512]).then_inc(v_in, 16)
                    pool.dma_start(V[:, t0:t0 + n, A_KV:], src[:, :, 1024:1280]).then_inc(v_in, 16)
                pool.memset(qs[:], 0.0).then_inc(qs_clear, 1)
                pool.wait_ge(qs_clear, 1)
                pool.wait_ge(qkt_done, 2 * NT + 2)
                for seg, kt in parts:
                    r0, n, _ = tokens_of(seg)
                    with pool.Fori(0, n) as i:
                        k = i + (1 + tiles_before[seg])
                        pool.wait_ge(scores, (k - 1) * MAPS + 1)
                        pool.sem_inc(pool_step, 1)
                        for kv in range(2):
                            r = slice(64 * kv, 64 * kv + 64)
                            pool.tensor_copy(qs[r, 2 * kv:2 * kv + 2, :], QKT[r, 0:2, ds(i * P + r0, P)]
                                             ).then_inc(qs_done, 1)
                        pool.wait_ge(qs_done, (k - 1) * 6 + 2)
                        pool.sem_inc(pool_step, 1)
                        for n in range(4):
                            r = slice(32 * n, 32 * n + 32)
                            pool.tensor_copy(qs[r, 4 + n:MAPS:4, :], QKT[r, 3:5, ds(i * P + r0, P)]
                                             ).then_inc(qs_done, 1)

            @block.scalar
            def _(act):
                act.wait_ge(lam_ready, 1)
                act.activation(lam_s[:, 2:4], lam_s[:, 0:2], ACT.Exp).then_inc(lam_exp, 1)
                for seg in ("ctx", "lat"):
                    with act.Fori(0, tokens_of(seg)[1]) as i:
                        k = i + (1 + FIRST[seg])
                        act.wait_ge(mean_done, k)
                        act.activation(small[:, 2, :], small[:, 1, :], ACT.Sqrt).then_inc(root_done, 1)
                        act.wait_ge(qkr_ps, k * 2)
                        act.activation(QKT[:, 4:7, ds(i * P + FIRST[seg] * P, P)],
                                       ps[:, 1, 0:3 * P].rearrange("p (t n) -> p t n", n=P),
                                       ACT.Copy).then_inc(qkt_done, 1)

                act.sem_inc(pT_done, 1)
                for seg, kt in parts:
                    nk = kt * P
                    chunks = turn_chunks(kt)
                    per_tile, k0, base = HEADS * len(chunks), tiles_before[seg], chunks_before[seg]
                    with act.Fori(0, tokens_of(seg)[1]) as i:
                        k = i + (1 + tiles_before[seg])

                        def exp(m):
                            act.wait_ge(max_done, (k - 1) * MAPS + (PLACE[m] + 1))
                            if m < 4:
                                turned = TURN[m - 1] + 1 if m else 0
                                act.wait_ge(chunk_ps, base + (k - k0 - 1) * per_tile + (turned * len(chunks) + 1))
                                dst = p_a
                            elif m % 2 == 0:
                                turned = TURN[2 + m // 2 - 2] + 1 if m >= 8 else 0
                                act.wait_ge(chunk_ps, base + (k - k0 - 1) * per_tile + (turned * len(chunks) + 1))
                                dst = p_b0[(m // 2) % 2]
                            else:
                                act.wait_ge(comb_done, (k - 1) * 4 + ((m - 5) // 2 + 1))
                                dst = p_b1
                            scale = (HD if m < 4 else 32) ** -0.5
                            act.activation(dst[:, 0:nk], SCORE[PLACE[m] % 2][:, 0:nk], ACT.Exp, bias=nm[:, m:m + 1],
                                           scale=scale, accum_out=sums[:, m:m + 1]).then_inc(exp_done, 1)

                        def take(h):
                            act.wait_ge(pv_done, (k - 1) * HEADS + (TURN[h] + 1))
                            for c, (t, n) in enumerate(chunks):
                                at = TURN[h] * len(chunks) + c
                                act.wait_ge(chunk_ps, base + (k - k0 - 1) * per_tile + (at + 2))
                                act.activation(pT[h // 4][:, t * P:(t + n) * P], ps[:, 6, 0:n * P],
                                               ACT.Copy).then_inc(pT_done, 1)

                        for j in range(4):
                            if j == 0:
                                exp(0)
                            exp(4 + 2 * j)
                            if j > 0:
                                take(3 + j)
                            exp(5 + 2 * j)
                            take(j)
                            if j < 3:
                                exp(j + 1)
                        take(7)
                        act.wait_ge(y_mean, k)
                        act.activation(yst[:, 2, :], yst[:, 1, :], ACT.Sqrt).then_inc(y_root, 1)

            @block.vector
            def _(dve):
                dve.sem_inc(comb_done, 1)
                dve.wait_ge(c_in, 16 * 15)
                dve.tensor_tensor(lam_pr[:], lam_in[:, 0:2, :], lam_in[:, 2:4, :], ALU.mult)
                dve.drain()
                dve.tensor_reduce(lam_s[:, 0:2], lam_pr[:], AX.X, ALU.add).then_inc(lam_ready, 1)
                dve.tensor_scalar(sub_gain[:], sub_gain[:], 1.0 - lam_init, None, ALU.mult)
                dve.wait_ge(lam_exp, 1)
                dve.scalar_tensor_tensor(neg_lam[:], lam_s[:, 3:4], -lam_init, lam_s[:, 2:3],
                                         ALU.add, ALU.subtract)
                for seg in ("ctx", "lat"):
                    with dve.Fori(0, tokens_of(seg)[1]) as i:
                        k = i + (1 + FIRST[seg])
                        A, B = slice(0, 384), slice(384, QK_W)
                        dve.wait_ge(qk_in, k * 48)
                        dve.tensor_tensor(turned[:, A], qk[:, A], qk[:, A], ALU.mult)
                        dve.drain()
                        dve.tensor_reduce(small[:, 0, :], turned[:, A].rearrange("p (h d) -> p h d", d=HD),
                                          AX.X, ALU.add)
                        dve.drain()
                        dve.tensor_scalar(small[:, 1, :], small[:, 0, :], 1.0 / HD, EPS, ALU.mult, ALU.add
                                          ).then_inc(mean_done, 1)
                        dve.wait_ge(root_done, k)
                        dve.reciprocal(small[:, 3, :], small[:, 2, :])
                        dve.drain()
                        heads = qk[:, A].rearrange("p (h d) -> p h d", d=HD)
                        dve.tensor_tensor(heads, heads, small[:, 3, :].unsqueeze(2).broadcast_to([P, 6, HD]), ALU.mult)
                        dve.drain()
                        dve.tensor_tensor(heads, heads, gains[:], ALU.mult)
                        dve.drain()
                        if seg == "lat":
                            for cols, q in ((A, 16), (B, 8)):
                                x4 = qk[:, cols].rearrange("p (b j q) -> p b j q", j=2, q=q)
                                t4 = turned[:, cols].rearrange("p (b j q) -> p b j q", j=2, q=q)
                                s4 = rope[:, 1, cols].rearrange("p (b j q) -> p b j q", j=2, q=q)
                                for j in range(2):
                                    dve.tensor_tensor(t4[:, :, j, :], x4[:, :, 1 - j, :], s4[:, :, j, :], ALU.mult)
                            dve.drain()
                            dve.tensor_tensor(qk[:], qk[:], rope[:, 0, :], ALU.mult)
                            dve.drain()
                            dve.tensor_tensor(qk[:], qk[:], turned[:], ALU.add)
                            dve.drain()
                        dve.tensor_copy(qkr[:, 0:A_Q].rearrange("p (g k d) -> p k g d", g=2, k=2),
                                        qk[:, 0:A_Q].rearrange("p (k g d) -> p k g d", g=2, k=2)).then_inc(qkr_done, 1)
                        dve.tensor_copy(qkr[:, A_Q:], qk[:, A_Q:]).then_inc(qkr_done, 1)
                        dve.wait_ge(qkr_done, k * 2)
                        dve.sem_inc(qk_used, 1)
                        dve.wait_ge(qkr_ps, k * 2)
                        dve.tensor_copy(QKT[:, 0:4, ds(i * P + FIRST[seg] * P, P)],
                                        ps[:, 0, :].rearrange("p (t n) -> p t n", n=P)).then_inc(qkt_done, 1)

                dve.sem_inc(o_used, 1)
                for seg, kt in parts:
                    nk = kt * P
                    chunks = turn_chunks(kt)
                    per_tile, k0, base = HEADS * len(chunks), tiles_before[seg], chunks_before[seg]
                    with dve.Fori(0, tokens_of(seg)[1]) as i:
                        k = i + (1 + tiles_before[seg])

                        def find_max(m):
                            scale = (HD if m < 4 else 32) ** -0.5
                            dve.wait_ge(scores, (k - 1) * MAPS + (PLACE[m] + 1) + 1)
                            dve.tensor_reduce(mx[:, m:m + 1], SCORE[PLACE[m] % 2][:, 0:nk], AX.X, ALU.max)
                            dve.drain()
                            dve.tensor_scalar(nm[:, m:m + 1], mx[:, m:m + 1], -scale, None, ALU.mult
                                              ).then_inc(max_done, 1)

                        def combine(j):
                            m = 4 + 2 * j
                            dve.wait_ge(exp_done, (k - 1) * MAPS + (PLACE[m + 1] + 3))
                            dve.reciprocal(cs[:, 0, j:j + 1], sums[:, m + 1:m + 2])
                            dve.drain()
                            dve.scalar_tensor_tensor(cs[:, 2, j:j + 1], cs[:, 0, j:j + 1], sums[:, m:m + 1],
                                                     neg_lam[:], ALU.mult, ALU.mult)
                            dve.drain()
                            dve.scalar_tensor_tensor(p_b0[j % 2][:, 0:nk], p_b1[:, 0:nk], cs[:, 2, j:j + 1],
                                                     p_b0[j % 2][:, 0:nk], ALU.mult, ALU.add).then_inc(comb_done, 1)

                        for j in range(4):
                            find_max(j) if j == 0 else None
                            find_max(4 + 2 * j)
                            find_max(5 + 2 * j)
                            find_max(j + 1) if j < 3 else None
                            combine(j)
                        dve.reciprocal(rs[:, 0:4], sums[:, 0:4])
                        dve.reciprocal(rs[:, 4:8], sums[:, 4:12:2])
                        dve.drain()
                        dve.wait_ge(pv_done, k * HEADS + 2)
                        o3 = yo[:].rearrange("p (h d) -> p h d", d=HD)
                        dve.wait_ge(stored, k * 16)
                        dve.tensor_tensor(o3, O.rearrange("p (h d) -> p h d", d=HD),
                                          rs[:].unsqueeze(2).broadcast_to([P, HEADS, HD]), ALU.mult).then_inc(o_used, 1)
                        dve.drain()
                        yb = yo[:, 256:512]
                        dve.tensor_tensor(ysq[:], yb, yb, ALU.mult)
                        dve.drain()
                        dve.tensor_reduce(yst[:, 0, :], ysq[:].rearrange("p (h d) -> p h d", d=HD), AX.X, ALU.add)
                        dve.drain()
                        dve.tensor_scalar(yst[:, 1, :], yst[:, 0, :], 1.0 / HD, EPS, ALU.mult, ALU.add
                                          ).then_inc(y_mean, 1)
                        dve.wait_ge(y_root, k)
                        dve.reciprocal(yst[:, 3, :], yst[:, 2, :])
                        dve.drain()
                        dve.tensor_tensor(o3[:, 4:8, :], o3[:, 4:8, :],
                                          yst[:, 3, :].unsqueeze(2).broadcast_to([P, 4, HD]), ALU.mult)
                        dve.drain()
                        dve.tensor_tensor(o3[:, 4:8, :], o3[:, 4:8, :], sub_gain[:], ALU.mult).then_inc(y_done, 1)

            @block.tensor
            def _(pe):
                pe.wait_ge(c_in, 16 * 15)
                pe.sem_inc(qkt_done, 2)
                for seg in ("ctx", "lat"):
                    with pe.Fori(0, tokens_of(seg)[1]) as i:
                        k = i + (1 + FIRST[seg])
                        pe.wait_ge(qkr_done, k * 2)
                        pe.wait_ge(qkt_done, k * 2)
                        for t in range(QB):
                            tr = pe.transpose(ps[:, t // 4, (t % 4) * P:(t % 4 + 1) * P],
                                              qkr[:, t * P:(t + 1) * P], ident[:])
                            if t in (3, QB - 1):
                                tr.then_inc(qkr_ps, 1)

                pe.sem_inc(scores, 1)
                pe.sem_inc(chunk_ps, 1)
                pe.sem_inc(exp_done, 2)
                pe.sem_inc(pv_done, 2)
                pe.wait_ge(v_in, 64)
                pe.wait_ge(qkt_done, 2 * NT + 2)
                for seg, kt in parts:
                    nk = kt * P
                    chunks = turn_chunks(kt)
                    per_tile, k0, base = HEADS * len(chunks), tiles_before[seg], chunks_before[seg]
                    with pe.Fori(0, tokens_of(seg)[1]) as i:
                        k = i + (1 + tiles_before[seg])

                        def turn_chunk(h, c):
                            t0, n = chunks[c]
                            at = TURN[h] * len(chunks) + c
                            pe.wait_ge(pT_done, base + (k - k0 - 1) * per_tile + (at + 1))
                            for t in range(n):
                                tr = pe.transpose(ps[:, 6, t * P:(t + 1) * P],
                                                  weights(h)[:, (t0 + t) * P:(t0 + t + 1) * P], ident[:])
                            tr.then_inc(chunk_ps, 1)

                        def work(m=None, h=None):
                            if m is not None:
                                pe.wait_ge(exp_done, (k - 1) * MAPS + (PLACE[m] + 1))
                                q, kb = map_operands(m)
                            if h is not None and h < 4:
                                pe.wait_ge(exp_done, (k - 1) * MAPS + (PLACE[h] + 3))
                            elif h is not None:
                                pe.wait_ge(comb_done, (k - 1) * 4 + (h - 4 + 2))
                            for n, c in enumerate(range(0, nk, 512)):
                                if h is not None:
                                    turn_chunk(h, n)
                                if m is not None:
                                    w = min(512, nk - c)
                                    mm = pe.matmul(SCORE[PLACE[m] % 2][:, c:c + w], qs[:, q, :],
                                                   QKT[:, kb, c:c + w], start=True, stop=True)
                            if m is not None:
                                mm.then_inc(scores, 1)

                        def weigh(h):
                            pe.wait_ge(pT_done, base + (k - k0 - 1) * per_tile + ((TURN[h] + 1) * len(chunks) + 1))
                            v0 = HD * (h // 2) if h < 4 else A_KV + HD * (h - 4)
                            for t in range(kt):
                                mm = pe.matmul(O[:, h * HD:(h + 1) * HD], pT[h // 4][:, t * P:(t + 1) * P],
                                               V[:, t, v0:v0 + HD], start=(t == 0), stop=(t == kt - 1))
                            mm.then_inc(pv_done, 1)

                        pe.wait_ge(qs_done, k * 6)
                        work(m=0)
                        for j in range(4):
                            work(m=4 + 2 * j)
                            work(m=5 + 2 * j, h=3 + j if j > 0 else None)
                            if j > 0:
                                weigh(3 + j)
                            work(m=j + 1 if j < 3 else None, h=j)
                            if j == 0:
                                pe.wait_ge(o_used, k)
                            weigh(j)
                        work(h=7)
                        weigh(7)



SCAN_R, SCAN_V, SCAN_A, SCAN_B, SCAN_K, SCAN_L = 0, CW, 2 * CW, 3 * CW, 5 * CW, 7 * CW
DECAY = float(np.exp(np.float32(-0.5)))


def heads_of(ap, n=CH):
    return ap.rearrange("p (h d) -> p h d", d=HD)


def rwkv_input_phase(nc, net, ps, layer):
    ins = net.ins
    with phase(nc) as (sb, sem):
        ident = sb("ident", [P, P])
        mu = sb("mu", [P, CS])
        w2, a2 = sb("w2", [P, CW]), sb("a2", [P, CW])
        g2 = sb("g2", [P, CW])
        w0, a0 = sb("w0", [P, NZ, CW]), sb("a0", [P, NZ, CW])
        kk_g, ka_g, rk_g = sb("kk_g", [P, CW]), sb("ka_g", [P, CW]), sb("rk_g", [P, CW])
        cur, prev, nxt = sb("cur", [P, CS]), sb("prev", [P, CS]), sb("nxt", [P, CS])
        mix = sb("mix", [P, CS])
        pf = sb("pf", [P, CS])
        lt = sb("lt", [P, 3, P])
        pre = sb("pre", [P, 4, CW])
        kks, sq, kka, rr, kd_sum, rks = (sb(n, [P, CW]) for n in ("kks", "sq", "kka", "rr", "kd_sum", "rks"))
        a_out = sb("a_out", [P, CW])
        b_out, k_out, l_out = sb("b_out", [P, NZ, CW]), sb("k_out", [P, NZ, CW]), sb("l_out", [P, NZ, CW])
        gb = sb("gb", [P, 2, CW])
        st = sb("st", [P, 5, CH])
        c_in, t_in, t_used, pf_done, lt_ps, lt_done = (sem(n) for n in
                                                       ("c_in", "t_in", "t_used", "pf_done", "lt_ps", "lt_done"))
        proj, pre_done, sig_done, ss_done, root_done, outs_done, stored = (
            sem(n) for n in ("proj", "pre_done", "sig_done", "ss_done", "root_done", "outs_done", "stored"))
        pool_done, kd_done, g_done = sem("pool_done"), sem("kd_done"), sem("g_done")
        bc = lambda name: ins[name][layer].partition_broadcast(P)
        R, K, Vv = pf[:, 0:CW], pf[:, CW:2 * CW], pf[:, 2 * CW:3 * CW]
        with nc.Block() as block:
            @block.sync
            def _(sp):
                sp.dma_start(ident[:], ins["k_ident"]).then_inc(c_in, 16)
                sp.dma_start(mu[:], bc("c_mu")).then_inc(c_in, 16)
                sp.dma_start(w2[:], ins["c_w2"][layer].rearrange("z r c -> (z r) c")).then_inc(c_in, 16)
                sp.dma_start(a2[:], ins["c_a2"][layer].rearrange("z r c -> (z r) c")).then_inc(c_in, 16)
                sp.dma_start(g2[:], ins["c_g2"][layer]).then_inc(c_in, 16)
                sp.dma_start(w0[:], bc("c_w0")).then_inc(c_in, 16)
                sp.dma_start(a0[:], bc("c_a0")).then_inc(c_in, 16)
                sp.dma_start(kk_g[:], bc("c_k_k")).then_inc(c_in, 16)
                sp.dma_start(ka_g[:], bc("c_k_a")).then_inc(c_in, 16)
                rk = ins["c_r_k"][layer].rearrange("h d -> (h d)").partition_broadcast(P)
                sp.dma_start(rk_g[:], rk).then_inc(c_in, 16)
                sp.sem_inc(t_used, 1)
                for seg in ("ctx", "lat"):
                    _, n, pr = tokens_of(seg)
                    with sp.Fori(0, n) as i:
                        sp.wait_ge(t_used, i + (1 + FIRST[seg]))
                        for buf, off in ((cur, 0), (prev, -1), (nxt, 1)):
                            sp.dma_start(buf[:], rows(net.p, i * P + (pr + off))[:, ATT:IN_W]).then_inc(t_in, 16)

            @block.gpsimd
            def _(pool):
                pool.wait_ge(c_in, 160)
                for seg in ("ctx", "lat"):
                    with pool.Fori(0, tokens_of(seg)[1]) as i:
                        k = i + (1 + FIRST[seg])
                        pool.wait_ge(pf_done, k)
                        pool.tensor_tensor(kka[:], K, ka_g[:], ALU.mult).then_inc(pool_done, 1)
                        pool.tensor_tensor(rr[:], R, rk_g[:], ALU.mult).then_inc(pool_done, 1)
                        pool.wait_ge(kd_done, k)
                        pool.tensor_tensor(kd_sum[:], k_out[:, 0, :], k_out[:, 1, :], ALU.add).then_inc(pool_done, 1)
                        pool.wait_ge(pool_done, k * 4 - 1)
                        pool.tensor_tensor(rks[:], rr[:], kd_sum[:], ALU.mult).then_inc(pool_done, 1)

            @block.scalar
            def _(act):
                act.sem_inc(stored, 16 * 7)
                for seg in ("ctx", "lat"):
                    r0, n, _ = tokens_of(seg)
                    with act.Fori(0, n) as i:
                        k = i + (1 + FIRST[seg])
                        act.wait_ge(lt_ps, k)
                        act.activation(lt[:, 0, :], ps[:, 0, 0:P], ACT.Tanh).then_inc(lt_done, 1)
                        act.activation(lt[:, 1, :], ps[:, 0, P:2 * P], ACT.Copy).then_inc(lt_done, 1)
                        act.activation(lt[:, 2, :], ps[:, 0, 2 * P:3 * P], ACT.Sigmoid).then_inc(lt_done, 1)
                        act.wait_ge(pre_done, k)
                        act.activation(pre[:], pre[:], ACT.Sigmoid).then_inc(sig_done, 1)
                        act.wait_ge(stored, k * 16 * 7)
                        act.wait_ge(proj, k * 2)
                        act.activation(gb[:, 0, :], ps[:, 5, :], ACT.Copy).then_inc(g_done, 1)
                        act.wait_ge(ss_done, k)
                        act.activation(st[:, 1, :], st[:, 0, :], ACT.Sqrt).then_inc(root_done, 1)
                        act.wait_ge(outs_done, k)
                        act.wait_ge(g_done, k)
                        o = rows(net.scan, i * P + r0)
                        for buf, c0, w in ((R, SCAN_R, CW), (Vv, SCAN_V, CW), (a_out[:], SCAN_A, CW),
                                           (b_out[:].rearrange("p z c -> p (z c)"), SCAN_B, 2 * CW),
                                           (k_out[:].rearrange("p z c -> p (z c)"), SCAN_K, 2 * CW),
                                           (l_out[:].rearrange("p z c -> p (z c)"), SCAN_L, 2 * CW)):
                            act.dma_start(o[:, c0:c0 + w], buf).then_inc(stored, 16)
                        act.dma_start(rows(net.gb, i * P + r0), gb[:].rearrange("p j c -> p (j c)")
                                      ).then_inc(stored, 16)
                act.wait_ge(stored, 16 * 7 * (NT + 1))

            @block.vector
            def _(dve):
                dve.wait_ge(c_in, 160)
                for seg in ("ctx", "lat"):
                    with dve.Fori(0, tokens_of(seg)[1]) as i:
                        k = i + (1 + FIRST[seg])
                        dve.wait_ge(t_in, k * 48)
                        dve.tensor_tensor(mix[:], prev[:], nxt[:], ALU.add)
                        dve.drain()
                        dve.scalar_tensor_tensor(mix[:], mix[:], 0.5, cur[:], ALU.mult, ALU.subtract)
                        dve.drain()
                        dve.tensor_tensor(mix[:], mix[:], mu[:], ALU.mult)
                        dve.drain()
                        dve.wait_ge(stored, k * 16 * 7)
                        dve.tensor_tensor(pf[:], cur[:], mix[:], ALU.add).then_inc(pf_done, 1)
                        dve.drain()
                        dve.sem_inc(t_used, 1)
                        dve.tensor_tensor(kks[:], K, kk_g[:], ALU.mult)
                        dve.drain()
                        dve.tensor_tensor(sq[:], kks[:], kks[:], ALU.mult)
                        dve.drain()
                        dve.tensor_reduce(st[:, 0, :], heads_of(sq[:]), AX.X, ALU.add).then_inc(ss_done, 1)
                        dve.wait_ge(proj, k * 2 - 1)
                        dve.tensor_tensor(pre[:, 0:2, :], ps[:, 1:3, :], w0[:], ALU.add)
                        dve.tensor_tensor(pre[:, 2:4, :], ps[:, 3:5, :], a0[:], ALU.add)
                        dve.drain()
                        dve.sem_inc(pre_done, 1)
                        dve.wait_ge(root_done, k)
                        dve.tensor_scalar(st[:, 2, :], st[:, 1, :], 1e-12, None, ALU.max)
                        dve.drain()
                        dve.reciprocal(st[:, 3, :], st[:, 2, :])
                        dve.drain()
                        dve.tensor_scalar(st[:, 4, :], st[:, 3, :], -1.0, None, ALU.mult)
                        dve.drain()
                        dve.tensor_tensor(heads_of(a_out[:]), heads_of(kks[:]),
                                          st[:, 4, :].unsqueeze(2).broadcast_to([P, CH, HD]), ALU.mult)
                        dve.wait_ge(pool_done, k * 4 - 3)
                        dve.wait_ge(sig_done, k)
                        dve.tensor_scalar(l_out[:], pre[:, 0:2, :], -DECAY, None, ALU.mult)
                        for z in range(NZ):
                            dve.scalar_tensor_tensor(k_out[:, z, :], pre[:, 2 + z, :], 1.0, kka[:],
                                                     ALU.subtract, ALU.mult)
                        dve.drain()
                        for z in range(NZ):
                            dve.tensor_tensor(k_out[:, z, :], k_out[:, z, :], K, ALU.add)
                            dve.scalar_tensor_tensor(b_out[:, z, :], a_out[:], -1.0, pre[:, 2 + z, :],
                                                     ALU.mult, ALU.mult)
                        dve.drain()
                        dve.sem_inc(kd_done, 1)
                        dve.wait_ge(pool_done, k * 4)
                        dve.tensor_reduce(st[:, 0, :], heads_of(rks[:]), AX.X, ALU.add)
                        dve.drain()
                        dve.tensor_tensor(heads_of(gb[:, 1, :]), heads_of(Vv),
                                          st[:, 0, :].unsqueeze(2).broadcast_to([P, CH, HD]), ALU.mult
                                          ).then_inc(outs_done, 1)

            @block.tensor
            def _(pe):
                pe.wait_ge(c_in, 160)
                for seg in ("ctx", "lat"):
                    with pe.Fori(0, tokens_of(seg)[1]) as i:
                        k = i + (1 + FIRST[seg])
                        pe.wait_ge(pf_done, k)
                        for t in range(3):
                            tr = pe.transpose(ps[:, 0, t * P:(t + 1) * P],
                                              pf[:, 3 * CW + t * P:3 * CW + (t + 1) * P], ident[:])
                        tr.then_inc(lt_ps, 1)
                        pe.wait_ge(lt_done, k * 3)
                        for j, w in enumerate((w2, a2)):
                            for z in range(NZ):
                                q = slice(64 * z, 64 * z + 64)
                                mm = pe.matmul(ps[:, 1 + 2 * j + z, :], lt[q, j, :], w[q, :], start=True, stop=True)
                        mm.then_inc(proj, 1)
                        pe.matmul(ps[:, 5, :], lt[:, 2, :], g2[:], start=True, stop=True).then_inc(proj, 1)


def scan_phase(nc, net, ps, layer):
    ins = net.ins
    PAIR = 2
    GR = PAIR * NZ
    with phase(nc) as (sb, sem):
        ident = sb("ident", [P, P])
        tri = sb("tri", [C, NZ, 2 * P])
        mask = sb("mask", [P, NZ, P])
        levels = sb("levels", [P, LEVELS, NZ, C])
        ones = sb("ones", [C, 1])
        ra, kb = sb("ra", [P, PAIR, NZ, CW]), sb("kb", [P, PAIR, NZ, CW])
        v_raw = sb("v_raw", [C, PAIR, NZ, CW])
        lw = sb("lw", [C, PAIR, NZ, CW])
        rat, kbt = sb("rat", [P, PAIR, NZ, CW]), sb("kbt", [P, PAIR, NZ, CW])
        e_end = sb("e_end", [C, PAIR, ST])
        vu = sb("vu", [P, PAIR, ST, C])
        rac, kbc = sb("rac", [C, PAIR, ST, P]), sb("kbc", [C, PAIR, ST, P])
        G = sb("G", [P, PAIR, ST, P])
        at = sb("at", [P, 2, GR, CH, C])
        T, TT, YI = (sb(n, [P, GR, CH, C]) for n in ("T", "TT", "YI"))
        X = sb("X", [P, NZ, CH, C])
        state = sb("state", [C, 2, NZ, CH, C])
        yo = sb("yo", [C, PAIR, ST, C])
        hi = slice(C, P)
        pe_step, pool_step = sem("pe_step"), sem("pool_step")
        in_sem = [sem("in_sem%d" % j) for j in range(PAIR)]
        stored = [sem("stored%d" % j) for j in range(PAIR)]
        c_in, ones_set, in_used, cums, ends, exps, end_exp, v_done, scaled = (
            sem(n) for n in ("c_in", "ones_set", "in_used", "cums", "ends", "exps", "end_exp", "v_done", "scaled"))
        turned, rac_done, kbc_done, g_ps, g_done, at_done, tt0_done = (
            sem(n) for n in ("turned", "rac_done", "kbc_done", "g_ps", "g_done", "at_done", "tt0_done"))
        y_ps, yi_done, t_ps, t_done, tt_ps, tt_done = (
            sem(n) for n in ("y_ps", "yi_done", "t_ps", "t_done", "tt_ps", "tt_done"))
        x_ps, x_done, u_ps, u_done, out_ps, out_done, s_ps, s_done = (
            sem(n) for n in ("x_ps", "x_done", "u_ps", "u_done", "out_ps", "out_done", "s_ps", "s_done"))
        segs = [("ctx", NC_CTX, 0, 0), ("lat", NC_LAT, CTX, NC_CTX)]
        zs = lambda z: slice(CH * z, CH * z + CH)
        stc = lambda t, j, s: t[:, j, s // CH, (s % CH) * HD:(s % CH + 1) * HD]
        bank = lambda b, part: ps[part, b, :].rearrange("p (h c) -> p h c", c=C)
        eye8 = ident[hi, C:P].unsqueeze(1).broadcast_to([C, CH, C])
        row_of = lambda i, j, z, n, r0: (i * (PAIR * C) + (r0 + j * C) if z == 0
                                         else i * (-PAIR * C) + (r0 + (n - 1 - j) * C))
        with nc.Block() as block:
            @block.sync
            def _(sp):
                sp.dma_start(ident[:], ins["k_ident"]).then_inc(c_in, 16)
                sp.dma_start(tri[:].rearrange("p z n -> p (z n)"), ins["k_tri"]).then_inc(c_in, 16)
                sp.dma_start(mask[:].rearrange("p z n -> p (z n)"), ins["k_mask"]).then_inc(c_in, 16)
                sp.dma_start(levels[hi].rearrange("p l z n -> p (l z n)"), ins["k_levels"]).then_inc(c_in, 16)
                sp.sem_inc(in_used, PAIR)
                for seg, n, r0, before in segs:
                    with sp.Fori(0, n // PAIR) as i:
                        for j in range(PAIR):
                            sp.wait_ge(in_used, i * PAIR + (1 + j + before))
                            for z in range(NZ):
                                src = net.scan[ds(row_of(i, j, z, n, r0), C), :]
                                for dst, c0 in ((lw[:, j, z, :], SCAN_L + z * CW), (ra[0:C, j, z, :], SCAN_R),
                                                (ra[hi, j, z, :], SCAN_A), (kb[0:C, j, z, :], SCAN_K + z * CW),
                                                (kb[hi, j, z, :], SCAN_B + z * CW), (v_raw[:, j, z, :], SCAN_V)):
                                    sp.dma_start(dst, src[:, c0:c0 + CW]).then_inc(in_sem[j], 16)

            @block.gpsimd
            def _(pool):
                pool.memset(ones[:], 1.0).then_inc(ones_set, 1)
                pool.memset(state[:, 0], 0.0).then_inc(ones_set, 1)
                pool.wait_ge(c_in, 64)
                for seg, n, r0, before in segs:
                    with pool.Fori(0, n // PAIR) as i:
                        k = i + (1 + before // PAIR)
                        for j in range(PAIR):
                            pool.wait_ge(in_sem[j], k * 192)
                            pool.wait_ge(out_ps, (k - 1) * PAIR + (j + 1))
                            pool.sem_inc(pool_step, 1)
                            pool.tensor_copy(vu[0:C, j].rearrange("p (z h) d -> p z (h d)", z=NZ), v_raw[:, j]
                                             ).then_inc(v_done, 1)
                        for l in range(LEVELS):
                            for g in range(GR):
                                j, z = g // NZ, g % NZ
                                pool.wait_ge(g_done, (k - 1) * GR + (g + 1))
                                if l >= 2:
                                    pool.wait_ge(y_ps, (k - 1) * (LEVELS * GR) + ((l - 2) * GR + g + 1))
                                if l == 2:
                                    pool.wait_ge(tt0_done, (k - 1) * GR + (g + 1))
                                pool.tensor_tensor(at[hi, l % 2, g], G[hi, j, zs(z), C:P],
                                                   levels[hi, l, z, :].unsqueeze(1).broadcast_to([C, CH, C]),
                                                   ALU.mult).then_inc(at_done, 1)

            @block.scalar
            def _(act):
                for j in range(PAIR):
                    act.sem_inc(stored[j], 32)
                for seg, n, r0, before in segs:
                    with act.Fori(0, n // PAIR) as i:
                        k = i + (1 + before // PAIR)
                        for j in range(PAIR):
                            act.wait_ge(cums, (k - 1) * PAIR + (j + 1))
                            act.activation(rat[:, j], ps[:, GR * j:GR * j + 2, :], ACT.Exp).then_inc(exps, 1)
                            act.activation(kbt[:, j], ps[:, GR * j + 2:GR * j + 4, :], ACT.Exp).then_inc(exps, 1)
                            if j == 0:
                                act.wait_ge(ends, k * PAIR)
                                act.wait_ge(s_done, (k - 1) * 4 + 2)
                                act.activation(e_end[:].rearrange("p j s -> p (j s)"), ps[0:C, 7, 0:PAIR * ST],
                                               ACT.Exp).then_inc(end_exp, 1)
                        for j in range(PAIR):
                            act.wait_ge(turned, (k - 1) * 4 + (2 * j + 1))
                            act.activation(rac[:, j].rearrange("p s c -> p (s c)"),
                                           ps[0:C, 0:4, :].rearrange("p b n -> p (b n)"), ACT.Copy
                                           ).then_inc(rac_done, 1)
                        for l in range(1, LEVELS):
                            for g in range(GR if l < LEVELS - 1 else 0):
                                act.wait_ge(t_ps, (k - 1) * ((LEVELS - 2) * GR) + ((l - 1) * GR + g + 1))
                                act.activation(T[hi, g], bank(g, hi), ACT.Copy).then_inc(t_done, 1)
                            for g in range(GR):
                                act.wait_ge(tt_ps, (k - 1) * ((LEVELS - 1) * GR) + ((l - 1) * GR + g + 1))
                                act.activation(TT[hi, g], bank(4 + g, hi), ACT.Copy).then_inc(tt_done, 1)
                        for j in range(PAIR):
                            for z in range(NZ):
                                act.wait_ge(x_ps, (k - 1) * 4 + (2 * j + z + 1))
                                act.activation(X[hi, z], bank(z, hi), ACT.Copy).then_inc(x_done, 1)
                            for z in range(NZ):
                                act.wait_ge(u_ps, (k - 1) * 4 + (2 * j + z + 1))
                                act.activation(vu[hi, j, zs(z), :], bank(2 + z, hi), ACT.Copy).then_inc(u_done, 1)
                            act.wait_ge(out_ps, k * PAIR + (j + 1))
                            act.wait_ge(stored[j], k * 32)
                            act.activation(yo[:, j].rearrange("p (z h) c -> p z (h c)", z=NZ), ps[0:C, 6:8, :],
                                           ACT.Copy).then_inc(out_done, 1)
                            act.wait_ge(out_done, (k - 1) * PAIR + (j + 2))
                            for z in range(NZ):
                                act.dma_start(net.yd[z][ds(row_of(i, j, z, n, r0), C), :],
                                              yo[:, j, zs(z), :].rearrange("p h c -> p (h c)")
                                              ).then_inc(stored[j], 16)
                for j in range(PAIR):
                    act.wait_ge(stored[j], 32 * ((NC_LAT + NC_CTX) // PAIR + 1))

            @block.vector
            def _(dve):
                dve.wait_ge(c_in, 64)
                dve.wait_ge(ones_set, 2)
                dve.sem_inc(s_done, 2)
                for seg, n, r0, before in segs:
                    with dve.Fori(0, n // PAIR) as i:
                        k = i + (1 + before // PAIR)
                        for j in range(PAIR):
                            dve.wait_ge(in_sem[j], k * 192)
                            dve.wait_ge(exps, (k - 1) * 4 + (2 * j + 1))
                            dve.tensor_tensor(rat[:, j], ra[:, j], rat[:, j], ALU.mult).then_inc(scaled, 1)
                            dve.wait_ge(exps, (k - 1) * 4 + (2 * j + 2))
                            dve.tensor_tensor(kbt[:, j], kb[:, j], kbt[:, j], ALU.mult).then_inc(scaled, 1)
                            dve.wait_ge(v_done, (k - 1) * PAIR + (j + 1))
                            dve.wait_ge(scaled, (k - 1) * 4 + (2 * j + 2))
                            dve.sem_inc(in_used, 1)
                        for j in range(PAIR):
                            dve.wait_ge(turned, (k - 1) * 4 + (2 * j + 2))
                            dve.tensor_copy(kbc[:, j].rearrange("p s c -> p (s c)"),
                                            ps[0:C, 4:8, :].rearrange("p b n -> p (b n)")).then_inc(kbc_done, 1)
                        for g in range(GR):
                            j, z = g // NZ, g % NZ
                            dve.wait_ge(g_ps, (k - 1) * GR + (g + 1))
                            dve.tensor_tensor(G[:, j, zs(z), :],
                                              ps[:, 2 * g:2 * g + 2, :].rearrange("p b (s n) -> p (b s) n", n=P),
                                              mask[:, z, :].unsqueeze(1).broadcast_to([P, CH, P]), ALU.mult
                                              ).then_inc(g_done, 1)
                        for g in range(GR):
                            dve.wait_ge(at_done, (k - 1) * (LEVELS * GR) + (g + 1))
                            dve.tensor_tensor(TT[hi, g], at[hi, 0, g], eye8, ALU.add).then_inc(tt0_done, 1)
                        for l in range(LEVELS):
                            dst = T if l == 0 else YI
                            for g in range(GR):
                                dve.wait_ge(y_ps, (k - 1) * (LEVELS * GR) + (l * GR + g + 1))
                                dve.tensor_tensor(dst[hi, g], bank(g, hi), eye8, ALU.add).then_inc(yi_done, 1)
                        for j in range(PAIR):
                            for z in range(NZ):
                                dve.wait_ge(s_ps, (k - 1) * 4 + (2 * j + z + 1))
                                dve.tensor_tensor(state[:, 1 - j, z], state[:, j, z], bank(4 + z, slice(0, C)), ALU.add)
                                dve.drain()
                                dve.tensor_tensor(state[:, 1 - j, z], state[:, 1 - j, z],
                                                  e_end[:, j, zs(z)].unsqueeze(2).broadcast_to([C, CH, C]), ALU.mult
                                                  ).then_inc(s_done, 1)

            @block.tensor
            def _(pe):
                pe.wait_ge(c_in, 64)
                pe.sem_inc(out_done, 1)
                pe.sem_inc(out_ps, PAIR)
                for seg, n, r0, before in segs:
                    with pe.Fori(0, n // PAIR) as i:
                        k = i + (1 + before // PAIR)
                        pe.wait_ge(s_done, (k - 1) * 4 + 2)
                        for j in range(PAIR):
                            pe.wait_ge(in_sem[j], k * 192)
                            pe.wait_ge(out_done, (k - 1) * PAIR + 1)
                            pe.sem_inc(pe_step, 1)
                            for s in range(ST):
                                mm = pe.matmul(ps[0:C, 7, ST * j + s:ST * j + s + 1], stc(lw, j, s), ones[:],
                                               start=True, stop=True)
                            mm.then_inc(ends, 1)
                            for b in range(4):
                                if j == 1 and b == 3:
                                    pe.wait_ge(end_exp, k)
                                half = b // 2
                                mm = pe.matmul(ps[:, GR * j + b, :], tri[:, b % 2, half * P:half * P + P],
                                               lw[:, j, b % 2, :], start=True, stop=True)
                            mm.then_inc(cums, 1)
                        for j in range(PAIR):
                            for half, src in enumerate((rat, kbt)):
                                if j == 0:
                                    pe.wait_ge(exps, (k - 1) * 4 + (2 + 2 * half))
                                elif half == 0:
                                    pe.wait_ge(rac_done, (k - 1) * PAIR + j)
                                else:
                                    pe.wait_ge(kbc_done, (k - 1) * PAIR + j)
                                pe.wait_ge(scaled, (k - 1) * 4 + (2 * j + half + 1))
                                pe.sem_inc(pe_step, 1)
                                for s in range(ST):
                                    tr = pe.transpose(ps[0:C, 4 * half + s // 4, (s % 4) * P:(s % 4 + 1) * P],
                                                      stc(src, j, s), ident[:])
                                tr.then_inc(turned, 1)
                        for j in range(PAIR):
                            pe.wait_ge(rac_done, k * PAIR)
                            pe.wait_ge(kbc_done, (k - 1) * PAIR + (j + 1))
                            for s in range(ST):
                                mm = pe.matmul(ps[:, GR * j + s // 4, (s % 4) * P:(s % 4 + 1) * P], kbc[:, j, s, :],
                                               rac[:, j, s, :], start=True, stop=True)
                                if s % CH == CH - 1:
                                    mm.then_inc(g_ps, 1)
                        for l in range(LEVELS):
                            for g in range(GR):
                                pe.wait_ge(at_done, (k - 1) * (LEVELS * GR) + (l * GR + g + 1))
                                if l == 0:
                                    pe.wait_ge(g_done, (k - 1) * GR + (g // 2 + 1))
                                elif l == 1:
                                    pe.wait_ge(yi_done, (k - 1) * (LEVELS * GR) + (g + 1))
                                else:
                                    pe.wait_ge(t_done, (k - 1) * ((LEVELS - 2) * GR) + ((l - 2) * GR + g + 1))
                                pe.sem_inc(pe_step, 1)
                                for h in range(CH):
                                    rhs = ident[hi, C:P] if l == 0 else T[hi, g, h, :]
                                    mm = pe.matmul(bank(g, hi)[:, h, :], at[hi, l % 2, g, h, :], rhs,
                                                   start=True, stop=True)
                                mm.then_inc(y_ps, 1)
                            if l == 0:
                                continue
                            for out_t in ((True, False) if l < LEVELS - 1 else (False,)):
                                for g in range(GR):
                                    pe.wait_ge(yi_done, (k - 1) * (LEVELS * GR) + (l * GR + g + 1))
                                    if l == 1:
                                        pe.wait_ge(tt0_done, (k - 1) * GR + (g + 1))
                                    else:
                                        pe.wait_ge(tt_done, (k - 1) * ((LEVELS - 1) * GR) + ((l - 2) * GR + g + 1))
                                    pe.sem_inc(pe_step, 1)
                                    for h in range(CH):
                                        if out_t:
                                            mm = pe.matmul(bank(g, hi)[:, h, :], TT[hi, g, h, :], YI[hi, g, h, :],
                                                           start=True, stop=True)
                                        else:
                                            mm = pe.matmul(bank(4 + g, hi)[:, h, :], YI[hi, g, h, :], TT[hi, g, h, :],
                                                           start=True, stop=True)
                                    mm.then_inc(t_ps if out_t else tt_ps, 1)
                        for j in range(PAIR):
                            pe.wait_ge(v_done, (k - 1) * PAIR + (j + 1))
                            for z in range(NZ):
                                pe.wait_ge(yi_done, k * (LEVELS * GR))
                                pe.wait_ge(s_done, (k - 1) * 4 + (2 * j + z + 1))
                                pe.sem_inc(pe_step, 1)
                                for h in range(CH):
                                    s = CH * z + h
                                    pe.matmul(bank(z, hi)[:, h, :], rac[:, j, s, C:P], state[:, j, z, h, :],
                                              start=True, stop=False)
                                    mm = pe.matmul(bank(z, hi)[:, h, :], G[0:C, j, s, C:P], vu[0:C, j, s, :],
                                                   start=False, stop=True)
                                mm.then_inc(x_ps, 1)
                            for z in range(NZ):
                                pe.wait_ge(x_done, (k - 1) * 4 + (2 * j + z + 1))
                                pe.wait_ge(tt_done, (k - 1) * ((LEVELS - 1) * GR) + ((LEVELS - 2) * GR + NZ * j + z + 1))
                                pe.sem_inc(pe_step, 1)
                                for h in range(CH):
                                    mm = pe.matmul(bank(2 + z, hi)[:, h, :], TT[hi, NZ * j + z, h, :], X[hi, z, h, :],
                                                   start=True, stop=True)
                                mm.then_inc(u_ps, 1)
                            for z in range(NZ):
                                pe.wait_ge(u_done, (k - 1) * 4 + (2 * j + z + 1))
                                pe.wait_ge(tt_done, k * ((LEVELS - 1) * GR))
                                pe.sem_inc(pe_step, 1)
                                for h in range(CH):
                                    s = CH * z + h
                                    mm = pe.matmul(bank(4 + z, slice(0, C))[:, h, :], stc(kbt, j, s), vu[:, j, s, :],
                                                   start=True, stop=True)
                                mm.then_inc(s_ps, 1)
                            pe.wait_ge(out_done, (k - 1) * PAIR + (j + 1))
                            pe.sem_inc(pe_step, 1)
                            for s in range(ST):
                                y = bank(6 + s // CH, slice(0, C))[:, s % CH, :]
                                pe.matmul(y, rac[:, j, s, 0:C], state[:, j, s // CH, s % CH, :], start=True, stop=False)
                                mm = pe.matmul(y, G[:, j, s, 0:C], vu[:, j, s, :], start=False, stop=True)
                            mm.then_inc(out_ps, 1)


def mix_output_phase(nc, net, ps, layer):
    ins = net.ins
    last = layer == DEPTH - 1
    segs = [("lat", 0)] if last else [("ctx", 0), ("lat", CT)]
    n_all = LT if last else NT
    RW = NG + NE
    BIG = 1e30
    with phase(nc) as (sb, sem):
        ident = sb("ident", [P, P])
        w = sb("w", [P, DT, D])
        wr = sb("wr", [P, DT, RW])
        br = sb("br", [P, RW])
        rev = sb("rev", [P, RW])
        lnw, lnb = sb("lnw", [P, CW]), sb("lnb", [P, CW])
        gain = sb("gain", [P, D])
        GA, G, S = sb("GA", [P, 2, D]), sb("G", [P, 2, D]), sb("S", [P, 2, D])
        y = sb("y", [P, D])
        y2 = sb("y2", [P, CW])
        gb = sb("gb", [P, 2, CW])
        ysq = sb("ysq", [P, CW])
        st = sb("st", [P, 6, CH])
        yT, fT = sb("yT", [P, DT, P]), sb("fT", [P, DT, P])
        x, f, fs = sb("x", [P, D]), sb("f", [P, D]), sb("fs", [P, D])
        small = sb("small", [P, 4])
        lg = sb("lg", [P, RW])
        sel = sb("sel", [P, 4, RW])
        r1 = sb("r1", [P, 16])
        ex = sb("ex", [P, 2, NG + 1])
        c_in, c_ready, y_in, y_used, x_in, x_used, x_stored = (
            sem(n) for n in ("c_in", "c_ready", "y_in", "y_used", "x_in", "x_used", "x_stored"))
        var_done, root_done, y_done, y_ps, yT_done, prod = (
            sem(n) for n in ("var_done", "root_done", "y_done", "y_ps", "yT_done", "prod"))
        x_done, f_var, f_root, f_done, f_ps, fT_done, lg_ps, f_stored = (
            sem(n) for n in ("x_done", "f_var", "f_root", "f_done", "f_ps", "fT_done", "lg_ps", "f_stored"))
        diff_done, exp_done = sem("diff_done"), sem("exp_done")
        NCON = 16
        with nc.Block() as block:
            @block.sync
            def _(sp):
                bc = lambda ap: ap.partition_broadcast(P)
                sp.dma_start(ident[:], ins["k_ident"]).then_inc(c_in, 16)
                sp.dma_start(w[:], ins["w_out"][layer].rearrange("(t p) n -> p t n", p=P)).then_inc(c_in, 16)
                sp.dma_start(wr[:, :, 0:NG], ins["r_w_group"][layer].rearrange("(t p) n -> p t n", p=P)
                             ).then_inc(c_in, 16)
                sp.dma_start(wr[:, :, NG:], ins["r_w_expert"][layer].rearrange("(t p) n -> p t n", p=P)
                             ).then_inc(c_in, 16)
                sp.dma_start(br[:, 0:NG], bc(ins["r_b_group"][layer])).then_inc(c_in, 16)
                sp.dma_start(br[:, NG:], bc(ins["r_b_expert"][layer])).then_inc(c_in, 16)
                sp.dma_start(rev[:], bc(ins["k_rev"])).then_inc(c_in, 16)
                sp.dma_start(lnw[:], bc(ins["c_ln_w"][layer])).then_inc(c_in, 16)
                sp.dma_start(lnb[:], bc(ins["c_ln_b"][layer])).then_inc(c_in, 16)
                sp.dma_start(gain[:], bc(ins["g_ffn"][layer])).then_inc(c_in, 16)
                for j in range(2):
                    m = net.mod[layer][j]
                    sp.dma_start(GA[:, j, :], bc(m[2 * D:3 * D])).then_inc(c_in, 16)
                    sp.dma_start(S[:, j, :], bc(m[3 * D:4 * D])).then_inc(c_in, 16)
                    sp.dma_start(G[:, j, :], bc(m[4 * D:5 * D])).then_inc(c_in, 16)
                sp.sem_inc(y_used, 1)
                sp.sem_inc(x_stored, 16)
                for seg, before in segs:
                    r0, n, _ = tokens_of(seg)
                    with sp.Fori(0, n) as i:
                        k = i + (1 + before)
                        r = i * P + r0
                        sp.wait_ge(y_used, k)
                        sp.dma_start(y[:, 0:CW], rows(net.y, r)[:, 0:CW]).then_inc(y_in, 16)
                        sp.dma_start(y[:, CW:D], rows(net.yd[0], r)).then_inc(y_in, 16)
                        sp.dma_start(y2[:], rows(net.yd[1], r)).then_inc(y_in, 16)
                        sp.dma_start(gb[:].rearrange("p j c -> p (j c)"), rows(net.gb, r)).then_inc(y_in, 16)
                        sp.wait_ge(x_stored, k * 16)
                        sp.wait_ge(x_used, k)
                        sp.dma_start(x[:], rows(net.x, r)).then_inc(x_in, 16)

            @block.scalar
            def _(act):
                act.sem_inc(f_stored, 16)
                for seg, before in segs:
                    r0, n, _ = tokens_of(seg)
                    with act.Fori(0, n) as i:
                        k = i + (1 + before)
                        act.wait_ge(var_done, k)
                        act.activation(st[:, 3, :], st[:, 2, :], ACT.Sqrt).then_inc(root_done, 1)
                        act.wait_ge(y_ps, k * 2)
                        act.activation(yT[:, 4:8, :], ps[:, 1, :].rearrange("p (t n) -> p t n", n=P),
                                       ACT.Copy).then_inc(yT_done, 1)
                        act.wait_ge(x_done, k)
                        act.dma_start(rows(net.x, i * P + r0), x[:]).then_inc(x_stored, 16)
                        act.wait_ge(f_var, k)
                        act.activation(small[:, 2:3], small[:, 1:2], ACT.Sqrt).then_inc(f_root, 1)
                        act.wait_ge(f_ps, k * 2)
                        act.activation(fT[:, 4:8, :], ps[:, 5, :].rearrange("p (t n) -> p t n", n=P),
                                       ACT.Copy).then_inc(fT_done, 1)
                        act.dma_start(rows(net.f, i * P + r0), f[:]).then_inc(f_stored, 16)
                        act.wait_ge(diff_done, k)
                        act.activation(ex[:, 1, :], ex[:, 0, :], ACT.Exp).then_inc(exp_done, 1)
                act.wait_ge(f_stored, 16 * (n_all + 1))
                act.wait_ge(x_stored, 16 * (n_all + 1))

            @block.vector
            def _(dve):
                dve.wait_ge(c_in, 16 * NCON)
                for j in range(2):
                    dve.scalar_tensor_tensor(G[:, j, :], G[:, j, :], 1.0, gain[:], ALU.add, ALU.mult)
                dve.sem_inc(x_used, 1)
                for seg, before in segs:
                    r0, n, _ = tokens_of(seg)
                    j = 1 if seg == "ctx" else 0
                    with dve.Fori(0, n) as i:
                        k = i + (1 + before)
                        tile = i + r0 // P
                        yc = y[:, CW:D]
                        b8 = lambda q: st[:, q, :].unsqueeze(2).broadcast_to([P, CH, HD])
                        dve.wait_ge(y_in, k * 64)
                        dve.tensor_tensor(yc, yc, y2[:], ALU.add)
                        dve.drain()
                        dve.tensor_reduce(st[:, 0, :], heads_of(yc), AX.X, ALU.add)
                        dve.drain()
                        dve.tensor_scalar(st[:, 1, :], st[:, 0, :], -1.0 / HD, None, ALU.mult)
                        dve.drain()
                        dve.tensor_tensor(heads_of(yc), heads_of(yc), b8(1), ALU.add)
                        dve.drain()
                        dve.tensor_tensor(ysq[:], yc, yc, ALU.mult)
                        dve.drain()
                        dve.tensor_reduce(st[:, 0, :], heads_of(ysq[:]), AX.X, ALU.add)
                        dve.drain()
                        dve.tensor_scalar(st[:, 2, :], st[:, 0, :], 1.0 / HD, GN_EPS, ALU.mult, ALU.add
                                          ).then_inc(var_done, 1)
                        dve.wait_ge(root_done, k)
                        dve.reciprocal(st[:, 4, :], st[:, 3, :])
                        dve.drain()
                        dve.tensor_tensor(heads_of(yc), heads_of(yc), b8(4), ALU.mult)
                        dve.drain()
                        dve.tensor_tensor(yc, yc, lnw[:], ALU.mult)
                        dve.drain()
                        dve.tensor_tensor(yc, yc, lnb[:], ALU.add)
                        dve.drain()
                        dve.tensor_tensor(yc, yc, gb[:, 1, :], ALU.add)
                        dve.drain()
                        dve.tensor_tensor(yc, yc, gb[:, 0, :], ALU.mult).then_inc(y_done, 1)
                        dve.wait_ge(y_ps, k * 2)
                        dve.tensor_copy(yT[:, 0:4, :], ps[:, 0, :].rearrange("p (t n) -> p t n", n=P)
                                        ).then_inc(yT_done, 1)
                        dve.sem_inc(y_used, 1)
                        dve.wait_ge(prod, k)
                        dve.tensor_tensor(fs[:], ps[:, 2:4, :], GA[:, j, :].rearrange("p (a n) -> p a n", a=2), ALU.mult)
                        dve.drain()
                        dve.wait_ge(x_in, k * 16)
                        dve.tensor_tensor(x[:], x[:], fs[:], ALU.add).then_inc(x_done, 1)
                        dve.drain()
                        dve.scalar_tensor_tensor(fs[:], x[:], 1.0, x[:], ALU.mult, ALU.mult, accum_out=small[:, 0:1])
                        dve.drain()
                        dve.tensor_scalar(small[:, 1:2], small[:, 0:1], 1.0 / D, EPS, ALU.mult, ALU.add
                                          ).then_inc(f_var, 1)
                        dve.wait_ge(f_root, k)
                        dve.reciprocal(small[:, 3:4], small[:, 2:3])
                        dve.drain()
                        dve.scalar_tensor_tensor(fs[:], x[:], small[:, 3:4], G[:, j, :], ALU.mult, ALU.mult)
                        dve.drain()
                        dve.wait_ge(f_stored, k * 16)
                        dve.tensor_tensor(f[:], fs[:], S[:, j, :], ALU.add).then_inc(f_done, 1)
                        dve.sem_inc(x_used, 1)
                        dve.wait_ge(f_ps, k * 2 - 1)
                        dve.tensor_copy(fT[:, 0:4, :], ps[:, 4, :].rearrange("p (t n) -> p t n", n=P)
                                        ).then_inc(fT_done, 1)
                        dve.wait_ge(lg_ps, k)
                        dve.tensor_tensor(lg[:], ps[:, 6, 0:RW], br[:], ALU.add)
                        dve.drain()
                        gl, el = lg[:, 0:NG], lg[:, NG:]
                        el3 = el.rearrange("p (g e) -> p g e", g=NG)

                        def first_largest(v, r, top, out, at):
                            w_ = v.shape[-1]
                            dve.tensor_reduce(r1[:, top:top + 1], v, AX.X, ALU.max)
                            dve.drain()
                            c_ = sel[:, at, 0:w_]
                            dve.scalar_tensor_tensor(c_, v, r1[:, top:top + 1], r, ALU.is_equal, ALU.mult)
                            dve.drain()
                            dve.tensor_reduce(r1[:, top + 1:top + 2], c_, AX.X, ALU.max)
                            dve.drain()
                            dve.tensor_scalar(out, c_, r1[:, top + 1:top + 2], None, ALU.is_equal)
                            dve.drain()

                        pick = sel[:, 1, 0:NG]
                        first_largest(gl, rev[:, 0:NG], 0, pick, 0)
                        dve.tensor_scalar(ex[:, 0, 0:NG], gl, r1[:, 0:1], None, ALU.subtract)
                        dve.tensor_scalar(sel[:, 2, 0:NG], pick, 1.0, BIG, ALU.subtract, ALU.mult)
                        dve.drain()
                        dve.tensor_tensor(el3, el3, sel[:, 2, 0:NG].unsqueeze(2).broadcast_to([P, NG, EPG]), ALU.add)
                        dve.drain()
                        one, two = sel[:, 1, 0:NE], sel[:, 3, 0:NE]
                        first_largest(el, rev[:, NG:], 2, one, 0)
                        dve.tensor_copy(net.chosen[:, ds(tile, 1), 0, :], one.unsqueeze(1))
                        dve.scalar_tensor_tensor(el, one, -2.0 * BIG, el, ALU.mult, ALU.add)
                        dve.drain()
                        first_largest(el, rev[:, NG:], 4, two, 0)
                        dve.tensor_copy(net.chosen[:, ds(tile, 1), 1, :], two.unsqueeze(1))
                        dve.tensor_tensor(ex[:, 0, NG:NG + 1], r1[:, 4:5], r1[:, 2:3], ALU.subtract
                                          ).then_inc(diff_done, 1)
                        dve.wait_ge(exp_done, k)
                        dve.tensor_reduce(r1[:, 8:9], ex[:, 1, 0:NG], AX.X, ALU.add)
                        dve.tensor_scalar(r1[:, 9:10], ex[:, 1, NG:NG + 1], 1.0, None, ALU.add)
                        dve.drain()
                        dve.tensor_tensor(r1[:, 10:11], r1[:, 8:9], r1[:, 9:10], ALU.mult)
                        dve.drain()
                        dve.reciprocal(r1[:, 11:12], r1[:, 10:11])
                        dve.drain()
                        dve.tensor_tensor(r1[:, 12:13], r1[:, 11:12], ex[:, 1, NG:NG + 1], ALU.mult)
                        dve.drain()
                        dve.tensor_copy(net.gate[:, ds(tile, 1), :], r1[:, 11:13].unsqueeze(1))
                        dve.drain()

            @block.tensor
            def _(pe):
                pe.wait_ge(c_in, 16 * NCON)
                for seg, before in segs:
                    with pe.Fori(0, tokens_of(seg)[1]) as i:
                        k = i + (1 + before)
                        pe.wait_ge(y_done, k)
                        for t in range(DT):
                            tr = pe.transpose(ps[:, t // 4, (t % 4) * P:(t % 4 + 1) * P], y[:, t * P:(t + 1) * P], ident[:])
                            if t % 4 == 3:
                                tr.then_inc(y_ps, 1)
                        pe.wait_ge(yT_done, k * 2)
                        for c in range(2):
                            for t in range(DT):
                                mm = pe.matmul(ps[:, 2 + c, :], yT[:, t, :], w[:, t, c * 512:(c + 1) * 512],
                                               start=(t == 0), stop=(t == DT - 1))
                        mm.then_inc(prod, 1)
                        pe.wait_ge(f_done, k)
                        for t in range(DT):
                            tr = pe.transpose(ps[:, 4 + t // 4, (t % 4) * P:(t % 4 + 1) * P],
                                              f[:, t * P:(t + 1) * P], ident[:])
                            if t % 4 == 3:
                                tr.then_inc(f_ps, 1)
                        pe.wait_ge(fT_done, k * 2)
                        for t in range(DT):
                            mm = pe.matmul(ps[:, 6, 0:RW], fT[:, t, :], wr[:, t, :], start=(t == 0), stop=(t == DT - 1))
                        mm.then_inc(lg_ps, 1)


def placement_phase(nc, net, ps, layer):
    ins = net.ins
    t0 = CT if layer == DEPTH - 1 else 0
    n = NT - t0
    with phase(nc) as (sb, sem):
        ident, before, ones = sb("ident", [P, P]), sb("before", [P, P]), sb("ones", [P, P])
        before_e = sb("before_e", [NE, NE])
        e_row = sb("e_row", [P, NE])
        j_row = sb("j_row", [1, OVER])
        both = sb("both", [P, NT, NE])
        rank, place, w = sb("rank", [P, NT, NE]), sb("place", [P, NT, NE]), sb("w", [P, NT, NE])
        count, nov, shift = sb("count", [P, NE]), sb("nov", [P, NE]), sb("shift", [P, NE])
        novT = sb("novT", [NE, P])
        end = sb("end", [P, NE])
        cmp = sb("cmp", [1, OVER, NE])
        blk = sb("blk", [1, OVER + 1])
        rowf = sb("rowf", [P, NT, 2])
        token = sb("token", [P, NT], I32)
        zero = sb("zero", [P, NB], I32)
        c_in, both_done, rank_ps, nov_done, novT_ps, novT_done, ov_ps, rows_done, cleared, scattered, pool_c = (
            sem(s) for s in ("c_in", "both_done", "rank_ps", "nov_done", "novT_ps", "novT_done", "ov_ps",
                             "rows_done", "cleared", "scattered", "pool_c"))
        with nc.Block() as block:
            @block.sync
            def _(sp):
                sp.dma_start(ident[:], ins["k_ident"]).then_inc(c_in, 16)
                sp.dma_start(before[:], ins["k_before"]).then_inc(c_in, 16)
                sp.dma_start(before_e[:], ins["k_before_e"]).then_inc(c_in, 16)
                sp.dma_start(e_row[:], ins["k_e_row"].partition_broadcast(P)).then_inc(c_in, 16)
                sp.dma_start(j_row[:], ins["k_j_row"].partition_broadcast(1)).then_inc(c_in, 16)
                sp.wait_ge(pool_c, 3)
                sp.dma_start(net.table.rearrange("(p b) o -> p (b o)", p=P), zero[:]).then_inc(cleared, 16)

            @block.gpsimd
            def _(pool):
                pool.memset(ones[:], 1.0).then_inc(pool_c, 1)
                pool.memset(zero[:], 0).then_inc(pool_c, 1)
                pool.iota(token[:], pattern=[[P, NT]], base=0, channel_multiplier=1).then_inc(pool_c, 1)
                pool.wait_ge(pool_c, 3)
                pool.wait_ge(cleared, 16)
                pool.wait_ge(rows_done, 1)
                for t in range(t0, NT):
                    for j in range(2):
                        pool.indirect_dma_start(net.table, bass.IndirectOffsetOnAxis(net.row[:, t, j:j + 1], 0),
                                                token[:, t:t + 1], None).then_inc(scattered, 16)
                pool.wait_ge(scattered, 16 * 2 * n)

            @block.vector
            def _(dve):
                T = slice(t0, NT)
                dve.tensor_tensor(both[:, T], net.chosen[:, T, 0, :], net.chosen[:, T, 1, :], ALU.add
                                  ).then_inc(both_done, 1)
                dve.wait_ge(rank_ps, 1)
                dve.tensor_copy(rank[:, T], ps[:, 0, 0:n * NE].rearrange("p (t e) -> p t e", e=NE))
                dve.tensor_copy(count[:], ps[:, 1, 0:NE])
                dve.drain()
                dve.tensor_scalar(nov[:], count[:], float(P), None, ALU.is_gt)
                for m in range(2, NT):
                    dve.drain()
                    dve.scalar_tensor_tensor(nov[:], count[:], float(P * m), nov[:], ALU.is_gt, ALU.add)
                dve.drain()
                dve.sem_inc(nov_done, 1)
                dve.wait_ge(novT_ps, 1)
                dve.tensor_copy(novT[:], ps[0:NE, 2, 0:P]).then_inc(novT_done, 1)
                dve.wait_ge(ov_ps, 1)
                dve.tensor_scalar(shift[:], ps[:, 3, 0:NE], float(P), float((NE - 1) * P), ALU.mult, ALU.add)
                dve.tensor_tensor(end[:], ps[:, 3, 0:NE], nov[:], ALU.add)
                dve.drain()
                dve.wait_ge(c_in, 80)
                dve.tensor_tensor(shift[:], shift[:], e_row[:], ALU.subtract)
                dve.tensor_scalar(w[:, T], rank[:, T], float(P), None, ALU.is_ge)
                dve.tensor_tensor(place[:, T], rank[:, T], e_row[:].unsqueeze(1).broadcast_to([P, n, NE]), ALU.add)
                dve.drain()
                dve.tensor_tensor(w[:, T], w[:, T], shift[:].unsqueeze(1).broadcast_to([P, n, NE]), ALU.mult)
                dve.drain()
                dve.tensor_tensor(place[:, T], place[:, T], w[:, T], ALU.add)
                for j in range(2):
                    dve.drain()
                    dve.tensor_tensor(w[:, T], place[:, T], net.chosen[:, T, j, :], ALU.mult)
                    dve.drain()
                    dve.tensor_reduce(rowf[:, T, j], w[:, T], AX.X, ALU.add)
                dve.drain()
                dve.tensor_copy(net.row[:, T, :], rowf[:, T, :])
                e3 = end[0:1, :].unsqueeze(1).broadcast_to([1, OVER, NE])
                dve.tensor_tensor(cmp[:], e3, j_row[:].unsqueeze(2).broadcast_to([1, OVER, NE]), ALU.is_le)
                dve.drain()
                dve.tensor_reduce(blk[:, 0:OVER], cmp[:], AX.X, ALU.add)
                dve.tensor_copy(blk[:, OVER:OVER + 1], end[0:1, NE - 1:NE])
                dve.drain()
                dve.tensor_scalar(blk[:, 0:OVER], blk[:, 0:OVER], float(NE - 1), None, ALU.min)
                dve.drain()
                dve.tensor_copy(net.blocks[:], blk[:])
                dve.drain()
                dve.sem_inc(rows_done, 1)

            @block.tensor
            def _(pe):
                pe.wait_ge(c_in, 80)
                pe.wait_ge(pool_c, 3)
                pe.wait_ge(both_done, 1)
                for t in range(t0, NT):
                    o = ps[:, 0, (t - t0) * NE:(t - t0 + 1) * NE]
                    for u in range(t0, t):
                        pe.matmul(o, ones[:], both[:, u, :], start=(u == t0), stop=False)
                    mm = pe.matmul(o, before[:], both[:, t, :], start=(t == t0), stop=True)
                for t in range(t0, NT):
                    mm = pe.matmul(ps[:, 1, 0:NE], ones[:], both[:, t, :], start=(t == t0), stop=(t == NT - 1))
                mm.then_inc(rank_ps, 1)
                pe.wait_ge(nov_done, 1)
                pe.transpose(ps[0:NE, 2, 0:P], nov[:], ident[:]).then_inc(novT_ps, 1)
                pe.wait_ge(novT_done, 1)
                pe.matmul(ps[:, 3, 0:NE], novT[:], before_e[:], start=True, stop=True).then_inc(ov_ps, 1)


def expert_phase(nc, net, ps, layer):
    ins = net.ins
    HF = FF // P
    with phase(nc) as (sb, sem):
        ident = sb("ident", [P, P])
        w1 = [sb(f"w1{b}", [P, DT, FF]) for b in range(2)]
        w3 = [sb(f"w3{b}", [P, DT, FF]) for b in range(2)]
        w2 = [sb(f"w2{b}", [P, HF, D]) for b in range(2)]
        idx = [sb(f"idx{b}", [P, 1], I32) for b in range(2)]
        xg = [sb(f"xg{b}", [P, D]) for b in range(2)]
        xT = [sb(f"xT{b}", [P, DT, P]) for b in range(2)]
        sg = [sb(f"sg{b}", [P, FF]) for b in range(2)]
        h = [sb(f"h{b}", [P, FF]) for b in range(2)]
        hT = [sb(f"hT{b}", [P, HF, P]) for b in range(2)]
        yo = [sb(f"yo{b}", [P, D]) for b in range(2)]
        c_in, pool_step, act_step = sem("c_in"), sem("pool_step"), sem("act_step")
        w13_in = [sem(f"w13_in{b}") for b in range(2)]
        w2_in = [sem(f"w2_in{b}") for b in range(2)]
        idx_in = [sem(f"idx_in{b}") for b in range(2)]
        x_in = [sem(f"x_in{b}") for b in range(2)]
        stored = [sem(f"stored{b}") for b in range(2)]
        x_ps, xT_done, up, sig, h_done, h_ps, hT_done, down, y_done = (
            sem(n) for n in ("x_ps", "xT_done", "up", "sig", "h_done", "h_ps", "hT_done", "down", "y_done"))
        UP = lambda b: 2 + 2 * b
        XB = lambda b: 6 * b

        def pairs(eng, pair):
            used = eng.value_load(net.blocks[0:1, OVER:OVER + 1], min_val=0, max_val=OVER)
            with eng.Fori(0, NE // 2) as i:
                pair(i, 0)
            with eng.Fori(0, OVER // 2) as i:
                with eng.If(i * 2 < used):
                    pair(i, NE)
        with nc.Block() as block:
            @block.sync
            def _(sp):
                sp.dma_start(ident[:], ins["k_ident"]).then_inc(c_in, 16)
                sp.sem_inc(up, 2)
                sp.sem_inc(down, 2)

                def pair(i, before):
                    for b in range(2):
                        q = i * 2 + (b + before + 1)
                        e = i * 2 + b
                        if before:
                            e = sp.value_load(net.blocks[0:1, ds(i * 2 + b, 1)], min_val=0, max_val=NE - 1)
                        sp.wait_ge(up, q)
                        for w, name in ((w1[b], "e_w1"), (w3[b], "e_w3")):
                            src = ins[name][layer].rearrange("e (p t) f -> e p (t f)", p=P)[ds(e, 1)]
                            sp.dma_start(w[:].rearrange("p t f -> p (t f)"), src.rearrange("o p n -> (o p) n")
                                         ).then_inc(w13_in[b], 16)
                        sp.wait_ge(down, q)
                        src = ins["e_w2"][layer].rearrange("e (p t) f -> e p (t f)", p=P)[ds(e, 1)]
                        sp.dma_start(w2[b][:].rearrange("p t f -> p (t f)"), src.rearrange("o p n -> (o p) n")
                                     ).then_inc(w2_in[b], 16)
                pairs(sp, pair)

            @block.gpsimd
            def _(pool):
                pool.sem_inc(x_ps, 2)

                def pair(i, before):
                    m = i + (1 + before // 2)
                    for b in range(2):
                        q = i * 2 + (b + before + 1)
                        pool.wait_ge(x_ps, q)
                        pool.sem_inc(pool_step, 1)
                        pool.dma_start(idx[b][:], net.table[ds((i * 2 + (b + before)) * P, P), :]
                                       ).then_inc(idx_in[b], 16)
                        pool.wait_ge(idx_in[b], m * 16)
                        pool.sem_inc(pool_step, 1)
                        pool.indirect_dma_start(xg[b][:], None, net.f, bass.IndirectOffsetOnAxis(idx[b][:, 0:1], 0)
                                                ).then_inc(x_in[b], 16)
                pairs(pool, pair)

            @block.scalar
            def _(act):
                for b in range(2):
                    act.sem_inc(stored[b], 16)

                def pair(i, before):
                    m = i + (1 + before // 2)
                    for b in range(2):
                        q = i * 2 + (b + before + 1)
                        act.wait_ge(x_ps, q + 2)
                        act.activation(xT[b][:, 4:8, :], ps[:, XB(b) + 1, :].rearrange("p (t n) -> p t n", n=P),
                                       ACT.Copy).then_inc(xT_done, 1)
                    for b in range(2):
                        act.wait_ge(up, i * 2 + (b + before + 3))
                        act.activation(sg[b][:], ps[:, UP(b), :], ACT.Sigmoid).then_inc(sig, 1)
                    for b in range(2):
                        q = i * 2 + (b + before + 1)
                        act.wait_ge(h_ps, q)
                        act.activation(hT[b][:], ps[:, 6 + b, :].rearrange("p (t n) -> p t n", n=P), ACT.Copy
                                       ).then_inc(hT_done, 1)
                    for b in range(2):
                        q = i * 2 + (b + before + 1)
                        act.wait_ge(down, q + 2)
                        act.wait_ge(stored[b], m * 16)
                        act.activation(yo[b][:], ps[:, UP(b):UP(b) + 2, :], ACT.Copy).then_inc(y_done, 1)
                        act.wait_ge(y_done, q + 2)
                        act.dma_start(rows(net.ye, (i * 2 + (b + before)) * P), yo[b][:]).then_inc(stored[b], 16)
                    if before:
                        for b in range(2):
                            act.wait_ge(stored[b], (m + 1) * 16)
                        act.sem_inc(act_step, 1)
                pairs(act, pair)
                for b in range(2):
                    act.wait_ge(stored[b], 16 * (NE // 2 + 1))

            @block.vector
            def _(dve):
                def pair(i, before):
                    for b in range(2):
                        dve.wait_ge(x_ps, i * 2 + (b + before + 3))
                        dve.tensor_copy(xT[b][:, 0:4, :], ps[:, XB(b), :].rearrange("p (t n) -> p t n", n=P)
                                        ).then_inc(xT_done, 1)
                    for b in range(2):
                        dve.wait_ge(sig, i * 2 + (b + before + 1))
                        dve.tensor_tensor(sg[b][:], sg[b][:], ps[:, UP(b), :], ALU.mult)
                        dve.drain()
                        dve.tensor_tensor(h[b][:], sg[b][:], ps[:, UP(b) + 1, :], ALU.mult).then_inc(h_done, 1)
                pairs(dve, pair)

            @block.tensor
            def _(pe):
                pe.wait_ge(c_in, 16)
                pe.sem_inc(y_done, 2)

                def pair(i, before):
                    m = i + (1 + before // 2)
                    for b in range(2):
                        pe.wait_ge(x_in[b], m * 16)
                        for t in range(DT):
                            tr = pe.transpose(ps[:, XB(b) + t // 4, (t % 4) * P:(t % 4 + 1) * P],
                                              xg[b][:, t:D:DT], ident[:])
                        tr.then_inc(x_ps, 1)
                    for b in range(2):
                        q = i * 2 + (b + before + 1)
                        pe.wait_ge(xT_done, i * 4 + (4 + 2 * before))
                        pe.wait_ge(w13_in[b], m * 32)
                        pe.wait_ge(y_done, q)
                        for j, w in enumerate((w1[b], w3[b])):
                            for t in range(DT):
                                mm = pe.matmul(ps[:, UP(b) + j, :], xT[b][:, t, :], w[:, t, :],
                                               start=(t == 0), stop=(t == DT - 1))
                        mm.then_inc(up, 1)
                    for b in range(2):
                        q = i * 2 + (b + before + 1)
                        pe.wait_ge(h_done, q)
                        for t in range(HF):
                            tr = pe.transpose(ps[:, 6 + b, t * P:(t + 1) * P], h[b][:, t:FF:HF], ident[:])
                        tr.then_inc(h_ps, 1)
                        pe.wait_ge(hT_done, q)
                        pe.wait_ge(w2_in[b], m * 16)
                        for c in range(2):
                            for t in range(HF):
                                mm = pe.matmul(ps[:, UP(b) + c, :], hT[b][:, t, :], w2[b][:, t, c * 512:(c + 1) * 512],
                                               start=(t == 0), stop=(t == HF - 1))
                        mm.then_inc(down, 1)
                pairs(pe, pair)


def combine_phase(nc, net, ps, layer):
    ins = net.ins
    last = layer == DEPTH - 1
    segs = [("lat", 0)] if last else [("ctx", 0), ("lat", CT)]
    n_all = LT if last else NT
    with phase(nc) as (sb, sem):
        GA = sb("GA", [P, 2, D])
        gain = sb("gain", [P, D])
        x, mix, o = sb("x", [P, D]), sb("mix", [P, D]), sb("o", [P, D])
        y = [sb(f"y{j}", [P, D]) for j in range(2)]
        idx = [sb(f"idx{j}", [P, 1], U32) for j in range(2)]
        gate = sb("gate", [P, 2])
        small = sb("small", [P, 4])
        c_in, x_in, used, idx_done, y_in, mean_done, root_done, o_done, stored, pool_step = (
            sem(n) for n in ("c_in", "x_in", "used", "idx_done", "y_in", "mean_done", "root_done", "o_done",
                             "stored", "pool_step"))
        with nc.Block() as block:
            @block.sync
            def _(sp):
                for j in range(2):
                    sp.dma_start(GA[:, j, :], net.mod[layer][j][5 * D:6 * D].partition_broadcast(P)).then_inc(c_in, 16)
                sp.dma_start(gain[:], ins["g_final"].partition_broadcast(P)).then_inc(c_in, 16)
                sp.sem_inc(used, 1)
                for seg, before in segs:
                    r0, n, _ = tokens_of(seg)
                    with sp.Fori(0, n) as i:
                        sp.wait_ge(used, i + (1 + before))
                        sp.dma_start(x[:], rows(net.x, i * P + r0)).then_inc(x_in, 16)

            @block.gpsimd
            def _(pool):
                for seg, before in segs:
                    r0, n, _ = tokens_of(seg)
                    with pool.Fori(0, n) as i:
                        k = i + (1 + before)
                        pool.wait_ge(idx_done, k)
                        pool.sem_inc(pool_step, 1)
                        for j in range(2):
                            pool.indirect_dma_start(y[j][:], None, net.ye, bass.IndirectOffsetOnAxis(idx[j][:, 0:1], 0)
                                                    ).then_inc(y_in, 16)

            @block.scalar
            def _(act):
                act.sem_inc(stored, 16)
                for seg, before in segs:
                    r0, n, _ = tokens_of(seg)
                    with act.Fori(0, n) as i:
                        k = i + (1 + before)
                        if last:
                            act.wait_ge(mean_done, k)
                            act.activation(small[:, 2:3], small[:, 1:2], ACT.Sqrt).then_inc(root_done, 1)
                        act.wait_ge(o_done, k)
                        dst = rows(net.out[0], i * P) if last else rows(net.x, i * P + r0)
                        act.dma_start(dst, o[:]).then_inc(stored, 16)
                act.wait_ge(stored, 16 * (n_all + 1))

            @block.vector
            def _(dve):
                dve.wait_ge(c_in, 48)
                for seg, before in segs:
                    r0, n, _ = tokens_of(seg)
                    j = 1 if seg == "ctx" else 0
                    with dve.Fori(0, n) as i:
                        k = i + (1 + before)
                        tile = i + r0 // P
                        for q in range(2):
                            dve.tensor_copy(idx[q][:].unsqueeze(1), net.row[:, ds(tile, 1), q:q + 1])
                        dve.tensor_copy(gate[:].unsqueeze(1), net.gate[:, ds(tile, 1), :])
                        dve.drain()
                        dve.sem_inc(idx_done, 1)
                        dve.wait_ge(y_in, k * 32)
                        dve.tensor_scalar(mix[:], y[0][:], gate[:, 0:1], None, ALU.mult)
                        dve.drain()
                        dve.scalar_tensor_tensor(mix[:], y[1][:], gate[:, 1:2], mix[:], ALU.mult, ALU.add)
                        dve.drain()
                        dve.tensor_tensor(mix[:], mix[:], GA[:, j, :], ALU.mult)
                        dve.drain()
                        dve.wait_ge(x_in, k * 16)
                        dve.wait_ge(stored, k * 16)
                        if not last:
                            dve.tensor_tensor(o[:], x[:], mix[:], ALU.add).then_inc(o_done, 1)
                            dve.drain()
                            dve.sem_inc(used, 1)
                            continue
                        dve.tensor_tensor(x[:], x[:], mix[:], ALU.add)
                        dve.drain()
                        dve.scalar_tensor_tensor(mix[:], x[:], 1.0, x[:], ALU.mult, ALU.mult, accum_out=small[:, 0:1])
                        dve.drain()
                        dve.tensor_scalar(small[:, 1:2], small[:, 0:1], 1.0 / D, EPS, ALU.mult, ALU.add
                                          ).then_inc(mean_done, 1)
                        dve.wait_ge(root_done, k)
                        dve.reciprocal(small[:, 3:4], small[:, 2:3])
                        dve.drain()
                        dve.scalar_tensor_tensor(o[:], x[:], small[:, 3:4], gain[:], ALU.mult, ALU.mult
                                                 ).then_inc(o_done, 1)
                        dve.drain()
                        dve.sem_inc(used, 1)


INPUTS = ["x", "c", "ctx", "c_ctx", "w_mod", "b_mod", "g_mix", "g_ffn", "w_in", "a_q_gain", "a_k_gain",
          "b_lq1", "b_lk1", "b_lq2", "b_lk2", "b_subln", "c_mu", "c_w0", "c_w2", "c_a0", "c_a2", "c_g2",
          "c_k_k", "c_k_a", "c_r_k", "c_ln_w", "c_ln_b", "w_out", "r_w_group", "r_b_group",
          "r_w_expert", "r_b_expert", "e_w1", "e_w3", "e_w2", "g_final"]


def constants():
    tri, mask, levels = scan_constants()
    i = np.arange(P)
    return {
        "k_ident": np.eye(P, dtype=np.float32),
        "k_rope": rope_tables(),
        "k_tri": tri, "k_mask": mask, "k_levels": levels,
        "k_before": (i[:, None] < i[None, :]).astype(np.float32),
        "k_rev": np.concatenate([NG - np.arange(NG), NE - np.arange(NE)]).astype(np.float32),
        "k_e_row": (P * np.arange(NE)).astype(np.float32),
        "k_j_row": np.arange(OVER).astype(np.float32),
        "k_before_e": (np.arange(NE)[:, None] < np.arange(NE)[None, :]).astype(np.float32),
    }




def build(nc, ins, out):
    net = Net(nc, ins, out)
    with (nc.psum_tensor("ps", [P, 8, 512], F32) as ps_t, nc.sbuf_tensor("chosen", [P, NT, 2, NE], F32) as chosen,
          nc.sbuf_tensor("gate", [P, NT, 2], F32) as gate, nc.sbuf_tensor("row", [P, NT, 2], U32) as row,
          nc.sbuf_tensor("blocks", [1, OVER + 1], I32) as blocks):
        ps = ps_t[:]
        net.chosen, net.gate, net.row, net.blocks = chosen, gate, row, blocks
        steps = [lambda: modulation_phase(nc, net, ps)]
        for layer in range(DEPTH):
            for f in LAYER_PHASES:
                steps.append(lambda f=f, layer=layer: f(nc, net, ps, layer))
        for s in steps:
            s()


LAYER_PHASES = [input_projection_phase, attention_phase, rwkv_input_phase, scan_phase,
                mix_output_phase, placement_phase, expert_phase, combine_phase]


def kernel(**inputs):
    import concourse.bacc as bacc
    from concourse.bass_utils import run_bass_kernel_spmd

    nc = bacc.Bacc("TRN2", target_bir_lowering=False, num_devices=1)
    arrays, ins = {}, {}
    for name, a in {**{n: inputs[n] for n in INPUTS}, **constants()}.items():
        a = np.ascontiguousarray(a)
        arrays[f"in_{name}"] = a
        ins[name] = nc.dram_tensor(f"in_{name}", a.shape, mybir.dt.from_np(a.dtype), kind="ExternalInput").ap()
    out = nc.dram_tensor("out_0", (1, SEQ, D), F32, kind="ExternalOutput").ap()
    build(nc, ins, out)
    return run_bass_kernel_spmd(nc, [arrays], core_ids=[0]).results[0]["out_0"]
```

```python
from contextlib import ExitStack, contextmanager

import numpy as np

import concourse.bass as bass
from concourse import mybir

F32 = mybir.dt.float32
I32 = mybir.dt.int32
U32 = mybir.dt.uint32
ALU = mybir.AluOpType
ACT = mybir.ActivationFunctionType
AX = mybir.AxisListType
ds = bass.ds

P = 128
D = 1024
DT = D // P
DEPTH = 2
SEQ = 1024
CTX = 256
TOK = SEQ + CTX
NT = TOK // P
CT = CTX // P
LT = SEQ // P
GRID_W = 64
EPS = 1e-6
HD = 64
A_Q, A_KV, B_Q, B_V = 256, 128, 256, 256
ATT = A_Q + 2 * A_KV + 2 * B_Q + B_V
CW = 512
CH = 8
LORA = 384
CS = 3 * CW + LORA
IN_W = ATT + CS
GN_EPS = 64e-5
NG, EPG, NE, FF = 4, 8, 32, 512
SLOTS = TOK * 2
OVER = 2 * ((SLOTS - 1) // P // 2 + 1)
NB = NE + OVER
C = 64
NC_CTX = CTX // C
NC_LAT = SEQ // C
NZ = 2
ST = NZ * CH

PAD_ROWS = TOK + 3
SEGMENTS = {"ctx": (0, CT, 1), "lat": (CTX, LT, CTX + 2)}


def tokens_of(seg):
    return SEGMENTS[seg]


@contextmanager
def phase(nc):
    sems = []
    with ExitStack() as ctx:
        def sb(name, shape, dt=F32):
            return ctx.enter_context(nc.sbuf_tensor(nc_name(name), shape, dt))

        def sem(name):
            s = nc.alloc_semaphore(nc_name(name))
            sems.append(s)
            return s

        yield sb, sem
        nc.clear_and_free_semaphores(sems)
        nc.all_engine_barrier()


_names = {}


def nc_name(name):
    _names[name] = _names.get(name, 0) + 1
    return f"{name}_{_names[name]}"


def rows(ap, start, n=P):
    return ap[ds(start, n), :]


def rope_tables():
    def table(dim):
        half = dim // 2
        inv = np.float32(10000.0) ** (-np.arange(0, half, 2, dtype=np.float32) / np.float32(half))
        t = np.arange(SEQ)
        ar = (t // GRID_W).astype(np.float32)[:, None] * inv.astype(np.float32)
        ac = (t % GRID_W).astype(np.float32)[:, None] * inv.astype(np.float32)
        ang = np.concatenate([ar, ar, ac, ac], -1).astype(np.float32)
        q = dim // 4
        sign = np.tile(np.concatenate([-np.ones(q), np.ones(q)]), 2).astype(np.float32)
        return np.cos(ang).astype(np.float32), (np.sin(ang) * sign).astype(np.float32)
    ca, sa = table(64)
    cb, sb = table(32)
    return np.concatenate([np.tile(ca, 6), np.tile(cb, 16), np.tile(sa, 6), np.tile(sb, 16)], -1)


ROPE_W = 6 * 64 + 16 * 32


def scan_constants():
    i = np.arange(C)
    before = [i[:, None] < i[None, :], i[:, None] > i[None, :]]
    eye = np.eye(C, dtype=bool)
    tri = np.zeros((C, NZ, 2 * P), np.float32)
    mask = np.zeros((P, NZ, P), np.float32)
    for z in range(NZ):
        incl = (before[z] | eye).astype(np.float32)
        excl = before[z].astype(np.float32)
        tri[:, z] = np.concatenate([incl, excl, -incl, -incl], 1)
        half = np.concatenate([incl, excl], 1)
        mask[:, z] = np.concatenate([half, half], 0)
    levels = []
    n = 1
    while n < C:
        up = (i[:, None] // (2 * n) == i[None, :] // (2 * n)) & (i[:, None] // n != i[None, :] // n)
        levels.append(np.stack([(up & before[z]).astype(np.float32) for z in range(NZ)], 1))
        n *= 2
    lv = np.stack(levels, 1).reshape(C, -1)
    return tri.reshape(C, -1), mask.reshape(P, -1), lv


LEVELS = 6


class Net:

    def __init__(self, nc, ins, out):
        self.ins = ins
        self.out = out
        self.x = nc.dram_tensor("s_x", [TOK, D], F32).ap()
        self.mod = nc.dram_tensor("s_mod", [DEPTH, 2, 6 * D], F32).ap()
        self.p = nc.dram_tensor("s_p", [PAD_ROWS, IN_W], F32).ap()
        self.y = nc.dram_tensor("s_y", [TOK, D], F32).ap()
        self.scan = nc.dram_tensor("s_scan", [TOK, 9 * CW], F32).ap()
        self.gb = nc.dram_tensor("s_gb", [TOK, 2 * CW], F32).ap()
        self.yd = nc.dram_tensor("s_yd", [NZ, TOK, CW], F32).ap()
        self.f = nc.dram_tensor("s_f", [TOK, D], F32).ap()
        self.table = nc.dram_tensor("s_table", [NB * P, 1], I32).ap()
        self.ye = nc.dram_tensor("s_ye", [NB * P, D], F32).ap()


def modulation_phase(nc, net, ps):
    NW = 512
    NCH = 6 * D // NW
    ins = net.ins
    with phase(nc) as (sb, sem):
        cond = sb("cond", [P, 2, DT])
        sig = sb("sig", [P, 2, DT])
        act = sb("act", [P, DT, 2])
        wt = [sb(f"wt{b}", [P, DT, NW]) for b in range(2)]
        bias = [sb(f"bias{b}", [2, NW]) for b in range(2)]
        res = [sb(f"res{b}", [2, NW]) for b in range(2)]
        zrow = sb("zrow", [1, CS])
        cond_in, sig_done, act_done = sem("cond_in"), sem("sig_done"), sem("act_done")
        w_in = [sem(f"w_in{b}") for b in range(2)]
        sums, added, stored, zeroed, side = (sem(n) for n in ("sums", "added", "stored", "zeroed", "side"))
        with nc.Block() as block:
            @block.sync
            def _(sp):
                sp.dma_start(cond[:, 0, :], ins["c"].rearrange("o (p t) -> p (o t)", t=DT)).then_inc(cond_in, 16)
                sp.dma_start(cond[:, 1, :], ins["c_ctx"].rearrange("(p t) -> p t", t=DT)).then_inc(cond_in, 16)
                for layer in range(DEPTH):
                    w = ins["w_mod"][layer].rearrange("(p t) n -> p t n", t=DT)
                    with sp.Fori(0, NCH // 2) as i:
                        for b in range(2):
                            n = (i * 2 + b)
                            sp.wait_ge(sums, n + (1 + layer * NCH))
                            sp.dma_start(wt[b][:], w[:, :, ds(n * NW, NW)]).then_inc(w_in[b], 16)
                            sp.wait_ge(added, n + (1 + layer * NCH))
                            src = ins["b_mod"][layer][ds(n * NW, NW)].partition_broadcast(2)
                            sp.dma_start(bias[b][:], src).then_inc(w_in[b], 16)

            @block.gpsimd
            def _(pool):
                pool.memset(zrow[:], 0.0).then_inc(zeroed, 1)

            @block.scalar
            def _(act_e):
                act_e.wait_ge(cond_in, 32)
                act_e.activation(sig[:], cond[:], ACT.Sigmoid).then_inc(sig_done, 1)
                act_e.dma_start(net.x[0:CTX, :], ins["ctx"][0]).then_inc(side, 16)
                act_e.dma_start(net.x[CTX:TOK, :], ins["x"][0]).then_inc(side, 16)
                act_e.wait_ge(zeroed, 1)
                for r in (0, CTX + 1, PAD_ROWS - 1):
                    act_e.dma_start(net.p[r:r + 1, ATT:IN_W], zrow[:]).then_inc(side, 16)
                act_e.wait_ge(side, 5 * 16)
                for layer in range(DEPTH):
                    with act_e.Fori(0, NCH // 2) as i:
                        for b in range(2):
                            n = (i * 2 + b)
                            act_e.wait_ge(added, n + (3 + layer * NCH))
                            act_e.dma_start(net.mod[layer][:, ds(n * NW, NW)], res[b][:]).then_inc(stored, 16)
                            act_e.wait_ge(stored, (n + (3 + layer * NCH)) * 16)

            @block.vector
            def _(dve):
                dve.wait_ge(sig_done, 1)
                dve.tensor_tensor(act[:].rearrange("p t j -> p j t"), cond[:], sig[:], ALU.mult).then_inc(act_done, 1)
                dve.sem_inc(stored, 32)
                dve.sem_inc(added, 2)
                for layer in range(DEPTH):
                    with dve.Fori(0, NCH // 2) as i:
                        for b in range(2):
                            n = (i * 2 + b)
                            dve.wait_ge(sums, n + (3 + layer * NCH))
                            dve.wait_ge(stored, (n + (1 + layer * NCH)) * 16)
                            dve.tensor_tensor(res[b][:], ps[0:2, b, :], bias[b][:], ALU.add).then_inc(added, 1)

            @block.tensor
            def _(pe):
                pe.sem_inc(sums, 2)
                pe.wait_ge(act_done, 1)
                for layer in range(DEPTH):
                    with pe.Fori(0, NCH // 2) as i:
                        for b in range(2):
                            n = (i * 2 + b)
                            pe.wait_ge(w_in[b], (i + 1 + layer * NCH // 2) * 32)
                            pe.wait_ge(added, n + (1 + layer * NCH))
                            for t in range(DT):
                                mm = pe.matmul(ps[0:2, b, :], act[:, t, :], wt[b][:, t, :],
                                               start=(t == 0), stop=(t == DT - 1))
                            mm.then_inc(sums, 1)



NCK = [(n, min(512, IN_W - n)) for n in range(0, IN_W, 512)]
FIRST = {"ctx": 0, "lat": CT}


def input_projection_phase(nc, net, ps, layer):
    ins = net.ins
    with phase(nc) as (sb, sem):
        w = sb("w", [P, DT, IN_W])
        ident = sb("ident", [P, P])
        gain = sb("gain", [P, D])
        G = sb("G", [P, 2, D])
        S = sb("S", [P, 2, D])
        x = sb("x", [P, D])
        h = sb("h", [P, D])
        hT = sb("hT", [P, DT, P])
        small = sb("small", [P, 4])
        minus_half = sb("minus_half", [P, 1])
        po = sb("po", [P, IN_W])
        const_set = sem("const_set")
        c_in, x_in, x_used = sem("c_in"), sem("x_in"), sem("x_used")
        w_in = [sem(f"w_in{c}") for c in range(len(NCK))]
        mean_done, root_done, h_done = sem("mean_done"), sem("root_done"), sem("h_done")
        hT_ps, hT_done, prod, out_done, stored = (sem(n) for n in ("hT_ps", "hT_done", "prod", "out_done", "stored"))
        with nc.Block() as block:
            @block.sync
            def _(sp):
                sp.dma_start(ident[:], ins["k_ident"]).then_inc(c_in, 16)
                sp.dma_start(gain[:], ins["g_mix"][layer].partition_broadcast(P)).then_inc(c_in, 16)
                for j in range(2):
                    m = net.mod[layer][j]
                    sp.dma_start(S[:, j, :], m[0:D].partition_broadcast(P)).then_inc(c_in, 16)
                    sp.dma_start(G[:, j, :], m[D:2 * D].partition_broadcast(P)).then_inc(c_in, 16)
                sp.sem_inc(x_used, 1)
                for seg in ("ctx", "lat"):
                    r0, n, _ = tokens_of(seg)
                    with sp.Fori(0, n) as i:
                        sp.wait_ge(x_used, i + (1 + FIRST[seg]))
                        sp.dma_start(x[:], rows(net.x, i * P + r0)).then_inc(x_in, 16)

            @block.gpsimd
            def _(pool):
                pool.memset(minus_half[:], -0.5).then_inc(const_set, 1)
                pool.wait_ge(const_set, 1)
                for seg in ("ctx", "lat"):
                    with pool.Fori(0, tokens_of(seg)[1]) as i:
                        pool.wait_ge(mean_done, i + (1 + FIRST[seg]))
                        pool.tensor_tensor(small[:, 3:4], small[:, 1:2], minus_half[:], ALU.pow).then_inc(root_done, 1)

            @block.scalar
            def _(act):
                act.wait_ge(c_in, 16 * 6)
                src = ins["w_in"][layer].rearrange("(t p) n -> p t n", p=P)
                for c, (c0, cn) in enumerate(NCK):
                    act.dma_start(w[:, :, c0:c0 + cn], src[:, :, c0:c0 + cn]).then_inc(w_in[c], 16)
                act.sem_inc(out_done, 6)
                act.sem_inc(stored, 16)
                for seg in ("ctx", "lat"):
                    _, n, pr = tokens_of(seg)
                    with act.Fori(0, n) as i:
                        k = i + (1 + FIRST[seg])
                        act.wait_ge(hT_ps, k * 2 + 2)
                        act.wait_ge(prod, (k - 1) * len(NCK) + 1)
                        act.activation(hT[:, 4:8, :], ps[:, 1, :].rearrange("p (t n) -> p t n", n=P),
                                       ACT.Copy).then_inc(hT_done, 1)
                        act.wait_ge(stored, k * 16)
                        for c, (c0, cn) in enumerate(NCK):
                            act.wait_ge(prod, (k - 1) * len(NCK) + (c + 2))
                            act.activation(po[:, c0:c0 + cn], ps[:, 2 + c % 6, 0:cn], ACT.Copy).then_inc(out_done, 1)
                        act.wait_ge(out_done, k * len(NCK) + 6)
                        act.dma_start(rows(net.p, i * P + pr), po[:]).then_inc(stored, 16)
                act.wait_ge(stored, 16 * (NT + 1))

            @block.vector
            def _(dve):
                dve.wait_ge(c_in, 16 * 6)
                for j in range(2):
                    dve.scalar_tensor_tensor(G[:, j, :], G[:, j, :], 1.0, gain[:], ALU.add, ALU.mult)
                dve.sem_inc(hT_ps, 2)
                dve.drain()
                for seg in ("ctx", "lat"):
                    _, n, _ = tokens_of(seg)
                    j = 1 if seg == "ctx" else 0
                    with dve.Fori(0, n) as i:
                        k = i + (1 + FIRST[seg])
                        dve.wait_ge(x_in, k * 16)
                        dve.wait_ge(hT_ps, (k - 1) * 2 + 2)
                        dve.scalar_tensor_tensor(h[:], x[:], 1.0, x[:], ALU.mult, ALU.mult, accum_out=small[:, 0:1])
                        dve.drain()
                        dve.tensor_scalar(small[:, 1:2], small[:, 0:1], 1.0 / D, EPS, ALU.mult, ALU.add
                                          ).then_inc(mean_done, 1)
                        dve.wait_ge(root_done, k)
                        dve.scalar_tensor_tensor(h[:], x[:], small[:, 3:4], G[:, j, :], ALU.mult, ALU.mult
                                                 ).then_inc(x_used, 1)
                        dve.drain()
                        dve.tensor_tensor(h[:], h[:], S[:, j, :], ALU.add).then_inc(h_done, 1)
                        dve.wait_ge(hT_ps, k * 2 + 1)
                        dve.wait_ge(prod, (k - 1) * len(NCK) + 1)
                        dve.tensor_copy(hT[:, 0:4, :], ps[:, 0, :].rearrange("p (t n) -> p t n", n=P)
                                        ).then_inc(hT_done, 1)

            @block.tensor
            def _(pe):
                pe.sem_inc(prod, 1)
                pe.wait_ge(c_in, 16 * 6)
                for seg in ("ctx", "lat"):
                    _, n, _ = tokens_of(seg)
                    with pe.Fori(0, n) as i:
                        k = i + (1 + FIRST[seg])
                        pe.wait_ge(h_done, k)
                        for t in range(DT):
                            tr = pe.transpose(ps[:, t // 4, (t % 4) * P:(t % 4 + 1) * P],
                                              h[:, t * P:(t + 1) * P], ident[:])
                            if t % 4 == 3:
                                tr.then_inc(hT_ps, 1)
                        pe.wait_ge(hT_done, k * 2)
                        for c, (c0, cn) in enumerate(NCK):
                            pe.wait_ge(w_in[c], 16)
                            pe.wait_ge(out_done, (k - 1) * len(NCK) + (c + 1))
                            for t in range(DT):
                                mm = pe.matmul(ps[:, 2 + c % 6, 0:cn], hT[:, t, :], w[:, t, c0:c0 + cn],
                                               start=(t == 0), stop=(t == DT - 1))
                            mm.then_inc(prod, 1)



QK_W = A_Q + A_KV + 2 * B_Q
QB = QK_W // P
MAPS = 12
HEADS = 8
ORDER = [m for j in range(4) for m in (j, 4 + 2 * j, 5 + 2 * j)]
PLACE = [ORDER.index(m) for m in range(MAPS)]
HEAD_ORDER = [0, 4, 1, 5, 2, 6, 3, 7]
TURN = [HEAD_ORDER.index(h) for h in range(HEADS)]


def map_operands(m):
    return m, 2 if m < 4 else 5 + (m - 4) // 4


def attention_phase(nc, net, ps, layer):
    ins = net.ins
    lam_init = 0.8 - 0.6 * float(np.exp(-0.3 * layer))
    parts = [("ctx", CT)] * (layer < DEPTH - 1) + [("lat", NT)]
    tiles_before = {"ctx": 0, "lat": CT if layer < DEPTH - 1 else 0}
    n_tiles = tiles_before["lat"] + LT
    chunks_before = {"ctx": 0, "lat": tiles_before["lat"] * HEADS}
    with phase(nc) as (sb, sem):
        ident = sb("ident", [P, P])
        QKT = sb("QKT", [P, QB, TOK])
        V = sb("V", [P, NT, A_KV + B_V])
        gains = sb("gains", [P, 6, HD])
        sub_gain = sb("sub_gain", [P, 4, HD])
        lam_in = sb("lam_in", [P, 4, 32])
        lam_pr = sb("lam_pr", [P, 2, 32])
        lam_s = sb("lam_s", [P, 4])
        neg_lam = sb("neg_lam", [P, 1])
        qks = [sb(f"qk{b}", [P, QK_W]) for b in range(2)]
        ropes = [sb(f"rope{b}", [P, 2, ROPE_W]) for b in range(2)]
        turned = sb("turned", [P, QK_W])
        qkr = sb("qkr", [P, QK_W])
        small = sb("small", [P, 3, 6])
        qs = [sb(f"qs{n}", [P, MAPS, P]) for n in range(2)]
        p_a, p_b1 = sb("p_a", [P, TOK]), sb("p_b1", [P, TOK])
        p_b0 = [sb(f"p_b0_{n}", [P, TOK]) for n in range(2)]
        weights = lambda h: p_a if h < 4 else p_b0[h % 2]
        pT = [sb(f"pT{s}", [P, TOK]) for s in range(2)]
        mx = sb("mx", [P, MAPS])
        nm = sb("nm", [P, MAPS])
        sums = sb("sums", [P, 2, MAPS])
        cs = sb("cs", [P, 3, 4])
        rs = sb("rs", [P, HEADS])
        yo = sb("yo", [P, HEADS * HD])
        ysq = sb("ysq", [P, 4 * HD])
        yst = sb("yst", [P, 3, 4])
        minus_half = sb("minus_half", [P, 6])
        c_in, v_in, lam_ready, lam_exp = sem("c_in"), sem("v_in"), sem("lam_ready"), sem("lam_exp")
        qk_in = [sem(f"qk_in{b}") for b in range(2)]
        qk_used, mean_done, root_done, qkr_a_done, qkr_b_done, b_step, qkr_ps, qkt_done = (
            sem(n) for n in ("qk_used", "mean_done", "root_done", "qkr_a_done", "qkr_b_done", "b_step", "qkr_ps",
                             "qkt_done"))
        qs_clear, pool_step = sem("qs_clear"), sem("pool_step")
        zero = sb("zero", [P, D])
        zero_set, ye_clear = sem("zero_set"), sem("ye_clear")
        qs_done, scores, max_done, exp_done, comb_done = (
            sem(n) for n in ("qs_done", "scores", "max_done", "exp_done", "comb_done"))
        chunk_ps, pT_done, pv_done, o_used = sem("chunk_ps"), sem("pT_done"), sem("pv_done"), sem("o_used")
        y_mean, y_root, y_done, stored = sem("y_mean"), sem("y_root"), sem("y_done"), sem("stored")
        SCORE = [ps[:, 3 * s:3 * s + 3, :].rearrange("p b n -> p (b n)") for s in range(2)]

        def turn_chunks(kt):
            return [(t, min(4, kt - t)) for t in range(0, kt, 4)]
        O = ps[:, 7, :]

        def tiles(eng, n, tile):
            tile(0, 0, True, False)
            if n == 2:
                return tile(1, 1, False, True)
            with eng.Fori(0, (n - 2) // 2) as q:
                for o in (1, 2):
                    tile(q * 2 + o, o % 2, False, False)
            tile(n - 1, 1, False, True)
        with nc.Block() as block:
            @block.sync
            def _(sp):
                sp.dma_start(ident[:], ins["k_ident"]).then_inc(c_in, 16)
                for g, (src, n) in enumerate((("a_q_gain", 4), ("a_k_gain", 2))):
                    for h in range(n):
                        sp.dma_start(gains[:, 4 * g + h, :], ins[src][layer].partition_broadcast(P)
                                     ).then_inc(c_in, 16)
                for j, src in enumerate(("b_lq1", "b_lq2", "b_lk1", "b_lk2")):
                    sp.dma_start(lam_in[:, j, :], ins[src][layer].partition_broadcast(P)).then_inc(c_in, 16)
                for j in range(4):
                    sp.dma_start(sub_gain[:, j, :], ins["b_subln"][layer].partition_broadcast(P)
                                 ).then_inc(c_in, 16)
                sp.sem_inc(qk_used, 2)
                for seg in ("ctx", "lat"):
                    _, n, pr = tokens_of(seg)
                    with sp.Fori(0, n // 2) as q:
                        for b in range(2):
                            sp.wait_ge(qk_used, q * 2 + (b + 1 + FIRST[seg]))
                            src = rows(net.p, q * (2 * P) + (b * P + pr))
                            sp.dma_start(qks[b][:, 0:384], src[:, 0:384]).then_inc(qk_in[b], 16)
                            sp.dma_start(qks[b][:, 384:QK_W], src[:, 512:1024]).then_inc(qk_in[b], 16)
                            table = ins["k_rope"].rearrange("t (j w) -> t j w", j=2)
                            sp.dma_start(ropes[b][:], table[ds(q * (2 * P) + b * P, P), :, :]).then_inc(qk_in[b], 16)
                sp.sem_inc(stored, 16)
                for seg, _ in parts:
                    r0, n, _ = tokens_of(seg)
                    with sp.Fori(0, n) as i:
                        k = i + (1 + tiles_before[seg])
                        sp.wait_ge(y_done, k)
                        sp.dma_start(rows(net.y, i * P + r0)[:, 0:512], yo[:]).then_inc(stored, 16)
                sp.wait_ge(stored, (n_tiles + 1) * 16)

            @block.gpsimd
            def _(pool):
                for seg in ("ctx", "lat"):
                    _, n, pr = tokens_of(seg)
                    src = net.p[pr:pr + n * P, :].rearrange("(t p) n -> p t n", p=P)
                    t0 = FIRST[seg]
                    pool.dma_start(V[:, t0:t0 + n, 0:A_KV], src[:, :, 384:512]).then_inc(v_in, 16)
                    pool.dma_start(V[:, t0:t0 + n, A_KV:], src[:, :, 1024:1280]).then_inc(v_in, 16)
                pool.memset(minus_half[:], -0.5).then_inc(qs_clear, 1)
                pool.wait_ge(qs_clear, 1)
                for seg in ("ctx", "lat"):
                    with pool.Fori(0, tokens_of(seg)[1] // 2) as q:
                        for b in range(2):
                            k = q * 2 + (b + 1 + FIRST[seg])
                            qk, rope, B = qks[b], ropes[b], slice(384, QK_W)
                            pool.wait_ge(mean_done, k)
                            pool.sem_inc(pool_step, 1)
                            pool.tensor_tensor(small[:, 2, :], small[:, 1, :], minus_half[:], ALU.pow
                                               ).then_inc(root_done, 1)
                            pool.wait_ge(root_done, k)
                            if seg == "ctx":
                                pool.wait_ge(qkr_ps, (k - 1) * 2 + 1)
                                pool.sem_inc(pool_step, 1)
                                pool.tensor_copy(qkr[:, A_Q + A_KV:], qk[:, B]).then_inc(qkr_b_done, 1)
                                continue
                            x4 = qk[:, B].rearrange("p (b j q) -> p b j q", j=2, q=8)
                            t4 = turned[:, B].rearrange("p (b j q) -> p b j q", j=2, q=8)
                            s4 = rope[:, 1, B].rearrange("p (b j q) -> p b j q", j=2, q=8)
                            n0 = (k - (1 + CT)) * 3
                            for j in range(2):
                                pool.tensor_tensor(t4[:, :, j, :], x4[:, :, 1 - j, :], s4[:, :, j, :], ALU.mult
                                                   ).then_inc(b_step, 1)
                                pool.wait_ge(b_step, n0 + (j + 1))
                            pool.tensor_tensor(qk[:, B], qk[:, B], rope[:, 0, B], ALU.mult).then_inc(b_step, 1)
                            pool.wait_ge(b_step, n0 + 3)
                            pool.wait_ge(qkr_ps, (k - 1) * 2 + 1)
                            pool.sem_inc(pool_step, 1)
                            pool.tensor_tensor(qkr[:, A_Q + A_KV:], qk[:, B], turned[:, B], ALU.add
                                               ).then_inc(qkr_b_done, 1)
                for q in qs:
                    pool.memset(q[:], 0.0).then_inc(qs_clear, 1)
                pool.wait_ge(qs_clear, 3)
                pool.wait_ge(qkt_done, 2 * NT + 2)
                if layer == 0:
                    pool.memset(zero[:], 0.0).then_inc(zero_set, 1)
                    pool.wait_ge(zero_set, 1)
                    pool.dma_start(net.ye[NE * P:].rearrange("(b p) n -> p b n", p=P),
                                   zero[:].unsqueeze(1).broadcast_to([P, OVER, D])).then_inc(ye_clear, 16)
                for seg, kt in parts:
                    r0, n, _ = tokens_of(seg)

                    def queries(i, par):
                        k = i + (1 + tiles_before[seg])
                        if not isinstance(i, int) or i >= 2:
                            pool.wait_ge(scores, (k - 2) * MAPS + 1)
                        else:
                            pool.wait_ge(scores, tiles_before[seg] * MAPS + 1)
                        if not isinstance(k, int) or k > 1:
                            pool.wait_ge(qs_done, (k - 1) * 6)
                        pool.sem_inc(pool_step, 1)
                        for kv in range(2):
                            r = slice(64 * kv, 64 * kv + 64)
                            pool.tensor_copy(qs[par][r, 2 * kv:2 * kv + 2, :], QKT[r, 0:2, ds(i * P + r0, P)]
                                             ).then_inc(qs_done, 1)
                        pool.wait_ge(qs_done, (k - 1) * 6 + 2)
                        pool.sem_inc(pool_step, 1)
                        for b in range(4):
                            r = slice(32 * b, 32 * b + 32)
                            pool.tensor_copy(qs[par][r, 4 + b:MAPS:4, :], QKT[r, 3:5, ds(i * P + r0, P)]
                                             ).then_inc(qs_done, 1)

                    def root(k):
                        pool.wait_ge(y_mean, k)
                        pool.sem_inc(pool_step, 1)
                        pool.tensor_tensor(yst[:, 2, :], yst[:, 1, :], minus_half[:, 0:4], ALU.pow).then_inc(y_root, 1)

                    def tile(i, par, first, last):
                        k = i + (1 + tiles_before[seg])
                        if first:
                            queries(i, par)
                        else:
                            pool.wait_ge(qs_done, k * 6)
                            root(k - 1)
                            pool.wait_ge(y_root, k - 1)
                        if last:
                            root(k)
                            pool.wait_ge(y_root, k)
                        else:
                            queries(i + 1, 1 - par)

                    tiles(pool, n, tile)
                if layer == 0:
                    pool.wait_ge(ye_clear, 16)

            @block.scalar
            def _(act):
                act.wait_ge(lam_ready, 1)
                act.activation(lam_s[:, 2:4], lam_s[:, 0:2], ACT.Exp).then_inc(lam_exp, 1)
                for seg in ("ctx", "lat"):
                    with act.Fori(0, tokens_of(seg)[1]) as i:
                        k = i + (1 + FIRST[seg])
                        for half, (t0, n) in enumerate(((0, 4), (4, 3))):
                            act.wait_ge(qkr_ps, k * 2 + half)
                            act.activation(QKT[:, t0:t0 + n, ds(i * P + FIRST[seg] * P, P)],
                                           ps[:, half, 0:n * P].rearrange("p (t n) -> p t n", n=P),
                                           ACT.Copy).then_inc(qkt_done, 1)

                act.sem_inc(pT_done, 1)
                for seg, kt in parts:
                    nk = kt * P
                    chunks = turn_chunks(kt)
                    per_tile, k0, base = HEADS * len(chunks), tiles_before[seg], chunks_before[seg]

                    def exp(k, m, par, first):
                        act.wait_ge(max_done, (k - 1) * MAPS + (PLACE[m] + 1))
                        if m % 2 == 0 or m < 4:
                            if m in (0, 4):
                                turned = 0 if first else (TURN[3] if m == 0 else TURN[6]) + 1 - HEADS
                            elif m < 4:
                                turned = TURN[m - 1] + 1
                            else:
                                turned = TURN[2 + m // 2 - 2] + 1 if m >= 8 else 0
                            act.wait_ge(chunk_ps, (k - k0 - 1) * per_tile + (base + turned * len(chunks) + 1))
                            dst = p_a if m < 4 else p_b0[(m // 2) % 2]
                        else:
                            act.wait_ge(comb_done, (k - 1) * 4 + ((m - 5) // 2 + 1))
                            dst = p_b1
                        scale = (HD if m < 4 else 32) ** -0.5
                        act.activation(dst[:, 0:nk], SCORE[PLACE[m] % 2][:, 0:nk], ACT.Exp, bias=nm[:, m:m + 1],
                                       scale=scale, accum_out=sums[:, par, m:m + 1]).then_inc(exp_done, 1)

                    def take(k, h):
                        act.wait_ge(pv_done, (k - 1) * HEADS + (TURN[h] + 1))
                        for c, (t, n) in enumerate(chunks):
                            at = TURN[h] * len(chunks) + c
                            act.wait_ge(chunk_ps, (k - k0 - 1) * per_tile + (base + at + 2))
                            act.activation(pT[h // 4][:, t * P:(t + n) * P], ps[:, 6, 0:n * P],
                                           ACT.Copy).then_inc(pT_done, 1)

                    def tile(i, par, first, last):
                        k = i + (1 + tiles_before[seg])
                        if first:
                            exp(k, 0, par, first)
                            exp(k, 4, par, first)
                        for j in range(4):
                            if j > 0:
                                exp(k, 4 + 2 * j, par, first)
                                take(k, 3 + j)
                            exp(k, 5 + 2 * j, par, first)
                            take(k, j)
                            if j < 3:
                                exp(k, j + 1, par, first)
                        if not last:
                            exp(k + 1, 0, 1 - par, False)
                            exp(k + 1, 4, 1 - par, False)
                        take(k, 7)

                    tiles(act, tokens_of(seg)[1], tile)

            @block.vector
            def _(dve):
                dve.sem_inc(comb_done, 1)
                dve.wait_ge(c_in, 16 * 15)
                dve.tensor_tensor(lam_pr[:], lam_in[:, 0:2, :], lam_in[:, 2:4, :], ALU.mult)
                dve.drain()
                dve.tensor_reduce(lam_s[:, 0:2], lam_pr[:], AX.X, ALU.add).then_inc(lam_ready, 1)
                dve.tensor_scalar(sub_gain[:], sub_gain[:], 1.0 - lam_init, None, ALU.mult)
                dve.wait_ge(lam_exp, 1)
                dve.scalar_tensor_tensor(neg_lam[:], lam_s[:, 3:4], -lam_init, lam_s[:, 2:3],
                                         ALU.add, ALU.subtract)
                for seg in ("ctx", "lat"):
                    with dve.Fori(0, tokens_of(seg)[1] // 2) as q:
                        for b in range(2):
                            k = q * 2 + (b + 1 + FIRST[seg])
                            qk, rope, A = qks[b], ropes[b], slice(0, 384)
                            dve.wait_ge(qk_in[b], (q + (1 + FIRST[seg] // 2)) * 48)
                            dve.tensor_tensor(turned[:, A], qk[:, A], qk[:, A], ALU.mult)
                            dve.drain()
                            dve.tensor_reduce(small[:, 0, :], turned[:, A].rearrange("p (h d) -> p h d", d=HD),
                                              AX.X, ALU.add)
                            dve.drain()
                            dve.tensor_scalar(small[:, 1, :], small[:, 0, :], 1.0 / HD, EPS, ALU.mult, ALU.add
                                              ).then_inc(mean_done, 1)
                            heads = qk[:, A].rearrange("p (h d) -> p h d", d=HD)
                            dve.tensor_tensor(heads, heads, gains[:], ALU.mult)
                            dve.drain()
                            dve.wait_ge(root_done, k)
                            dve.tensor_tensor(heads, heads, small[:, 2, :].unsqueeze(2).broadcast_to([P, 6, HD]),
                                              ALU.mult)
                            dve.drain()
                            if seg == "lat":
                                x4 = qk[:, A].rearrange("p (b j q) -> p b j q", j=2, q=16)
                                t4 = turned[:, A].rearrange("p (b j q) -> p b j q", j=2, q=16)
                                s4 = rope[:, 1, A].rearrange("p (b j q) -> p b j q", j=2, q=16)
                                for j in range(2):
                                    dve.tensor_tensor(t4[:, :, j, :], x4[:, :, 1 - j, :], s4[:, :, j, :], ALU.mult)
                                dve.drain()
                                dve.tensor_tensor(qk[:, A], qk[:, A], rope[:, 0, A], ALU.mult)
                                dve.drain()
                                dve.tensor_tensor(qk[:, A], qk[:, A], turned[:, A], ALU.add)
                                dve.drain()
                            dve.wait_ge(qkr_ps, (k - 1) * 2 + 1)
                            dve.tensor_copy(qkr[:, 0:A_Q].rearrange("p (g k d) -> p k g d", g=2, k=2),
                                            qk[:, 0:A_Q].rearrange("p (k g d) -> p k g d", g=2, k=2)
                                            ).then_inc(qkr_a_done, 1)
                            dve.tensor_copy(qkr[:, A_Q:A_Q + A_KV], qk[:, A_Q:A_Q + A_KV]).then_inc(qkr_a_done, 1)
                            dve.wait_ge(qkr_a_done, k * 2)
                            dve.wait_ge(qkr_b_done, k)
                            dve.sem_inc(qk_used, 1)

                dve.sem_inc(o_used, 1)
                for seg, kt in parts:
                    nk = kt * P
                    chunks = turn_chunks(kt)
                    per_tile, k0, base = HEADS * len(chunks), tiles_before[seg], chunks_before[seg]

                    def find_max(k, m):
                        scale = (HD if m < 4 else 32) ** -0.5
                        dve.wait_ge(scores, (k - 1) * MAPS + (PLACE[m] + 1) + 1)
                        dve.tensor_reduce(mx[:, m:m + 1], SCORE[PLACE[m] % 2][:, 0:nk], AX.X, ALU.max)
                        dve.drain()
                        dve.tensor_scalar(nm[:, m:m + 1], mx[:, m:m + 1], -scale, None, ALU.mult
                                          ).then_inc(max_done, 1)

                    def combine(k, j, par):
                        m = 4 + 2 * j
                        dve.wait_ge(exp_done, (k - 1) * MAPS + (PLACE[m + 1] + 3))
                        dve.reciprocal(cs[:, 0, j:j + 1], sums[:, par, m + 1:m + 2])
                        dve.drain()
                        dve.scalar_tensor_tensor(cs[:, 2, j:j + 1], cs[:, 0, j:j + 1], sums[:, par, m:m + 1],
                                                 neg_lam[:], ALU.mult, ALU.mult)
                        dve.drain()
                        dve.scalar_tensor_tensor(p_b0[j % 2][:, 0:nk], p_b1[:, 0:nk], cs[:, 2, j:j + 1],
                                                 p_b0[j % 2][:, 0:nk], ALU.mult, ALU.add).then_inc(comb_done, 1)

                    o3 = yo[:].rearrange("p (h d) -> p h d", d=HD)

                    def divide(k, par):
                        dve.reciprocal(rs[:, 0:4], sums[:, par, 0:4])
                        dve.reciprocal(rs[:, 4:8], sums[:, par, 4:12:2])
                        dve.drain()
                        dve.wait_ge(pv_done, k * HEADS + 2)
                        dve.wait_ge(stored, k * 16)
                        dve.tensor_tensor(o3, O.rearrange("p (h d) -> p h d", d=HD),
                                          rs[:].unsqueeze(2).broadcast_to([P, HEADS, HD]), ALU.mult).then_inc(o_used, 1)
                        dve.drain()
                        yb = yo[:, 256:512]
                        dve.tensor_tensor(ysq[:], yb, yb, ALU.mult)
                        dve.drain()
                        dve.tensor_reduce(yst[:, 0, :], ysq[:].rearrange("p (h d) -> p h d", d=HD), AX.X, ALU.add)
                        dve.drain()
                        dve.tensor_scalar(yst[:, 1, :], yst[:, 0, :], 1.0 / HD, EPS, ALU.mult, ALU.add
                                          ).then_inc(y_mean, 1)

                    def normalise(k):
                        dve.wait_ge(y_root, k)
                        dve.tensor_tensor(o3[:, 4:8, :], o3[:, 4:8, :],
                                          yst[:, 2, :].unsqueeze(2).broadcast_to([P, 4, HD]), ALU.mult)
                        dve.drain()
                        dve.tensor_tensor(o3[:, 4:8, :], o3[:, 4:8, :], sub_gain[:], ALU.mult).then_inc(y_done, 1)

                    def tile(i, par, first, last):
                        k = i + (1 + tiles_before[seg])
                        if first:
                            find_max(k, 0)
                            find_max(k, 4)
                        for j in range(4):
                            if j > 0:
                                find_max(k, 4 + 2 * j)
                            find_max(k, 5 + 2 * j)
                            if j == 0 and not first:
                                divide(k - 1, 1 - par)
                            if j < 3:
                                find_max(k, j + 1)
                            elif not last:
                                find_max(k + 1, 0)
                            if j == 0 and not first:
                                normalise(k - 1)
                            combine(k, j, par)
                        if last:
                            divide(k, par)
                            normalise(k)
                        else:
                            find_max(k + 1, 4)

                    tiles(dve, tokens_of(seg)[1], tile)

            @block.tensor
            def _(pe):
                pe.wait_ge(c_in, 16 * 15)
                pe.sem_inc(qkt_done, 2)
                pe.sem_inc(qkr_ps, 1)
                for seg in ("ctx", "lat"):
                    with pe.Fori(0, tokens_of(seg)[1]) as i:
                        k = i + (1 + FIRST[seg])
                        pe.wait_ge(qkr_a_done, k * 2)
                        pe.wait_ge(qkr_b_done, k)
                        pe.wait_ge(qkt_done, k * 2)
                        for t in range(QB):
                            tr = pe.transpose(ps[:, t // 4, (t % 4) * P:(t % 4 + 1) * P],
                                              qkr[:, t * P:(t + 1) * P], ident[:])
                            if t in (3, QB - 1):
                                tr.then_inc(qkr_ps, 1)

                pe.sem_inc(scores, 1)
                pe.sem_inc(chunk_ps, 1)
                pe.sem_inc(exp_done, 2)
                pe.sem_inc(pv_done, 2)
                pe.wait_ge(v_in, 64)
                pe.wait_ge(qkt_done, 2 * NT + 2)
                for seg, kt in parts:
                    nk = kt * P
                    chunks = turn_chunks(kt)
                    per_tile, k0, base = HEADS * len(chunks), tiles_before[seg], chunks_before[seg]

                    def turn_chunk(k, h, c):
                        t0, n = chunks[c]
                        at = TURN[h] * len(chunks) + c
                        pe.wait_ge(pT_done, (k - k0 - 1) * per_tile + (base + at + 1))
                        for t in range(n):
                            tr = pe.transpose(ps[:, 6, t * P:(t + 1) * P],
                                              weights(h)[:, (t0 + t) * P:(t0 + t + 1) * P], ident[:])
                        tr.then_inc(chunk_ps, 1)

                    def work(m=None, h=None, q=None):
                        if m is not None:
                            k, mp = m
                            pe.wait_ge(exp_done, (k - 1) * MAPS + (PLACE[mp] + 1))
                            slot, kb = map_operands(mp)
                        if h is not None:
                            kh, hd = h
                            if hd < 4:
                                pe.wait_ge(exp_done, (kh - 1) * MAPS + (PLACE[hd] + 3))
                            else:
                                pe.wait_ge(comb_done, (kh - 1) * 4 + (hd - 4 + 2))
                        for n, c in enumerate(range(0, nk, 512)):
                            if h is not None:
                                turn_chunk(kh, hd, n)
                            if m is not None:
                                w = min(512, nk - c)
                                mm = pe.matmul(SCORE[PLACE[mp] % 2][:, c:c + w], q[:, slot, :],
                                               QKT[:, kb, c:c + w], start=True, stop=True)
                        if m is not None:
                            mm.then_inc(scores, 1)

                    def weigh(k, h):
                        pe.wait_ge(pT_done, (k - k0 - 1) * per_tile + (base + (TURN[h] + 1) * len(chunks) + 1))
                        v0 = HD * (h // 2) if h < 4 else A_KV + HD * (h - 4)
                        for t in range(kt):
                            mm = pe.matmul(O[:, h * HD:(h + 1) * HD], pT[h // 4][:, t * P:(t + 1) * P],
                                           V[:, t, v0:v0 + HD], start=(t == 0), stop=(t == kt - 1))
                        mm.then_inc(pv_done, 1)

                    def tile(i, par, first, last):
                        k = i + (1 + tiles_before[seg])
                        q = qs[par]
                        if first:
                            pe.wait_ge(qs_done, k * 6)
                            work(m=(k, 0), q=q)
                            work(m=(k, 4), q=q)
                            work(m=(k, 5), q=q)
                        else:
                            work(m=(k, 5), h=(k - 1, 7), q=q)
                            weigh(k - 1, 7)
                        for j in range(4):
                            if j > 0:
                                work(m=(k, 4 + 2 * j), q=q)
                                work(m=(k, 5 + 2 * j), h=(k, 3 + j), q=q)
                                weigh(k, 3 + j)
                            if j < 3:
                                work(m=(k, j + 1), h=(k, j), q=q)
                            elif last:
                                work(h=(k, 3))
                            else:
                                pe.wait_ge(qs_done, k * 6 + 6)
                                work(m=(k + 1, 0), h=(k, 3), q=qs[1 - par])
                            if j == 0:
                                pe.wait_ge(o_used, k)
                            weigh(k, j)
                        if last:
                            work(h=(k, 7))
                            weigh(k, 7)
                        else:
                            work(m=(k + 1, 4), q=qs[1 - par])

                    tiles(pe, tokens_of(seg)[1], tile)


SCAN_R, SCAN_V, SCAN_A, SCAN_B, SCAN_K, SCAN_L = 0, CW, 2 * CW, 3 * CW, 5 * CW, 7 * CW
DECAY = float(np.exp(np.float32(-0.5)))


def heads_of(ap, n=CH):
    return ap.rearrange("p (h d) -> p h d", d=HD)


def rwkv_input_phase(nc, net, ps, layer):
    ins = net.ins
    QW = CS // 4
    NCON = 9
    with phase(nc) as (sb, sem):
        ident = sb("ident", [P, P])
        shift, around = sb("shift", [P, P]), sb("around", [P, P])
        minus_half = sb("minus_half", [P, CH])
        mu = sb("mu", [P, CS])
        w2, a2 = sb("w2", [P, CW]), sb("a2", [P, CW])
        g2 = sb("g2", [P, CW])
        w0, a0 = sb("w0", [P, NZ, CW]), sb("a0", [P, NZ, CW])
        kk_g, ka_g, rk_g = sb("kk_g", [P, CW]), sb("ka_g", [P, CW]), sb("rk_g", [P, CW])
        cur, halo = sb("cur", [P, CS]), sb("halo", [P, CS])
        mix = sb("mix", [P, CS])
        pfs = sb("pfs", [P, 2, CS])
        lt = sb("lt", [P, 3, P])
        pre = sb("pre", [P, 4, CW])
        kks, sq, kka, rr, kd_sum, rks = (sb(n, [P, CW]) for n in ("kks", "sq", "kka", "rr", "kd_sum", "rks"))
        a_out = sb("a_out", [P, CW])
        b_out, k_out, l_out = sb("b_out", [P, NZ, CW]), sb("k_out", [P, NZ, CW]), sb("l_out", [P, NZ, CW])
        gbs = sb("gbs", [P, 2, 2, CW])
        st = sb("st", [P, 4, CH])
        c_in, half_set, t_in, t_used, shifted, pf_done, lt_ps, lt_done = (
            sem(n) for n in ("c_in", "half_set", "t_in", "t_used", "shifted", "pf_done", "lt_ps", "lt_done"))
        proj, g_ps, g_done, pre_done, sig_done, l_done, ss_done, root_done = (
            sem(n) for n in ("proj", "g_ps", "g_done", "pre_done", "sig_done", "l_done", "ss_done", "root_done"))
        kka_done, kd_done, kd_sum_done, rks_done, bonus_done, outs_stored, c_first, halo_set, pool_step = (
            sem(n) for n in ("kka_done", "kd_done", "kd_sum_done", "rks_done", "bonus_done", "outs_stored",
                              "c_first", "halo_set", "pool_step"))
        rv_stored = [sem("rv_stored%d" % j) for j in range(2)]
        gb_stored = [sem("gb_stored%d" % j) for j in range(2)]
        bc = lambda name: ins[name][layer].partition_broadcast(P)
        R, K, V = (lambda par, c=c: pfs[:, par, c * CW:(c + 1) * CW] for c in range(3))

        def steps(eng, step):
            def peeled(i):
                step(i, lambda d: 0 <= i + d < NT, lambda d: (i + d) % 2, lambda d: (i + d) // 2)
            peeled(-1)
            peeled(0)
            with eng.Fori(0, (NT - 2) // 2) as q:
                for o in (1, 2):
                    step(q * 2 + o, lambda d: True, lambda d: (o + d) % 2, lambda d: q + (o + d) // 2)
            peeled(NT - 1)
            peeled(NT)

        with nc.Block() as block:
            @block.sync
            def _(sp):
                sp.dma_start(shift[:], ins["k_shift"]).then_inc(c_first, 16)
                sp.dma_start(around[:], ins["k_around"]).then_inc(c_first, 16)
                sp.dma_start(ident[:], ins["k_ident"]).then_inc(c_first, 16)
                sp.sem_inc(t_used, 1)

                def load(t, pr):
                    sp.wait_ge(t_used, t + 1)
                    r = t * P + pr
                    sp.dma_start(cur[:], rows(net.p, r)[:, ATT:IN_W]).then_inc(t_in, 16)
                    sp.dma_start(halo[0:1, :], rows(net.p, r - 1, 1)[:, ATT:IN_W]).then_inc(t_in, 16)
                    sp.dma_start(halo[1:2, :], rows(net.p, r + P, 1)[:, ATT:IN_W]).then_inc(t_in, 16)

                sp.wait_ge(halo_set, 1)
                load(0, 1)
                sp.dma_start(mu[:], bc("c_mu")).then_inc(c_in, 16)
                sp.dma_start(w2[:], ins["c_w2"][layer].rearrange("z r c -> (z r) c")).then_inc(c_in, 16)
                sp.dma_start(a2[:], ins["c_a2"][layer].rearrange("z r c -> (z r) c")).then_inc(c_in, 16)
                sp.dma_start(g2[:], ins["c_g2"][layer]).then_inc(c_in, 16)
                sp.dma_start(w0[:], bc("c_w0")).then_inc(c_in, 16)
                sp.dma_start(a0[:], bc("c_a0")).then_inc(c_in, 16)
                sp.dma_start(kk_g[:], bc("c_k_k")).then_inc(c_in, 16)
                sp.dma_start(ka_g[:], bc("c_k_a")).then_inc(c_in, 16)
                rk = ins["c_r_k"][layer].rearrange("h d -> (h d)").partition_broadcast(P)
                sp.dma_start(rk_g[:], rk).then_inc(c_in, 16)
                for t in range(1, CT):
                    load(t, 1)
                with sp.Fori(CT, NT) as t:
                    load(t, 2)

            @block.gpsimd
            def _(pool):
                pool.memset(halo[:], 0.0).then_inc(halo_set, 1)
                pool.memset(minus_half[:], -0.5).then_inc(half_set, 1)
                pool.wait_ge(half_set, 1)
                pool.wait_ge(c_in, 16 * NCON)

                def step(i, has, par, nth):
                    k = i + 1
                    if not has(0):
                        return
                    pool.wait_ge(pf_done, k)
                    if has(-1):
                        pool.wait_ge(kd_done, k - 1)
                    pool.sem_inc(pool_step, 1)
                    pool.tensor_tensor(kka[:], K(par(0)), ka_g[:], ALU.mult).then_inc(kka_done, 1)
                    pool.wait_ge(ss_done, k)
                    pool.sem_inc(pool_step, 1)
                    pool.tensor_tensor(st[:, 2, :], st[:, 1, :], minus_half[:], ALU.pow).then_inc(root_done, 1)
                    pool.wait_ge(root_done, k)
                    pool.tensor_tensor(rr[:], R(par(0)), rk_g[:], ALU.mult).then_inc(kka_done, 1)
                    pool.wait_ge(kd_done, k)
                    pool.tensor_tensor(kd_sum[:], k_out[:, 0, :], k_out[:, 1, :], ALU.add).then_inc(kd_sum_done, 1)
                    pool.wait_ge(kd_sum_done, k)
                    pool.wait_ge(kka_done, k * 2)
                    pool.tensor_tensor(rks[:], rr[:], kd_sum[:], ALU.mult).then_inc(rks_done, 1)

                steps(pool, step)

            @block.scalar
            def _(act):
                act.sem_inc(outs_stored, 16 * 4)
                for j in range(2):
                    act.sem_inc(rv_stored[j], 16 * 2)
                    act.sem_inc(gb_stored[j], 16)

                def step(i, has, par, nth):
                    k = i + 1
                    if has(0):
                        act.wait_ge(pre_done, k)
                        act.activation(pre[:], pre[:], ACT.Sigmoid).then_inc(sig_done, 1)
                    if has(-1):
                        act.wait_ge(bonus_done, k - 1)
                        act.wait_ge(g_done, k - 1)
                        act.dma_start(rows(net.gb, (i - 1) * P), gbs[:, par(-1)].rearrange("p j c -> p (j c)")
                                      ).then_inc(gb_stored[par(-1)], 16)
                    if has(1):
                        act.wait_ge(pf_done, k + 1)
                        o = rows(net.scan, (i + 1) * P)
                        act.dma_start(o[:, SCAN_R:SCAN_R + CW], R(par(1))).then_inc(rv_stored[par(1)], 16)
                        act.dma_start(o[:, SCAN_V:SCAN_V + CW], V(par(1))).then_inc(rv_stored[par(1)], 16)
                        act.wait_ge(lt_ps, k + 1)
                        act.activation(lt[:, 0, :], ps[:, 4, 0:P], ACT.Tanh).then_inc(lt_done, 1)
                        act.activation(lt[:, 1, :], ps[:, 4, P:2 * P], ACT.Copy).then_inc(lt_done, 1)
                        act.activation(lt[:, 2, :], ps[:, 4, 2 * P:3 * P], ACT.Sigmoid).then_inc(lt_done, 1)
                    if has(0):
                        act.wait_ge(outs_stored, k * 64)
                        act.wait_ge(sig_done, k)
                        act.activation(l_out[:], pre[:, 0:2, :], ACT.Copy, scale=-DECAY).then_inc(l_done, 1)
                    if has(1):
                        act.wait_ge(g_ps, k + 1)
                        act.wait_ge(gb_stored[par(1)], (nth(1) + 1) * 16)
                        act.activation(gbs[:, par(1), 0, :], ps[:, 5, :], ACT.Copy).then_inc(g_done, 1)
                    if has(0):
                        act.wait_ge(l_done, k)
                        act.wait_ge(kd_done, k)
                        o = rows(net.scan, i * P)
                        for buf, c0, w in ((a_out[:], SCAN_A, CW),
                                           (b_out[:].rearrange("p z c -> p (z c)"), SCAN_B, 2 * CW),
                                           (k_out[:].rearrange("p z c -> p (z c)"), SCAN_K, 2 * CW),
                                           (l_out[:].rearrange("p z c -> p (z c)"), SCAN_L, 2 * CW)):
                            act.dma_start(o[:, c0:c0 + w], buf).then_inc(outs_stored, 16)

                steps(act, step)
                act.wait_ge(outs_stored, 64 * (NT + 1))
                for j in range(2):
                    act.wait_ge(rv_stored[j], 32 * (NT // 2 + 1))
                    act.wait_ge(gb_stored[j], 16 * (NT // 2 + 1))

            @block.vector
            def _(dve):
                dve.wait_ge(c_in, 16 * NCON)

                def step(i, has, par, nth):
                    k = i + 1
                    if has(0):
                        dve.wait_ge(proj, k)
                        if has(-1):
                            dve.wait_ge(l_done, k - 1)
                        dve.tensor_tensor(pre[:, 0:2, :], ps[:, 0:2, :], w0[:], ALU.add)
                        dve.tensor_tensor(pre[:, 2:4, :], ps[:, 2:4, :], a0[:], ALU.add)
                        dve.drain()
                        dve.sem_inc(pre_done, 1)
                    if has(-1):
                        dve.wait_ge(rks_done, k - 1)
                        dve.tensor_reduce(st[:, 3, :], heads_of(rks[:]), AX.X, ALU.add)
                        dve.drain()
                        dve.wait_ge(gb_stored[par(-1)], (nth(-1) + 1) * 16)
                        dve.tensor_tensor(heads_of(gbs[:, par(-1), 1, :]), heads_of(V(par(-1))),
                                          st[:, 3, :].unsqueeze(2).broadcast_to([P, CH, HD]), ALU.mult
                                          ).then_inc(bonus_done, 1)
                    if has(0):
                        dve.tensor_tensor(kks[:], K(par(0)), kk_g[:], ALU.mult)
                        dve.drain()
                        dve.tensor_tensor(sq[:], kks[:], kks[:], ALU.mult)
                        dve.drain()
                        dve.tensor_reduce(st[:, 0, :], heads_of(sq[:]), AX.X, ALU.add)
                        dve.drain()
                        dve.tensor_scalar(st[:, 1, :], st[:, 0, :], 1e-24, None, ALU.max).then_inc(ss_done, 1)
                    if has(1):
                        dve.wait_ge(shifted, k + 1)
                        dve.tensor_tensor(mix[:].rearrange("p (b n) -> p b n", b=4), ps[:, 4:8, 0:QW],
                                          mu[:].rearrange("p (b n) -> p b n", b=4), ALU.mult)
                        dve.drain()
                        dve.wait_ge(rv_stored[par(1)], (nth(1) + 1) * 32)
                        dve.tensor_tensor(pfs[:, par(1), :], cur[:], mix[:], ALU.add).then_inc(pf_done, 1)
                        dve.drain()
                        dve.sem_inc(t_used, 1)
                    if has(0):
                        dve.wait_ge(outs_stored, k * 64)
                        dve.wait_ge(root_done, k)
                        dve.scalar_tensor_tensor(heads_of(a_out[:]), heads_of(kks[:]), -1.0,
                                                 st[:, 2, :].unsqueeze(2).broadcast_to([P, CH, HD]),
                                                 ALU.mult, ALU.mult)
                        dve.wait_ge(kka_done, k * 2 - 1)
                        dve.wait_ge(sig_done, k)
                        for z in range(NZ):
                            dve.scalar_tensor_tensor(k_out[:, z, :], pre[:, 2 + z, :], 1.0, kka[:],
                                                     ALU.subtract, ALU.mult)
                        dve.drain()
                        for z in range(NZ):
                            dve.tensor_tensor(k_out[:, z, :], k_out[:, z, :], K(par(0)), ALU.add)
                            dve.scalar_tensor_tensor(b_out[:, z, :], a_out[:], -1.0, pre[:, 2 + z, :],
                                                     ALU.mult, ALU.mult)
                        dve.drain()
                        dve.sem_inc(kd_done, 1)

                steps(dve, step)

            @block.tensor
            def _(pe):
                pe.wait_ge(c_first, 16 * 3)

                def step(i, has, par, nth):
                    k = i + 1
                    if not has(1):
                        return
                    pe.wait_ge(t_in, (k + 1) * 48)
                    if has(0):
                        pe.wait_ge(lt_done, k * 3)
                        pe.wait_ge(g_done, k)
                    for b in range(4):
                        q = slice(b * QW, (b + 1) * QW)
                        pe.matmul(ps[:, 4 + b, 0:QW], shift[:], cur[:, q], start=True, stop=False)
                        mm = pe.matmul(ps[:, 4 + b, 0:QW], around[:], halo[:, q], start=False, stop=True)
                    mm.then_inc(shifted, 1)
                    pe.wait_ge(pf_done, k + 1)
                    for t in range(3):
                        tr = pe.transpose(ps[:, 4, t * P:(t + 1) * P],
                                          pfs[:, par(1), 3 * CW + t * P:3 * CW + (t + 1) * P], ident[:])
                    tr.then_inc(lt_ps, 1)
                    pe.wait_ge(c_in, 16 * NCON)
                    pe.wait_ge(lt_done, (k + 1) * 3)
                    if has(0):
                        pe.wait_ge(pre_done, k)
                    for j, w in enumerate((w2, a2)):
                        for z in range(NZ):
                            q = slice(64 * z, 64 * z + 64)
                            mm = pe.matmul(ps[:, 2 * j + z, :], lt[q, j, :], w[q, :], start=True, stop=True)
                    mm.then_inc(proj, 1)
                    pe.matmul(ps[:, 5, :], lt[:, 2, :], g2[:], start=True, stop=True).then_inc(g_ps, 1)

                steps(pe, step)


def scan_phase(nc, net, ps, layer):
    ins = net.ins
    PAIR = 2
    GR = PAIR * NZ
    TOP = LEVELS - 1
    with phase(nc) as (sb, sem):
        ident = sb("ident", [P, P])
        tri = sb("tri", [C, NZ, 2 * P])
        mask = sb("mask", [P, NZ, P])
        levels = sb("levels", [P, LEVELS, NZ, C])
        ones = sb("ones", [C, 1])
        ra, kb = sb("ra", [P, PAIR, NZ, CW]), sb("kb", [P, PAIR, NZ, CW])
        v_raw = sb("v_raw", [C, PAIR, NZ, CW])
        lw = sb("lw", [C, PAIR, NZ, CW])
        rat, kbt = sb("rat", [P, PAIR, NZ, CW]), sb("kbt", [P, PAIR, NZ, CW])
        e_end = sb("e_end", [C, PAIR, ST])
        vu = sb("vu", [P, PAIR, ST, C])
        rac, kbc = sb("rac", [C, PAIR, ST, P]), sb("kbc", [C, PAIR, ST, P])
        G = sb("G", [P, PAIR, ST, P])
        at = sb("at", [P, 2, GR, CH, C])
        T, TT, YI = (sb(n, [P, GR, CH, C]) for n in ("T", "TT", "YI"))
        X = sb("X", [P, NZ, CH, C])
        state = sb("state", [C, 2, NZ, CH, C])
        yo = sb("yo", [C, PAIR, ST, C])
        hi = slice(C, P)
        pe_step, pool_step = sem("pe_step"), sem("pool_step")
        in_sem = [sem("in_sem%d" % j) for j in range(PAIR)]
        stored = [sem("stored%d" % j) for j in range(PAIR)]
        c_in, ones_set, in_used, cums, ends, exps, end_exp, v_done, scaled = (
            sem(n) for n in ("c_in", "ones_set", "in_used", "cums", "ends", "exps", "end_exp", "v_done", "scaled"))
        turned, rac_done, kbc_done, g_ps, g_done, at_done, tt0_done = (
            sem(n) for n in ("turned", "rac_done", "kbc_done", "g_ps", "g_done", "at_done", "tt0_done"))
        t0_done, y_ps, yi_done, t_ps, t_done, tt_done, tt_ps, top_done = (
            sem(n) for n in ("t0_done", "y_ps", "yi_done", "t_ps", "t_done", "tt_done", "tt_ps", "top_done"))
        x_ps, x_done, u_ps, u_done, out_ps, out_done, s_ps, s_done = (
            sem(n) for n in ("x_ps", "x_done", "u_ps", "u_done", "out_ps", "out_done", "s_ps", "s_done"))
        nth_at = lambda l, g: 2 * g + l if l < 2 else l * GR + g
        segs = [("ctx", NC_CTX, 0, 0), ("lat", NC_LAT, CTX, NC_CTX)]
        zs = lambda z: slice(CH * z, CH * z + CH)
        stc = lambda t, j, s: t[:, j, s // CH, (s % CH) * HD:(s % CH + 1) * HD]
        two = lambda t, j, s2: t[:, j, s2 // (CH // 2), (s2 % (CH // 2)) * P:(s2 % (CH // 2) + 1) * P]
        halves = (slice(0, C), slice(C, P))
        turned_to = lambda j, kind, odd: ps[halves[odd], GR * j + 2 * kind:GR * j + 2 * kind + 2, :].rearrange(
            "p b n -> p (b n)")
        heads_in = lambda t, j, odd: t[:, j].rearrange("p (s2 odd) c -> p odd s2 c", odd=2)[:, odd]
        bank = lambda b, part: ps[part, b, :].rearrange("p (h c) -> p h c", c=C)
        eye8 = ident[hi, C:P].unsqueeze(1).broadcast_to([C, CH, C])
        row_of = lambda i, j, z, n, r0: (i * (PAIR * C) + (r0 + j * C) if z == 0
                                         else i * (-PAIR * C) + (r0 + (n - 1 - j) * C))
        with nc.Block() as block:
            @block.sync
            def _(sp):
                sp.dma_start(ident[:], ins["k_ident"]).then_inc(c_in, 16)
                sp.dma_start(tri[:].rearrange("p z n -> p (z n)"), ins["k_tri"]).then_inc(c_in, 16)
                sp.dma_start(mask[:].rearrange("p z n -> p (z n)"), ins["k_mask"]).then_inc(c_in, 16)
                sp.dma_start(levels[hi].rearrange("p l z n -> p (l z n)"), ins["k_levels"]).then_inc(c_in, 16)
                sp.sem_inc(in_used, PAIR)
                for seg, n, r0, before in segs:
                    with sp.Fori(0, n // PAIR) as i:
                        for j in range(PAIR):
                            sp.wait_ge(in_used, i * PAIR + (1 + j + before))
                            for z in range(NZ):
                                src = net.scan[ds(row_of(i, j, z, n, r0), C), :]
                                for dst, c0 in ((lw[:, j, z, :], SCAN_L + z * CW), (ra[0:C, j, z, :], SCAN_R),
                                                (ra[hi, j, z, :], SCAN_A), (kb[0:C, j, z, :], SCAN_K + z * CW),
                                                (kb[hi, j, z, :], SCAN_B + z * CW), (v_raw[:, j, z, :], SCAN_V)):
                                    sp.dma_start(dst, src[:, c0:c0 + CW]).then_inc(in_sem[j], 16)

            @block.gpsimd
            def _(pool):
                pool.memset(ones[:], 1.0).then_inc(ones_set, 1)
                pool.memset(state[:, 0], 0.0).then_inc(ones_set, 1)
                pool.wait_ge(c_in, 64)
                for seg, n, r0, before in segs:
                    with pool.Fori(0, n // PAIR) as i:
                        k = i + (1 + before // PAIR)
                        for j in range(PAIR):
                            pool.wait_ge(in_sem[j], k * 192)
                            pool.wait_ge(out_ps, (k - 1) * PAIR + (j + 1))
                            pool.sem_inc(pool_step, 1)
                            pool.tensor_copy(vu[0:C, j].rearrange("p (z h) d -> p z (h d)", z=NZ), v_raw[:, j]
                                             ).then_inc(v_done, 1)
                        for l, g in sorted(((l, g) for l in range(LEVELS) for g in range(GR)),
                                           key=lambda lg: nth_at(*lg)):
                            j, z = g // NZ, g % NZ
                            pool.wait_ge(g_done, (k - 1) * GR + (g + 1))
                            if l == 2:
                                pool.wait_ge(tt0_done, (k - 1) * GR + (g + 1))
                            elif l > 2:
                                pool.wait_ge(y_ps, (k - 1) * (TOP * GR) + ((l - 3) * GR + g + 1))
                            pool.tensor_tensor(at[hi, l % 2, g], G[hi, j, zs(z), C:P],
                                               levels[hi, l, z, :].unsqueeze(1).broadcast_to([C, CH, C]),
                                               ALU.mult).then_inc(at_done, 1)

            @block.scalar
            def _(act):
                for j in range(PAIR):
                    act.sem_inc(stored[j], 32)
                for seg, n, r0, before in segs:
                    with act.Fori(0, n // PAIR) as i:
                        k = i + (1 + before // PAIR)
                        for j in range(PAIR):
                            act.wait_ge(cums, (k - 1) * PAIR + (j + 1))
                            act.activation(rat[:, j], ps[:, GR * j:GR * j + 2, :], ACT.Exp).then_inc(exps, 1)
                            act.activation(kbt[:, j], ps[:, GR * j + 2:GR * j + 4, :], ACT.Exp).then_inc(exps, 1)
                        for j in range(PAIR):
                            act.wait_ge(turned, (k - 1) * 4 + (2 * j + 1))
                            for odd in range(2):
                                act.activation(heads_in(rac, j, odd), turned_to(j, 0, odd).rearrange(
                                    "p (s c) -> p s c", c=P), ACT.Copy).then_inc(rac_done, 1)
                            if j == 0:
                                act.wait_ge(ends, k)
                                act.wait_ge(s_done, (k - 1) * 4 + 2)
                                for odd in range(2):
                                    act.activation(e_end[:].rearrange("p j (s2 odd) -> p odd (j s2)", odd=2)[:, odd],
                                                   ps[halves[odd], 6, 0:PAIR * ST // 2], ACT.Exp
                                                   ).then_inc(end_exp, 1)
                        for l in range(1, TOP):
                            for g in range(GR):
                                act.wait_ge(t_ps, (k - 1) * ((TOP - 1) * GR) + ((l - 1) * GR + g + 1))
                                act.activation(T[hi, g], bank(4 + g, hi), ACT.Copy).then_inc(t_done, 1)
                        for g in range(GR):
                            act.wait_ge(tt_ps, (k - 1) * GR + (g + 1))
                            act.activation(TT[hi, g], bank(4 + g, hi), ACT.Copy).then_inc(top_done, 1)
                        for j in range(PAIR):
                            for z in range(NZ):
                                act.wait_ge(x_ps, (k - 1) * 4 + (2 * j + z + 1))
                                act.activation(X[hi, z], bank(z, hi), ACT.Copy).then_inc(x_done, 1)
                            for z in range(NZ):
                                act.wait_ge(u_ps, (k - 1) * 4 + (2 * j + z + 1))
                                act.activation(vu[hi, j, zs(z), :], bank(2 + z, hi), ACT.Copy).then_inc(u_done, 1)
                            act.wait_ge(out_ps, k * PAIR + (j + 1))
                            act.wait_ge(stored[j], k * 32)
                            act.activation(yo[:, j].rearrange("p (z h) c -> p z (h c)", z=NZ), ps[0:C, 6:8, :],
                                           ACT.Copy).then_inc(out_done, 1)
                            act.wait_ge(out_done, (k - 1) * PAIR + (j + 2))
                            for z in range(NZ):
                                act.dma_start(net.yd[z][ds(row_of(i, j, z, n, r0), C), :],
                                              yo[:, j, zs(z), :].rearrange("p h c -> p (h c)")
                                              ).then_inc(stored[j], 16)
                for j in range(PAIR):
                    act.wait_ge(stored[j], 32 * ((NC_LAT + NC_CTX) // PAIR + 1))

            @block.vector
            def _(dve):
                dve.wait_ge(c_in, 64)
                dve.wait_ge(ones_set, 2)
                dve.sem_inc(s_done, 2)
                for seg, n, r0, before in segs:
                    with dve.Fori(0, n // PAIR) as i:
                        k = i + (1 + before // PAIR)
                        for j in range(PAIR):
                            dve.wait_ge(in_sem[j], k * 192)
                            dve.wait_ge(exps, (k - 1) * 4 + (2 * j + 1))
                            dve.tensor_tensor(rat[:, j], ra[:, j], rat[:, j], ALU.mult).then_inc(scaled, 1)
                            dve.wait_ge(exps, (k - 1) * 4 + (2 * j + 2))
                            dve.tensor_tensor(kbt[:, j], kb[:, j], kbt[:, j], ALU.mult).then_inc(scaled, 1)
                            dve.wait_ge(v_done, (k - 1) * PAIR + (j + 1))
                            dve.wait_ge(scaled, (k - 1) * 4 + (2 * j + 2))
                        for j in range(PAIR):
                            dve.wait_ge(turned, (k - 1) * 4 + (2 * j + 2))
                            for odd in range(2):
                                dve.tensor_copy(heads_in(kbc, j, odd), turned_to(j, 1, odd).rearrange(
                                    "p (s c) -> p s c", c=P)).then_inc(kbc_done, 1)
                        dve.wait_ge(ends, k)
                        dve.sem_inc(in_used, PAIR)
                        for g in range(GR):
                            j, z = g // NZ, g % NZ
                            dve.wait_ge(g_ps, (k - 1) * GR + (g + 1))
                            dve.tensor_tensor(G[:, j, zs(z), :],
                                              ps[:, 2 * g:2 * g + 2, :].rearrange("p b (s n) -> p (b s) n", n=P),
                                              mask[:, z, :].unsqueeze(1).broadcast_to([P, CH, P]), ALU.mult
                                              ).then_inc(g_done, 1)
                        for g in range(GR):
                            dve.wait_ge(at_done, (k - 1) * (LEVELS * GR) + (nth_at(0, g) + 1))
                            dve.tensor_tensor(TT[hi, g], at[hi, 0, g], eye8, ALU.add).then_inc(tt0_done, 1)
                            dve.wait_ge(tt0_done, (k - 1) * GR + (g + 1))
                            dve.transpose(T[hi, g], TT[hi, g]).then_inc(t0_done, 1)
                        for l in range(1, LEVELS):
                            for g in range(GR):
                                dve.wait_ge(y_ps, (k - 1) * (TOP * GR) + ((l - 1) * GR + g + 1))
                                dve.tensor_tensor(YI[hi, g], bank(g, hi), eye8, ALU.add).then_inc(yi_done, 1)
                            for g in range(GR if l < TOP else 0):
                                dve.wait_ge(t_done, (k - 1) * ((TOP - 1) * GR) + ((l - 1) * GR + g + 1))
                                dve.transpose(TT[hi, g], T[hi, g]).then_inc(tt_done, 1)
                        for j in range(PAIR):
                            for z in range(NZ):
                                dve.wait_ge(s_ps, (k - 1) * 4 + (2 * j + z + 1))
                                dve.tensor_tensor(state[:, 1 - j, z], state[:, j, z], bank(4 + z, slice(0, C)), ALU.add)
                                dve.drain()
                                dve.tensor_tensor(state[:, 1 - j, z], state[:, 1 - j, z],
                                                  e_end[:, j, zs(z)].unsqueeze(2).broadcast_to([C, CH, C]), ALU.mult
                                                  ).then_inc(s_done, 1)

            @block.tensor
            def _(pe):
                pe.wait_ge(c_in, 64)
                pe.sem_inc(out_done, 1)
                pe.sem_inc(out_ps, PAIR)
                for seg, n, r0, before in segs:
                    with pe.Fori(0, n // PAIR) as i:
                        k = i + (1 + before // PAIR)
                        pe.wait_ge(s_done, (k - 1) * 4 + 2)
                        for j in range(PAIR):
                            pe.wait_ge(in_sem[j], k * 192)
                            if j == 1:
                                pe.wait_ge(out_done, (k - 1) * PAIR + 1)
                            for b in range(4):
                                kind = b // 2
                                mm = pe.matmul(ps[:, GR * j + b, :], tri[:, b % 2, kind * P:kind * P + P],
                                               lw[:, j, b % 2, :], start=True, stop=True)
                            mm.then_inc(cums, 1)
                        for j in range(PAIR):
                            for kind, src in enumerate((rat, kbt)):
                                if j == 1 and kind == 0:
                                    pe.wait_ge(exps, k * 4)
                                    pe.sem_inc(pe_step, 1)
                                    for s2 in range(PAIR * ST // 2):
                                        mm = pe.matmul(ps[:, 6, s2:s2 + 1], two(lw, s2 // (ST // 2), s2 % (ST // 2)),
                                                       ones[:], start=True, stop=True)
                                    mm.then_inc(ends, 1)
                                elif j == 1:
                                    pe.wait_ge(end_exp, k * 2)
                                pe.wait_ge(scaled, (k - 1) * 4 + (2 * j + kind + 1))
                                pe.sem_inc(pe_step, 1)
                                for s2 in range(ST // 2):
                                    tr = pe.transpose(ps[:, GR * j + 2 * kind + s2 // 4, (s2 % 4) * P:(s2 % 4 + 1) * P],
                                                      two(src, j, s2), ident[:])
                                tr.then_inc(turned, 1)
                        for j in range(PAIR):
                            pe.wait_ge(rac_done, (k - 1) * 4 + (2 * j + 2))
                            pe.wait_ge(kbc_done, (k - 1) * 4 + (2 * j + 2))
                            pe.sem_inc(pe_step, 1)
                            for s in range(ST):
                                mm = pe.matmul(ps[:, GR * j + s // 4, (s % 4) * P:(s % 4 + 1) * P], kbc[:, j, s, :],
                                               rac[:, j, s, :], start=True, stop=True)
                                if s % CH == CH - 1:
                                    mm.then_inc(g_ps, 1)
                        for l in range(1, LEVELS):
                            for g in range(GR):
                                pe.wait_ge(at_done, (k - 1) * (LEVELS * GR) + (nth_at(l, g) + 1))
                                if l == 1:
                                    pe.wait_ge(g_done, (k - 1) * GR + (g // 2 + 1))
                                    pe.wait_ge(t0_done, (k - 1) * GR + (g + 1))
                                else:
                                    pe.wait_ge(t_done, (k - 1) * ((TOP - 1) * GR) + ((l - 2) * GR + g + 1))
                                pe.sem_inc(pe_step, 1)
                                for h in range(CH):
                                    mm = pe.matmul(bank(g, hi)[:, h, :], at[hi, l % 2, g, h, :], T[hi, g, h, :],
                                                   start=True, stop=True)
                                mm.then_inc(y_ps, 1)
                            for g in range(GR):
                                pe.wait_ge(yi_done, (k - 1) * (TOP * GR) + ((l - 1) * GR + g + 1))
                                if l == 1:
                                    pe.wait_ge(g_done, k * GR)
                                else:
                                    pe.wait_ge(tt_done, (k - 1) * ((TOP - 1) * GR) + ((l - 2) * GR + g + 1))
                                pe.sem_inc(pe_step, 1)
                                for h in range(CH):
                                    left, right = (TT, YI) if l < TOP else (YI, TT)
                                    mm = pe.matmul(bank(4 + g, hi)[:, h, :], left[hi, g, h, :], right[hi, g, h, :],
                                                   start=True, stop=True)
                                mm.then_inc(t_ps if l < TOP else tt_ps, 1)
                        for j in range(PAIR):
                            pe.wait_ge(v_done, (k - 1) * PAIR + (j + 1))
                            for z in range(NZ):
                                pe.wait_ge(yi_done, k * (TOP * GR))
                                pe.wait_ge(s_done, (k - 1) * 4 + (2 * j + z + 1))
                                pe.sem_inc(pe_step, 1)
                                for h in range(CH):
                                    s = CH * z + h
                                    pe.matmul(bank(z, hi)[:, h, :], rac[:, j, s, C:P], state[:, j, z, h, :],
                                              start=True, stop=False)
                                    mm = pe.matmul(bank(z, hi)[:, h, :], G[0:C, j, s, C:P], vu[0:C, j, s, :],
                                                   start=False, stop=True)
                                mm.then_inc(x_ps, 1)
                            for z in range(NZ):
                                pe.wait_ge(x_done, (k - 1) * 4 + (2 * j + z + 1))
                                pe.wait_ge(top_done, (k - 1) * GR + (NZ * j + z + 1))
                                pe.sem_inc(pe_step, 1)
                                for h in range(CH):
                                    mm = pe.matmul(bank(2 + z, hi)[:, h, :], TT[hi, NZ * j + z, h, :], X[hi, z, h, :],
                                                   start=True, stop=True)
                                mm.then_inc(u_ps, 1)
                            for z in range(NZ):
                                pe.wait_ge(u_done, (k - 1) * 4 + (2 * j + z + 1))
                                pe.wait_ge(top_done, k * GR)
                                pe.sem_inc(pe_step, 1)
                                for h in range(CH):
                                    s = CH * z + h
                                    mm = pe.matmul(bank(4 + z, slice(0, C))[:, h, :], stc(kbt, j, s), vu[:, j, s, :],
                                                   start=True, stop=True)
                                mm.then_inc(s_ps, 1)
                            pe.wait_ge(out_done, (k - 1) * PAIR + (j + 1))
                            pe.sem_inc(pe_step, 1)
                            for s in range(ST):
                                y = bank(6 + s // CH, slice(0, C))[:, s % CH, :]
                                pe.matmul(y, rac[:, j, s, 0:C], state[:, j, s // CH, s % CH, :], start=True, stop=False)
                                mm = pe.matmul(y, G[:, j, s, 0:C], vu[:, j, s, :], start=False, stop=True)
                            mm.then_inc(out_ps, 1)


def mix_output_phase(nc, net, ps, layer):
    ins = net.ins
    last = layer == DEPTH - 1
    T0 = CT if last else 0
    n_all = NT - T0
    RW = NG + NE
    BIG = 1e30
    with phase(nc) as (sb, sem):
        ident = sb("ident", [P, P])
        w = sb("w", [P, DT, D])
        wr = sb("wr", [P, DT, RW])
        br = sb("br", [P, RW])
        rev = sb("rev", [P, RW])
        lnw, lnb = sb("lnw", [P, CW]), sb("lnb", [P, CW])
        gain = sb("gain", [P, D])
        GA, G, S = sb("GA", [P, 2, D]), sb("G", [P, 2, D]), sb("S", [P, 2, D])
        y = sb("y", [P, D])
        y1, y2 = sb("y1", [P, CW]), sb("y2", [P, CW])
        gb = sb("gb", [P, 2, CW])
        ysq = sb("ysq", [P, CW])
        st = sb("st", [P, 6, CH])
        yT, fT = sb("yT", [P, DT, P]), sb("fT", [P, DT, P])
        x, f, fs, xg = sb("x", [P, D]), sb("f", [P, D]), sb("fs", [P, D]), sb("xg", [P, D])
        small = sb("small", [P, 4])
        minus_half = sb("minus_half", [P, CH])
        lg = sb("lg", [P, RW])
        sel = sb("sel", [P, 4, RW])
        r1 = sb("r1", [P, 16])
        ex = sb("ex", [P, 2, NG + 1])
        c_in, c_ready, d_in, y_free, x_in, x_used, x_stored = (
            sem(n) for n in ("c_in", "c_ready", "d_in", "y_free", "x_in", "x_used", "x_stored"))
        var_done, root_done, y_done, y_ps, yT_done, prod = (
            sem(n) for n in ("var_done", "root_done", "y_done", "y_ps", "yT_done", "prod"))
        x_done, f_var, f_root, f_done, f_ps, fT_done, lg_ps, f_stored = (
            sem(n) for n in ("x_done", "f_var", "f_root", "f_done", "f_ps", "fT_done", "lg_ps", "f_stored"))
        diff_done, exp_done, y_mid, y_aff, prod_used, lg_used, pool_step, half_set = (
            sem(n) for n in ("diff_done", "exp_done", "y_mid", "y_aff", "prod_used", "lg_used", "pool_step", "half_set"))
        y_summed, gb_in, ya_in, w_in = sem("y_summed"), sem("gb_in"), sem("ya_in"), sem("w_in")
        NCON = 15

        def steps(eng, step):
            lo = max(T0 + 3, CT + 1)
            for i in range(T0 - 1, lo):
                step(i, lambda d, i=i: T0 <= i + d < NT)
            with eng.Fori(lo, NT - 1) as i:
                step(i, lambda d: True)
            for i in range(NT - 1, NT + 3):
                step(i, lambda d, i=i: T0 <= i + d < NT)

        def cond(i, d):
            return 1 if isinstance(i, int) and i + d < CT else 0

        with nc.Block() as block:
            @block.sync
            def _(sp):
                bc = lambda ap: ap.partition_broadcast(P)
                sp.dma_start(ident[:], ins["k_ident"]).then_inc(c_in, 16)
                sp.dma_start(wr[:, :, 0:NG], ins["r_w_group"][layer].rearrange("(t p) n -> p t n", p=P)
                             ).then_inc(c_in, 16)
                sp.dma_start(wr[:, :, NG:], ins["r_w_expert"][layer].rearrange("(t p) n -> p t n", p=P)
                             ).then_inc(c_in, 16)
                sp.dma_start(br[:, 0:NG], bc(ins["r_b_group"][layer])).then_inc(c_in, 16)
                sp.dma_start(br[:, NG:], bc(ins["r_b_expert"][layer])).then_inc(c_in, 16)
                sp.dma_start(rev[:], bc(ins["k_rev"])).then_inc(c_in, 16)
                sp.dma_start(lnw[:], bc(ins["c_ln_w"][layer])).then_inc(c_in, 16)
                sp.dma_start(lnb[:], bc(ins["c_ln_b"][layer])).then_inc(c_in, 16)
                sp.dma_start(gain[:], bc(ins["g_ffn"][layer])).then_inc(c_in, 16)
                for j in range(2):
                    m = net.mod[layer][j]
                    sp.dma_start(GA[:, j, :], bc(m[2 * D:3 * D])).then_inc(c_in, 16)
                    sp.dma_start(S[:, j, :], bc(m[3 * D:4 * D])).then_inc(c_in, 16)
                    sp.dma_start(G[:, j, :], bc(m[4 * D:5 * D])).then_inc(c_in, 16)
                sp.sem_inc(y_summed, 1)
                sp.sem_inc(y_done, 1)
                sp.sem_inc(y_free, 1)
                sp.sem_inc(x_stored, 16)

                def load_y(t):
                    r = t * P
                    sp.wait_ge(y_summed, t + (1 - T0))
                    sp.dma_start(y1[:], rows(net.yd[0], r)).then_inc(d_in, 16)
                    sp.dma_start(y2[:], rows(net.yd[1], r)).then_inc(d_in, 16)
                    sp.wait_ge(y_done, t + (1 - T0))
                    sp.dma_start(gb[:].rearrange("p j c -> p (j c)"), rows(net.gb, r)).then_inc(gb_in, 16)
                    sp.wait_ge(y_free, t + (1 - T0))
                    sp.dma_start(y[:, 0:CW], rows(net.y, r)[:, 0:CW]).then_inc(ya_in, 16)

                def load_x(t):
                    sp.wait_ge(x_stored, (t + (1 - T0)) * 16)
                    sp.wait_ge(x_used, t + (1 - T0))
                    sp.dma_start(x[:], rows(net.x, t * P)).then_inc(x_in, 16)

                load_y(T0)
                sp.dma_start(w[:], ins["w_out"][layer].rearrange("(t p) n -> p t n", p=P)).then_inc(w_in, 16)
                with sp.Fori(T0, NT - 1) as t:
                    load_y(t + 1)
                    load_x(t)
                load_x(NT - 1)

            @block.gpsimd
            def _(pool):
                pool.memset(minus_half[:], -0.5).then_inc(half_set, 1)
                pool.wait_ge(half_set, 1)
                pool.wait_ge(c_in, 16 * NCON)

                def step(i, tile):
                    k = i + (1 - T0)
                    if tile(-1):
                        pool.wait_ge(f_var, k - 1)
                        pool.sem_inc(pool_step, 1)
                        pool.tensor_tensor(small[:, 2:3], small[:, 1:2], minus_half[:, 0:1], ALU.pow).then_inc(f_root, 1)
                    if tile(1):
                        pool.wait_ge(var_done, k + 1)
                        pool.sem_inc(pool_step, 1)
                        pool.tensor_tensor(st[:, 3, :], st[:, 2, :], minus_half[:], ALU.pow).then_inc(root_done, 1)
                        yc = y[:, CW:D]
                        pool.wait_ge(y_mid, k + 1)
                        pool.tensor_tensor(yc, yc, lnw[:], ALU.mult).then_inc(y_aff, 1)
                        pool.wait_ge(y_aff, k * 3 + 1)
                        pool.tensor_tensor(yc, yc, lnb[:], ALU.add).then_inc(y_aff, 1)
                        pool.wait_ge(y_aff, k * 3 + 2)
                        pool.wait_ge(gb_in, (k + 1) * 16)
                        pool.sem_inc(pool_step, 1)
                        pool.tensor_tensor(yc, yc, gb[:, 1, :], ALU.add).then_inc(y_aff, 1)
                        pool.wait_ge(y_aff, k * 3 + 3)
                        pool.tensor_tensor(yc, yc, gb[:, 0, :], ALU.mult).then_inc(y_done, 1)

                steps(pool, step)

            @block.scalar
            def _(act):
                act.sem_inc(f_stored, 16)

                def step(i, tile):
                    k = i + (1 - T0)
                    if tile(-1):
                        act.wait_ge(x_done, k - 1)
                        act.dma_start(rows(net.x, (i - 1) * P), x[:]).then_inc(x_stored, 16)
                        act.wait_ge(f_ps, k - 1)
                        act.activation(fT[:], ps[:, 4:6, :].rearrange("p b (t n) -> p (b t) n", n=P), ACT.Copy
                                       ).then_inc(fT_done, 1)
                        act.dma_start(rows(net.f, (i - 1) * P), f[:]).then_inc(f_stored, 16)
                    if tile(1):
                        act.wait_ge(y_ps, k + 1)
                        act.activation(yT[:], ps[:, 0:2, :].rearrange("p b (t n) -> p (b t) n", n=P), ACT.Copy
                                       ).then_inc(yT_done, 1)
                        act.sem_inc(y_free, 1)
                    if tile(-2):
                        act.wait_ge(diff_done, k - 2)
                        act.activation(ex[:, 1, :], ex[:, 0, :], ACT.Exp).then_inc(exp_done, 1)

                steps(act, step)
                act.wait_ge(f_stored, 16 * (n_all + 1))
                act.wait_ge(x_stored, 16 * (n_all + 1))

            @block.vector
            def _(dve):
                dve.wait_ge(c_in, 16 * NCON)
                for j in range(2):
                    dve.scalar_tensor_tensor(G[:, j, :], G[:, j, :], 1.0, gain[:], ALU.add, ALU.mult)
                dve.sem_inc(x_used, 1)
                b8 = lambda q: st[:, q, :].unsqueeze(2).broadcast_to([P, CH, HD])
                yc = y[:, CW:D]

                def step(i, tile):
                    k = i + (1 - T0)
                    j = cond(i, -1)
                    if tile(-1):
                        dve.wait_ge(prod, k - 1)
                        dve.tensor_tensor(xg[:], ps[:, 2:4, :], GA[:, j, :].rearrange("p (a n) -> p a n", a=2), ALU.mult
                                          ).then_inc(prod_used, 1)
                        dve.drain()
                        dve.wait_ge(x_in, (k - 1) * 16)
                        dve.tensor_tensor(x[:], x[:], xg[:], ALU.add).then_inc(x_done, 1)
                        dve.drain()
                        dve.scalar_tensor_tensor(fs[:], x[:], 1.0, x[:], ALU.mult, ALU.mult, accum_out=small[:, 0:1])
                        dve.drain()
                        dve.tensor_scalar(small[:, 1:2], small[:, 0:1], 1.0 / D, EPS, ALU.mult, ALU.add
                                          ).then_inc(f_var, 1)
                    if tile(1):
                        dve.wait_ge(d_in, (k + 1) * 32)
                        dve.wait_ge(y_free, k + 1)
                        dve.tensor_tensor(yc, y1[:], y2[:], ALU.add).then_inc(y_summed, 1)
                        dve.drain()
                        dve.tensor_reduce(st[:, 0, :], heads_of(yc), AX.X, ALU.add)
                        dve.drain()
                        dve.tensor_scalar(st[:, 1, :], st[:, 0, :], -1.0 / HD, None, ALU.mult)
                        dve.drain()
                        dve.tensor_tensor(heads_of(yc), heads_of(yc), b8(1), ALU.add)
                        dve.drain()
                        dve.tensor_tensor(ysq[:], yc, yc, ALU.mult)
                        dve.drain()
                        dve.tensor_reduce(st[:, 0, :], heads_of(ysq[:]), AX.X, ALU.add)
                        dve.drain()
                        dve.tensor_scalar(st[:, 2, :], st[:, 0, :], 1.0 / HD, GN_EPS, ALU.mult, ALU.add
                                          ).then_inc(var_done, 1)
                    if tile(-1):
                        dve.wait_ge(f_root, k - 1)
                        dve.scalar_tensor_tensor(fs[:], x[:], small[:, 2:3], G[:, j, :], ALU.mult, ALU.mult)
                        dve.drain()
                        dve.sem_inc(x_used, 1)
                        dve.wait_ge(f_stored, (k - 1) * 16)
                        if tile(-2):
                            dve.wait_ge(f_ps, k - 2)
                        dve.tensor_tensor(f[:], fs[:], S[:, j, :], ALU.add).then_inc(f_done, 1)
                    if tile(1):
                        dve.wait_ge(root_done, k + 1)
                        dve.tensor_tensor(heads_of(yc), heads_of(yc), b8(3), ALU.mult).then_inc(y_mid, 1)
                    if tile(-3):
                        dve.wait_ge(exp_done, k - 3)
                        dve.tensor_reduce(r1[:, 8:9], ex[:, 1, 0:NG], AX.X, ALU.add)
                        dve.tensor_scalar(r1[:, 9:10], ex[:, 1, NG:NG + 1], 1.0, None, ALU.add)
                        dve.drain()
                        dve.tensor_tensor(r1[:, 10:11], r1[:, 8:9], r1[:, 9:10], ALU.mult)
                        dve.drain()
                        dve.reciprocal(r1[:, 11:12], r1[:, 10:11])
                        dve.drain()
                        dve.tensor_tensor(r1[:, 12:13], r1[:, 11:12], ex[:, 1, NG:NG + 1], ALU.mult)
                        dve.drain()
                        dve.tensor_copy(net.gate[:, ds(i - 3, 1), :], r1[:, 11:13].unsqueeze(1))
                    if tile(-2):
                        dve.wait_ge(lg_ps, k - 2)
                        dve.tensor_tensor(lg[:], ps[:, 6, 0:RW], br[:], ALU.add).then_inc(lg_used, 1)
                        dve.drain()
                        gl, el = lg[:, 0:NG], lg[:, NG:]
                        el3 = el.rearrange("p (g e) -> p g e", g=NG)

                        def first_largest(v, r, top, out, at):
                            w_ = v.shape[-1]
                            dve.tensor_reduce(r1[:, top:top + 1], v, AX.X, ALU.max)
                            dve.drain()
                            c_ = sel[:, at, 0:w_]
                            dve.scalar_tensor_tensor(c_, v, r1[:, top:top + 1], r, ALU.is_equal, ALU.mult)
                            dve.drain()
                            dve.tensor_reduce(r1[:, top + 1:top + 2], c_, AX.X, ALU.max)
                            dve.drain()
                            dve.tensor_scalar(out, c_, r1[:, top + 1:top + 2], None, ALU.is_equal)
                            dve.drain()

                        pick = sel[:, 1, 0:NG]
                        first_largest(gl, rev[:, 0:NG], 0, pick, 0)
                        dve.tensor_scalar(ex[:, 0, 0:NG], gl, r1[:, 0:1], None, ALU.subtract)
                        dve.tensor_scalar(sel[:, 2, 0:NG], pick, 1.0, BIG, ALU.subtract, ALU.mult)
                        dve.drain()
                        dve.tensor_tensor(el3, el3, sel[:, 2, 0:NG].unsqueeze(2).broadcast_to([P, NG, EPG]), ALU.add)
                        dve.drain()
                        one, two = sel[:, 1, 0:NE], sel[:, 3, 0:NE]
                        first_largest(el, rev[:, NG:], 2, one, 0)
                        dve.tensor_copy(net.chosen[:, ds(i - 2, 1), 0, :], one.unsqueeze(1))
                        dve.scalar_tensor_tensor(el, one, -2.0 * BIG, el, ALU.mult, ALU.add)
                        dve.drain()
                        first_largest(el, rev[:, NG:], 4, two, 0)
                        dve.tensor_copy(net.chosen[:, ds(i - 2, 1), 1, :], two.unsqueeze(1))
                        dve.tensor_tensor(ex[:, 0, NG:NG + 1], r1[:, 4:5], r1[:, 2:3], ALU.subtract
                                          ).then_inc(diff_done, 1)

                steps(dve, step)
                dve.drain()

            @block.tensor
            def _(pe):
                pe.wait_ge(c_in, 16 * NCON)

                def step(i, tile):
                    k = i + (1 - T0)
                    if tile(0):
                        pe.wait_ge(w_in, 16)
                        pe.wait_ge(yT_done, k)
                        if tile(-1):
                            pe.wait_ge(prod_used, k - 1)
                        for c in range(2):
                            for t in range(DT):
                                mm = pe.matmul(ps[:, 2 + c, :], yT[:, t, :], w[:, t, c * 512:(c + 1) * 512],
                                               start=(t == 0), stop=(t == DT - 1))
                        mm.then_inc(prod, 1)
                    if tile(-1):
                        pe.wait_ge(f_done, k - 1)
                        for t in range(DT):
                            tr = pe.transpose(ps[:, 4 + t // 4, (t % 4) * P:(t % 4 + 1) * P],
                                              f[:, t * P:(t + 1) * P], ident[:])
                        tr.then_inc(f_ps, 1)
                    if tile(1):
                        pe.wait_ge(y_done, k + 2)
                        pe.wait_ge(ya_in, (k + 1) * 16)
                        for t in range(DT):
                            tr = pe.transpose(ps[:, t // 4, (t % 4) * P:(t % 4 + 1) * P], y[:, t * P:(t + 1) * P],
                                              ident[:])
                        tr.then_inc(y_ps, 1)
                    if tile(-1):
                        pe.wait_ge(fT_done, k - 1)
                        if tile(-2):
                            pe.wait_ge(lg_used, k - 2)
                        for t in range(DT):
                            mm = pe.matmul(ps[:, 6, 0:RW], fT[:, t, :], wr[:, t, :], start=(t == 0), stop=(t == DT - 1))
                        mm.then_inc(lg_ps, 1)

                steps(pe, step)


def placement_phase(nc, net, ps, layer):
    ins = net.ins
    t0 = CT if layer == DEPTH - 1 else 0
    n = NT - t0
    with phase(nc) as (sb, sem):
        ident, before, ones = sb("ident", [P, P]), sb("before", [P, P]), sb("ones", [P, P])
        before_e = sb("before_e", [NE, NE])
        e_row = sb("e_row", [P, NE])
        j_row = sb("j_row", [1, OVER])
        both = sb("both", [P, NT, NE])
        rank, place, w = sb("rank", [P, NT, NE]), sb("place", [P, NT, NE]), sb("w", [P, NT, NE])
        count, nov, shift = sb("count", [P, NE]), sb("nov", [P, NE]), sb("shift", [P, NE])
        novT = sb("novT", [NE, P])
        end = sb("end", [P, NE])
        cmp = sb("cmp", [1, OVER, NE])
        blk = sb("blk", [1, OVER + 1])
        rowf = sb("rowf", [P, NT, 2])
        token = sb("token", [P, NT], I32)
        zero = sb("zero", [P, NB], I32)
        c_in, both_done, rank_ps, nov_done, novT_ps, novT_done, ov_ps, rows_done, cleared, scattered, pool_c = (
            sem(s) for s in ("c_in", "both_done", "rank_ps", "nov_done", "novT_ps", "novT_done", "ov_ps",
                             "rows_done", "cleared", "scattered", "pool_c"))
        with nc.Block() as block:
            @block.sync
            def _(sp):
                sp.dma_start(ident[:], ins["k_ident"]).then_inc(c_in, 16)
                sp.dma_start(before[:], ins["k_before"]).then_inc(c_in, 16)
                sp.dma_start(before_e[:], ins["k_before_e"]).then_inc(c_in, 16)
                sp.dma_start(e_row[:], ins["k_e_row"].partition_broadcast(P)).then_inc(c_in, 16)
                sp.dma_start(j_row[:], ins["k_j_row"].partition_broadcast(1)).then_inc(c_in, 16)
                sp.wait_ge(pool_c, 3)
                sp.dma_start(net.table.rearrange("(p b) o -> p (b o)", p=P), zero[:]).then_inc(cleared, 16)

            @block.gpsimd
            def _(pool):
                pool.memset(ones[:], 1.0).then_inc(pool_c, 1)
                pool.memset(zero[:], 0).then_inc(pool_c, 1)
                pool.iota(token[:], pattern=[[P, NT]], base=0, channel_multiplier=1).then_inc(pool_c, 1)
                pool.wait_ge(pool_c, 3)
                pool.wait_ge(cleared, 16)
                pool.wait_ge(rows_done, 1)
                for t in range(t0, NT):
                    for j in range(2):
                        pool.indirect_dma_start(net.table, bass.IndirectOffsetOnAxis(net.row[:, t, j:j + 1], 0),
                                                token[:, t:t + 1], None).then_inc(scattered, 16)
                pool.wait_ge(scattered, 16 * 2 * n)

            @block.vector
            def _(dve):
                T = slice(t0, NT)
                dve.tensor_tensor(both[:, T], net.chosen[:, T, 0, :], net.chosen[:, T, 1, :], ALU.add
                                  ).then_inc(both_done, 1)
                dve.wait_ge(rank_ps, 1)
                dve.tensor_copy(rank[:, T], ps[:, 0, 0:n * NE].rearrange("p (t e) -> p t e", e=NE))
                dve.tensor_copy(count[:], ps[:, 1, 0:NE])
                dve.drain()
                dve.tensor_scalar(nov[:], count[:], float(P), None, ALU.is_gt)
                for m in range(2, NT):
                    dve.drain()
                    dve.scalar_tensor_tensor(nov[:], count[:], float(P * m), nov[:], ALU.is_gt, ALU.add)
                dve.drain()
                dve.sem_inc(nov_done, 1)
                dve.wait_ge(novT_ps, 1)
                dve.tensor_copy(novT[:], ps[0:NE, 2, 0:P]).then_inc(novT_done, 1)
                dve.wait_ge(ov_ps, 1)
                dve.tensor_scalar(shift[:], ps[:, 3, 0:NE], float(P), float((NE - 1) * P), ALU.mult, ALU.add)
                dve.tensor_tensor(end[:], ps[:, 3, 0:NE], nov[:], ALU.add)
                dve.drain()
                dve.wait_ge(c_in, 80)
                dve.tensor_tensor(shift[:], shift[:], e_row[:], ALU.subtract)
                dve.tensor_scalar(w[:, T], rank[:, T], float(P), None, ALU.is_ge)
                dve.tensor_tensor(place[:, T], rank[:, T], e_row[:].unsqueeze(1).broadcast_to([P, n, NE]), ALU.add)
                dve.drain()
                dve.tensor_tensor(w[:, T], w[:, T], shift[:].unsqueeze(1).broadcast_to([P, n, NE]), ALU.mult)
                dve.drain()
                dve.tensor_tensor(place[:, T], place[:, T], w[:, T], ALU.add)
                for j in range(2):
                    dve.drain()
                    dve.tensor_tensor(w[:, T], place[:, T], net.chosen[:, T, j, :], ALU.mult)
                    dve.drain()
                    dve.tensor_reduce(rowf[:, T, j], w[:, T], AX.X, ALU.add)
                dve.drain()
                dve.tensor_copy(net.row[:, T, :], rowf[:, T, :])
                e3 = end[0:1, :].unsqueeze(1).broadcast_to([1, OVER, NE])
                dve.tensor_tensor(cmp[:], e3, j_row[:].unsqueeze(2).broadcast_to([1, OVER, NE]), ALU.is_le)
                dve.drain()
                dve.tensor_reduce(blk[:, 0:OVER], cmp[:], AX.X, ALU.add)
                dve.tensor_copy(blk[:, OVER:OVER + 1], end[0:1, NE - 1:NE])
                dve.drain()
                dve.tensor_scalar(blk[:, 0:OVER], blk[:, 0:OVER], float(NE - 1), None, ALU.min)
                dve.drain()
                dve.tensor_copy(net.blocks[:], blk[:])
                dve.drain()
                dve.sem_inc(rows_done, 1)

            @block.tensor
            def _(pe):
                pe.wait_ge(c_in, 80)
                pe.wait_ge(pool_c, 3)
                pe.wait_ge(both_done, 1)
                for t in range(t0, NT):
                    o = ps[:, 0, (t - t0) * NE:(t - t0 + 1) * NE]
                    for u in range(t0, t):
                        pe.matmul(o, ones[:], both[:, u, :], start=(u == t0), stop=False)
                    mm = pe.matmul(o, before[:], both[:, t, :], start=(t == t0), stop=True)
                for t in range(t0, NT):
                    mm = pe.matmul(ps[:, 1, 0:NE], ones[:], both[:, t, :], start=(t == t0), stop=(t == NT - 1))
                mm.then_inc(rank_ps, 1)
                pe.wait_ge(nov_done, 1)
                pe.transpose(ps[0:NE, 2, 0:P], nov[:], ident[:]).then_inc(novT_ps, 1)
                pe.wait_ge(novT_done, 1)
                pe.matmul(ps[:, 3, 0:NE], novT[:], before_e[:], start=True, stop=True).then_inc(ov_ps, 1)


def expert_phase(nc, net, ps, layer):
    ins = net.ins
    HF = FF // P
    with phase(nc) as (sb, sem):
        ident = sb("ident", [P, P])
        w1 = [sb(f"w1{b}", [P, DT, FF]) for b in range(2)]
        w3 = [sb(f"w3{b}", [P, DT, FF]) for b in range(2)]
        w2 = [sb(f"w2{b}", [P, HF, D]) for b in range(2)]
        idx = [sb(f"idx{b}", [P, 1], I32) for b in range(2)]
        xg = [sb(f"xg{b}", [P, D]) for b in range(2)]
        xT = [sb(f"xT{b}", [P, DT, P]) for b in range(2)]
        sg = [sb(f"sg{b}", [P, FF]) for b in range(2)]
        h = [sb(f"h{b}", [P, FF]) for b in range(2)]
        hT = [sb(f"hT{b}", [P, HF, P]) for b in range(2)]
        yo = [sb(f"yo{b}", [P, D]) for b in range(2)]
        c_in, pool_step, act_step = sem("c_in"), sem("pool_step"), sem("act_step")
        w13_in = [sem(f"w13_in{b}") for b in range(2)]
        w2_in = [sem(f"w2_in{b}") for b in range(2)]
        idx_in = [sem(f"idx_in{b}") for b in range(2)]
        x_in = [sem(f"x_in{b}") for b in range(2)]
        stored = [sem(f"stored{b}") for b in range(2)]
        x_ps, xT_done, up, sig, h_done, h_ps, hT_done, down, y_done = (
            sem(n) for n in ("x_ps", "xT_done", "up", "sig", "h_done", "h_ps", "hT_done", "down", "y_done"))
        UP = lambda b: 2 + 2 * b
        XB = lambda b: 6 * b

        def pairs(eng, pair):
            used = eng.value_load(net.blocks[0:1, OVER:OVER + 1], min_val=0, max_val=OVER)
            with eng.Fori(0, NE // 2) as i:
                pair(i, 0)
            with eng.Fori(0, OVER // 2) as i:
                with eng.If(i * 2 < used):
                    pair(i, NE)
        with nc.Block() as block:
            @block.sync
            def _(sp):
                sp.dma_start(ident[:], ins["k_ident"]).then_inc(c_in, 16)
                sp.sem_inc(up, 2)
                sp.sem_inc(down, 2)

                def pair(i, before):
                    for b in range(2):
                        q = i * 2 + (b + before + 1)
                        e = i * 2 + b
                        if before:
                            e = sp.value_load(net.blocks[0:1, ds(i * 2 + b, 1)], min_val=0, max_val=NE - 1)
                        sp.wait_ge(up, q)
                        for w, name in ((w1[b], "e_w1"), (w3[b], "e_w3")):
                            src = ins[name][layer].rearrange("e (p t) f -> e p (t f)", p=P)[ds(e, 1)]
                            sp.dma_start(w[:].rearrange("p t f -> p (t f)"), src.rearrange("o p n -> (o p) n")
                                         ).then_inc(w13_in[b], 16)
                        sp.wait_ge(down, q)
                        src = ins["e_w2"][layer].rearrange("e (p t) f -> e p (t f)", p=P)[ds(e, 1)]
                        sp.dma_start(w2[b][:].rearrange("p t f -> p (t f)"), src.rearrange("o p n -> (o p) n")
                                     ).then_inc(w2_in[b], 16)
                pairs(sp, pair)

            @block.gpsimd
            def _(pool):
                pool.sem_inc(x_ps, 2)

                def pair(i, before):
                    m = i + (1 + before // 2)
                    for b in range(2):
                        q = i * 2 + (b + before + 1)
                        pool.wait_ge(x_ps, q)
                        pool.sem_inc(pool_step, 1)
                        pool.dma_start(idx[b][:], net.table[ds((i * 2 + (b + before)) * P, P), :]
                                       ).then_inc(idx_in[b], 16)
                        pool.wait_ge(idx_in[b], m * 16)
                        pool.sem_inc(pool_step, 1)
                        pool.indirect_dma_start(xg[b][:], None, net.f, bass.IndirectOffsetOnAxis(idx[b][:, 0:1], 0)
                                                ).then_inc(x_in[b], 16)
                pairs(pool, pair)

            @block.scalar
            def _(act):
                for b in range(2):
                    act.sem_inc(stored[b], 16)

                def pair(i, before):
                    m = i + (1 + before // 2)
                    for b in range(2):
                        q = i * 2 + (b + before + 1)
                        act.wait_ge(up, q + 2)
                        act.activation(sg[b][:], ps[:, UP(b), :], ACT.Sigmoid).then_inc(sig, 1)
                        act.wait_ge(h_ps, q)
                        act.activation(hT[b][:], ps[:, 6 + b, :].rearrange("p (t n) -> p t n", n=P), ACT.Copy
                                       ).then_inc(hT_done, 1)
                    for b in range(2):
                        q = i * 2 + (b + before + 1)
                        act.wait_ge(down, q + 2)
                        act.wait_ge(stored[b], m * 16)
                        act.activation(yo[b][:], ps[:, UP(b):UP(b) + 2, :], ACT.Copy).then_inc(y_done, 1)
                        act.wait_ge(y_done, q + 2)
                        act.dma_start(rows(net.ye, (i * 2 + (b + before)) * P), yo[b][:]).then_inc(stored[b], 16)
                    if before:
                        for b in range(2):
                            act.wait_ge(stored[b], (m + 1) * 16)
                        act.sem_inc(act_step, 1)
                pairs(act, pair)
                for b in range(2):
                    act.wait_ge(stored[b], 16 * (NE // 2 + 1))

            @block.vector
            def _(dve):
                def pair(i, before):
                    for b in range(2):
                        dve.wait_ge(x_ps, i * 2 + (b + before + 3))
                        dve.tensor_copy(xT[b][:], ps[:, XB(b):XB(b) + 2, :].rearrange("p b (t n) -> p (b t) n", n=P)
                                        ).then_inc(xT_done, 1)
                    for b in range(2):
                        dve.wait_ge(sig, i * 2 + (b + before + 1))
                        dve.tensor_tensor(sg[b][:], sg[b][:], ps[:, UP(b), :], ALU.mult)
                        dve.drain()
                        dve.tensor_tensor(h[b][:], sg[b][:], ps[:, UP(b) + 1, :], ALU.mult).then_inc(h_done, 1)
                pairs(dve, pair)

            @block.tensor
            def _(pe):
                pe.wait_ge(c_in, 16)
                pe.sem_inc(y_done, 2)

                def pair(i, before):
                    m = i + (1 + before // 2)
                    for b in range(2):
                        pe.wait_ge(x_in[b], m * 16)
                        for t in range(DT):
                            tr = pe.transpose(ps[:, XB(b) + t // 4, (t % 4) * P:(t % 4 + 1) * P],
                                              xg[b][:, t:D:DT], ident[:])
                        tr.then_inc(x_ps, 1)
                    def turn_h(b):
                        pe.wait_ge(h_done, i * 2 + (b + before + 1))
                        for t in range(HF):
                            tr = pe.transpose(ps[:, 6 + b, t * P:(t + 1) * P], h[b][:, t:FF:HF], ident[:])
                        tr.then_inc(h_ps, 1)

                    for b in range(2):
                        q = i * 2 + (b + before + 1)
                        pe.wait_ge(xT_done, q)
                        pe.wait_ge(w13_in[b], m * 32)
                        pe.wait_ge(y_done, q)
                        for j, w in enumerate((w1[b], w3[b])):
                            if b == 1 and j == 1:
                                turn_h(0)
                            for t in range(DT):
                                mm = pe.matmul(ps[:, UP(b) + j, :], xT[b][:, t, :], w[:, t, :],
                                               start=(t == 0), stop=(t == DT - 1))
                        mm.then_inc(up, 1)
                    for b in range(2):
                        pe.wait_ge(hT_done, i * 2 + (b + before + 1))
                        pe.wait_ge(w2_in[b], m * 16)
                        for c in range(2):
                            if b == 0 and c == 1:
                                turn_h(1)
                            for t in range(HF):
                                mm = pe.matmul(ps[:, UP(b) + c, :], hT[b][:, t, :], w2[b][:, t, c * 512:(c + 1) * 512],
                                               start=(t == 0), stop=(t == HF - 1))
                        mm.then_inc(down, 1)
                pairs(pe, pair)


def combine_phase(nc, net, ps, layer):
    ins = net.ins
    last = layer == DEPTH - 1
    T0 = CT if last else 0
    n_all = NT - T0
    with phase(nc) as (sb, sem):
        GA = sb("GA", [P, 2, D])
        gain = sb("gain", [P, D])
        x, mix, o = sb("x", [P, D]), sb("mix", [P, D]), sb("o", [P, D])
        y = [[sb(f"y{b}_{j}", [P, D]) for j in range(2)] for b in range(2)]
        idx = [[sb(f"idx{b}_{j}", [P, 1], U32) for j in range(2)] for b in range(2)]
        gate = sb("gate", [P, 2, 2])
        small = sb("small", [P, 4])
        c_in, x_in, used, idx_done, mean_done, root_done, o_done, stored, pool_step = (
            sem(n) for n in ("c_in", "x_in", "used", "idx_done", "mean_done", "root_done", "o_done",
                             "stored", "pool_step"))
        y_in = [sem(f"y_in{b}") for b in range(2)]

        def steps(eng, step):
            step(T0 - 1, 1, 0, True)
            for i in range(T0, CT):
                step(i, i % 2, (i - T0) // 2, True)
            with eng.Fori(0, (NT - CT) // 2 - 1) as q:
                for b in range(2):
                    step(q * 2 + (CT + b), b, q + (CT - T0) // 2, True)
            step(NT - 2, 0, (NT - 2 - T0) // 2, True)
            step(NT - 1, 1, (NT - 1 - T0) // 2, False)

        with nc.Block() as block:
            @block.sync
            def _(sp):
                for j in range(2):
                    sp.dma_start(GA[:, j, :], net.mod[layer][j][5 * D:6 * D].partition_broadcast(P)).then_inc(c_in, 16)
                sp.dma_start(gain[:], ins["g_final"].partition_broadcast(P)).then_inc(c_in, 16)
                sp.sem_inc(used, 1)
                with sp.Fori(T0, NT) as i:
                    sp.wait_ge(used, i + (1 - T0))
                    sp.dma_start(x[:], rows(net.x, i * P)).then_inc(x_in, 16)

            @block.gpsimd
            def _(pool):
                def step(i, par, nth, more):
                    if more:
                        pool.wait_ge(idx_done, i + (2 - T0))
                        pool.sem_inc(pool_step, 1)
                        for j in range(2):
                            pool.indirect_dma_start(y[1 - par][j][:], None, net.ye,
                                                    bass.IndirectOffsetOnAxis(idx[1 - par][j][:, 0:1], 0)
                                                    ).then_inc(y_in[1 - par], 16)

                steps(pool, step)

            @block.scalar
            def _(act):
                act.sem_inc(stored, 16)
                with act.Fori(T0, NT) as i:
                    k = i + (1 - T0)
                    if last:
                        act.wait_ge(mean_done, k)
                        act.activation(small[:, 2:3], small[:, 1:2], ACT.Sqrt).then_inc(root_done, 1)
                    act.wait_ge(o_done, k)
                    dst = rows(net.out[0], i * P - CTX) if last else rows(net.x, i * P)
                    act.dma_start(dst, o[:]).then_inc(stored, 16)
                act.wait_ge(stored, 16 * (n_all + 1))

            @block.vector
            def _(dve):
                dve.wait_ge(c_in, 48)

                def step(i, par, nth, more):
                    k = i + (1 - T0)
                    j = 1 if isinstance(i, int) and i < CT else 0
                    if more:
                        for q in range(2):
                            dve.tensor_copy(idx[1 - par][q][:].unsqueeze(1), net.row[:, ds(i + 1, 1), q:q + 1])
                        dve.tensor_copy(gate[:, 1 - par, :].unsqueeze(1), net.gate[:, ds(i + 1, 1), :])
                        dve.drain()
                        dve.sem_inc(idx_done, 1)
                    if isinstance(i, int) and i < T0:
                        return
                    y0, y1 = y[par]
                    dve.wait_ge(y_in[par], nth * 32 + 32)
                    dve.tensor_scalar(mix[:], y0[:], gate[:, par, 0:1], None, ALU.mult)
                    dve.drain()
                    dve.scalar_tensor_tensor(mix[:], y1[:], gate[:, par, 1:2], mix[:], ALU.mult, ALU.add)
                    dve.drain()
                    dve.tensor_tensor(mix[:], mix[:], GA[:, j, :], ALU.mult)
                    dve.drain()
                    dve.wait_ge(x_in, k * 16)
                    dve.wait_ge(stored, k * 16)
                    if not last:
                        dve.tensor_tensor(o[:], x[:], mix[:], ALU.add).then_inc(o_done, 1)
                        dve.drain()
                        dve.sem_inc(used, 1)
                        return
                    dve.tensor_tensor(x[:], x[:], mix[:], ALU.add)
                    dve.drain()
                    dve.scalar_tensor_tensor(mix[:], x[:], 1.0, x[:], ALU.mult, ALU.mult, accum_out=small[:, 0:1])
                    dve.drain()
                    dve.tensor_scalar(small[:, 1:2], small[:, 0:1], 1.0 / D, EPS, ALU.mult, ALU.add
                                      ).then_inc(mean_done, 1)
                    dve.wait_ge(root_done, k)
                    dve.reciprocal(small[:, 3:4], small[:, 2:3])
                    dve.drain()
                    dve.scalar_tensor_tensor(o[:], x[:], small[:, 3:4], gain[:], ALU.mult, ALU.mult
                                             ).then_inc(o_done, 1)
                    dve.drain()
                    dve.sem_inc(used, 1)

                steps(dve, step)


INPUTS = ["x", "c", "ctx", "c_ctx", "w_mod", "b_mod", "g_mix", "g_ffn", "w_in", "a_q_gain", "a_k_gain",
          "b_lq1", "b_lk1", "b_lq2", "b_lk2", "b_subln", "c_mu", "c_w0", "c_w2", "c_a0", "c_a2", "c_g2",
          "c_k_k", "c_k_a", "c_r_k", "c_ln_w", "c_ln_b", "w_out", "r_w_group", "r_b_group",
          "r_w_expert", "r_b_expert", "e_w1", "e_w3", "e_w2", "g_final"]


def constants():
    tri, mask, levels = scan_constants()
    i = np.arange(P)
    return {
        "k_ident": np.eye(P, dtype=np.float32),
        "k_shift": (0.5 * (abs(i[:, None] - i[None, :]) == 1) - np.eye(P)).astype(np.float32),
        "k_around": (0.5 * np.stack([i == 0, i == P - 1] + [i < 0] * (P - 2))).astype(np.float32),
        "k_rope": rope_tables(),
        "k_tri": tri, "k_mask": mask, "k_levels": levels,
        "k_before": (i[:, None] < i[None, :]).astype(np.float32),
        "k_rev": np.concatenate([NG - np.arange(NG), NE - np.arange(NE)]).astype(np.float32),
        "k_e_row": (P * np.arange(NE)).astype(np.float32),
        "k_j_row": np.arange(OVER).astype(np.float32),
        "k_before_e": (np.arange(NE)[:, None] < np.arange(NE)[None, :]).astype(np.float32),
    }




def build(nc, ins, out):
    net = Net(nc, ins, out)
    with (nc.psum_tensor("ps", [P, 8, 512], F32) as ps_t, nc.sbuf_tensor("chosen", [P, NT, 2, NE], F32) as chosen,
          nc.sbuf_tensor("gate", [P, NT, 2], F32) as gate, nc.sbuf_tensor("row", [P, NT, 2], U32) as row,
          nc.sbuf_tensor("blocks", [1, OVER + 1], I32) as blocks):
        ps = ps_t[:]
        net.chosen, net.gate, net.row, net.blocks = chosen, gate, row, blocks
        steps = [lambda: modulation_phase(nc, net, ps)]
        for layer in range(DEPTH):
            for f in LAYER_PHASES:
                steps.append(lambda f=f, layer=layer: f(nc, net, ps, layer))
        for s in steps:
            s()


LAYER_PHASES = [input_projection_phase, attention_phase, rwkv_input_phase, scan_phase,
                mix_output_phase, placement_phase, expert_phase, combine_phase]


def kernel(**inputs):
    import concourse.bacc as bacc
    from concourse.bass_utils import run_bass_kernel_spmd

    nc = bacc.Bacc("TRN2", target_bir_lowering=False, num_devices=1)
    arrays, ins = {}, {}
    for name, a in {**{n: inputs[n] for n in INPUTS}, **constants()}.items():
        a = np.ascontiguousarray(a)
        arrays[f"in_{name}"] = a
        ins[name] = nc.dram_tensor(f"in_{name}", a.shape, mybir.dt.from_np(a.dtype), kind="ExternalInput").ap()
    out = nc.dram_tensor("out_0", (1, SEQ, D), F32, kind="ExternalOutput").ap()
    build(nc, ins, out)
    return run_bass_kernel_spmd(nc, [arrays], core_ids=[0]).results[0]["out_0"]
```
